# Optimizing a Trainium2 kernel written in Bass

```python
import jax, jax.numpy as jnp
from jax import lax
import numpy as np
import math

D_MODEL = 1024
BATCH = 1
SEQ = 256
DEPTH = 1

N_MIXERS = 4
RMS_EPS = 1e-6
N_MOD = 6

SB_HEADS = 16
SB_HEAD_DIM = D_MODEL // SB_HEADS
SB_QBLOCK = 128

GLA_HEADS = 4
GLA_DK = D_MODEL // (2 * GLA_HEADS)
GLA_DV = D_MODEL // GLA_HEADS
GLA_GATE_RANK = 16
GLA_GATE_TAU = 16.0
GLA_CHUNK = 64
GLA_IN = 2 * GLA_HEADS * GLA_DK + 2 * GLA_HEADS * GLA_DV + GLA_GATE_RANK

CONV_WIDTH = 3

DIL_PATTERNS = ((128, 1), (512, 4), (2048, 16))
DIL_GROUPS = len(DIL_PATTERNS)
DIL_HEADS = 8
DIL_HEAD_DIM = 64
DIL_QBLOCK = 128

MOE_GROUPS = 4
MOE_PER_GROUP = 8
MOE_EXPERTS = MOE_GROUPS * MOE_PER_GROUP
MOE_TOPK = 2
MOE_D_FF = D_MODEL // 2
MOE_BLOCK = 128

N_SB = (DEPTH + 3) // N_MIXERS
N_GLA = (DEPTH + 2) // N_MIXERS
N_CONV = (DEPTH + 1) // N_MIXERS
N_DIL = DEPTH // N_MIXERS


def rms_norm(x, g):
    x32 = x.astype(jnp.float32)
    y = x32 * lax.rsqrt(jnp.mean(x32 * x32, axis=-1, keepdims=True) + RMS_EPS)
    return (y * g.astype(jnp.float32)).astype(x.dtype)

def stick_breaking_attention(q, k, v):
    B, H, S, d = q.shape
    nb = S // SB_QBLOCK
    scale = d ** -0.5
    kpos = jnp.arange(S)
    qb = jnp.moveaxis(q.reshape(B, H, nb, SB_QBLOCK, d), 2, 0)

    def one_block(args):
        q_blk, blk = args
        qpos = blk * SB_QBLOCK + jnp.arange(SB_QBLOCK)
        z = jnp.einsum('bhqd,bhkd->bhqk', q_blk, k, preferred_element_type=jnp.float32) * scale
        causal = kpos[None, :] < qpos[:, None]
        log_keep = jnp.where(causal, jax.nn.log_sigmoid(-z), 0.0)
        suffix = lax.cumsum(log_keep, axis=3, reverse=True) - log_keep
        a = jnp.where(causal, jnp.exp(jax.nn.log_sigmoid(z) + suffix), 0.0)
        return jnp.einsum('bhqk,bhkd->bhqd', a.astype(v.dtype), v)

    out = lax.map(one_block, (qb, jnp.arange(nb)))
    return jnp.moveaxis(out, 0, 2).reshape(B, H, S, d)

def sb_mixer(h, w_in, w_out):
    B, S, _ = h.shape
    qkv = (h @ w_in).reshape(B, S, 3, SB_HEADS, SB_HEAD_DIM)
    qkv = jnp.transpose(qkv, (2, 0, 3, 1, 4))
    o = stick_breaking_attention(qkv[0], qkv[1], qkv[2])
    return jnp.transpose(o, (0, 2, 1, 3)).reshape(B, S, SB_HEADS * SB_HEAD_DIM) @ w_out

def gla_chunked(q, k, v, log_a):
    B, H, S, dk = q.shape
    dv = v.shape[-1]
    C = GLA_CHUNK
    nc = S // C
    f32 = jnp.float32

    def chunks(a):
        return a.astype(f32).reshape(B, H, nc, C, a.shape[-1])

    q, k, v, g = chunks(q), chunks(k), chunks(v), chunks(log_a)
    b = jnp.cumsum(g, axis=3)
    b_last = b[:, :, :, -1:, :]
    q_in = q * jnp.exp(b)
    k_in = k * jnp.exp(-b)
    k_state = k * jnp.exp(b_last - b)
    causal = jnp.tril(jnp.ones((C, C), dtype=bool))
    scores = jnp.where(causal, jnp.einsum('bhnid,bhnjd->bhnij', q_in, k_in), 0.0)
    o_intra = jnp.einsum('bhnij,bhnjv->bhniv', scores, v)

    def step(state, inp):
        q_n, k_n, v_n, decay_n = inp
        o_n = jnp.einsum('bhid,bhdv->bhiv', q_n, state)
        state = decay_n[..., None] * state + jnp.einsum('bhjd,bhjv->bhdv', k_n, v_n)
        return state, o_n

    xs = (jnp.moveaxis(q_in, 2, 0), jnp.moveaxis(k_state, 2, 0), jnp.moveaxis(v, 2, 0),
          jnp.moveaxis(jnp.exp(b_last[:, :, :, 0, :]), 2, 0))
    _, o_inter = lax.scan(step, jnp.zeros((B, H, dk, dv), f32), xs)
    o = o_intra + jnp.moveaxis(o_inter, 0, 2)
    return o.reshape(B, H, S, dv)

def gla_mixer(h, w_in, w_gate_up, b_gate, norm_g, w_out):
    B, S, _ = h.shape
    dqk = GLA_HEADS * GLA_DK
    dv = GLA_HEADS * GLA_DV
    proj = h @ w_in
    q, k, v, r, g_down = jnp.split(proj, [dqk, 2 * dqk, 2 * dqk + dv, 2 * dqk + 2 * dv], axis=-1)
    log_a = jax.nn.log_sigmoid((g_down @ w_gate_up + b_gate).astype(jnp.float32)) / GLA_GATE_TAU

    def heads(a, d):
        return jnp.transpose(a.reshape(B, S, GLA_HEADS, d), (0, 2, 1, 3))

    o = gla_chunked(heads(q, GLA_DK) * GLA_DK ** -0.5, heads(k, GLA_DK),
                    heads(v, GLA_DV), heads(log_a, GLA_DK))
    o = rms_norm(o, norm_g)
    o = jnp.transpose(o, (0, 2, 1, 3)).reshape(B, S, dv).astype(h.dtype) * jax.nn.silu(r)
    return o @ w_out

def conv_mixer(h, w_in, conv_w, conv_b, w_out):
    S = h.shape[1]
    gate_b, gate_c, u = jnp.split(h @ w_in, 3, axis=-1)
    u = gate_c * u
    u_pad = jnp.pad(u, ((0, 0), (CONV_WIDTH - 1, 0), (0, 0)))
    y = sum(conv_w[j] * u_pad[:, j:j + S] for j in range(CONV_WIDTH)) + conv_b
    return (gate_b * y) @ w_out

def dilated_window_attention(q, k, v, window, dilation):
    B, H, S, d = q.shape
    Q = DIL_QBLOCK
    steps = window // dilation
    span = dilation * Q
    Sp = -(-S // span) * span
    L = Sp // dilation
    nb = L // Q

    def strided(a):
        a = jnp.pad(a, ((0, 0), (0, 0), (0, Sp - S), (0, 0)))
        a = jnp.transpose(a.reshape(B, H, L, dilation, d), (0, 1, 3, 2, 4))
        return a.reshape(B, H, dilation, nb, Q, d)

    def with_prev(a):
        prev = jnp.concatenate([jnp.zeros_like(a[:, :, :, :1]), a[:, :, :, :-1]], axis=3)
        return jnp.concatenate([prev, a], axis=4)

    qb = strided(q)
    kc, vc = with_prev(strided(k)), with_prev(strided(v))
    z = jnp.einsum('bhrnqd,bhrnkd->bhrnqk', qb, kc, preferred_element_type=jnp.float32) * d ** -0.5
    qi = jnp.arange(Q)[:, None]
    kj = jnp.arange(2 * Q)[None, :]
    dist = qi + Q - kj
    in_window = (dist >= 0) & (dist <= steps)
    before_start = (jnp.arange(nb)[:, None, None] == 0) & (kj < Q)[None]
    valid = in_window[None] & ~before_start
    z = jnp.where(valid, z, -jnp.inf)
    m = jnp.max(z, axis=-1, keepdims=True)
    lse = m + jnp.log(jnp.sum(jnp.exp(z - m), axis=-1, keepdims=True))
    p = jnp.exp(z - lse)
    o = jnp.einsum('bhrnqk,bhrnkd->bhrnqd', p.astype(vc.dtype), vc)

    def unstride(a):
        e = a.shape[-1]
        a = jnp.moveaxis(a.reshape(B, H, dilation, L, e), 2, 3).reshape(B, H, Sp, e)
        return a[:, :, :S]

    return unstride(o), unstride(lse)[..., 0]

def dil_mixer(h, w_in, w_out):
    B, S, _ = h.shape
    proj = (h @ w_in).reshape(B, S, DIL_GROUPS, 3, DIL_HEADS, DIL_HEAD_DIM)
    proj = jnp.transpose(proj, (2, 3, 0, 4, 1, 5))
    outs, lses = [], []
    for g, (window, dilation) in enumerate(DIL_PATTERNS):
        o_g, lse_g = dilated_window_attention(proj[g, 0], proj[g, 1], proj[g, 2], window, dilation)
        outs.append(o_g)
        lses.append(lse_g)
    o = jnp.stack(outs)
    w = jax.nn.softmax(jnp.stack(lses), axis=0)
    o = jnp.einsum('gbhs,gbhsd->bshd', w.astype(o.dtype), o).reshape(B, S, DIL_HEADS * DIL_HEAD_DIM)
    return o @ w_out

def hier_moe(h, w_grp, b_grp, w_exp, b_exp, w_gate, w_up, w_down):
    T, D = h.shape
    f32 = jnp.float32
    grp_logits = (h @ w_grp + b_grp).astype(f32)
    grp = jnp.argmax(grp_logits, axis=-1)
    p_grp = jnp.take_along_axis(jax.nn.softmax(grp_logits, axis=-1), grp[:, None], axis=-1)
    exp_logits = (h @ w_exp + b_exp).astype(f32).reshape(T, MOE_GROUPS, MOE_PER_GROUP)
    in_grp = jnp.take_along_axis(exp_logits, grp[:, None, None], axis=1)[:, 0]
    p_in, top_i = lax.top_k(jax.nn.softmax(in_grp, axis=-1), MOE_TOPK)
    gate = p_grp * p_in / jnp.sum(p_in, axis=-1, keepdims=True)
    expert = grp[:, None] * MOE_PER_GROUP + top_i

    A = T * MOE_TOPK
    flat_e = expert.reshape(A)
    order = jnp.argsort(flat_e)
    sorted_e = flat_e[order]
    sorted_tok = order // MOE_TOPK
    sorted_w = gate.reshape(A)[order]
    counts = jnp.bincount(flat_e, length=MOE_EXPERTS)
    padded = (counts + MOE_BLOCK - 1) // MOE_BLOCK * MOE_BLOCK
    pad_end = jnp.cumsum(padded)
    pad_start = pad_end - padded
    start = jnp.cumsum(counts) - counts
    dest = pad_start[sorted_e] + jnp.arange(A) - start[sorted_e]
    P = (-(-A // MOE_BLOCK) + MOE_EXPERTS) * MOE_BLOCK
    NB = P // MOE_BLOCK
    slot_tok = jnp.full((P,), T, dtype=jnp.int32).at[dest].set(sorted_tok.astype(jnp.int32))
    slot_w = jnp.zeros((P,), f32).at[dest].set(sorted_w)
    blk_e = jnp.minimum(jnp.searchsorted(pad_end, jnp.arange(NB) * MOE_BLOCK, side='right'),
                        MOE_EXPERTS - 1)
    h_pad = jnp.concatenate([h, jnp.zeros((1, D), h.dtype)], axis=0)
    xb = h_pad[slot_tok].reshape(NB, MOE_BLOCK, D)

    def expert_block(args):
        x_blk, e = args
        return (jax.nn.silu(x_blk @ w_gate[e]) * (x_blk @ w_up[e])) @ w_down[e]

    yb = lax.map(expert_block, (xb, blk_e)).reshape(P, D)
    y = jax.ops.segment_sum(yb.astype(f32) * slot_w[:, None], slot_tok, num_segments=T + 1)[:T]
    return y.astype(h.dtype)

def first_inputs(seed: int = 0) -> dict:
    key = jax.random.key(seed)
    keys = jax.random.split(key, 26)
    D = D_MODEL

    def nrm(i, shape, scale):
        return jax.random.normal(keys[i], shape, jnp.float32) * scale

    sb_w = SB_HEADS * SB_HEAD_DIM
    gla_dqk = GLA_HEADS * GLA_DK
    gla_dv = GLA_HEADS * GLA_DV
    dil_w = DIL_HEADS * DIL_HEAD_DIM
    return {
        "x": nrm(0, (BATCH, SEQ, D), 1.0),
        "c": nrm(1, (BATCH, D), 1.0),
        "ada_w": nrm(2, (DEPTH, D, N_MOD * D), 0.5 * D ** -0.5),
        "ada_b": nrm(3, (DEPTH, N_MOD * D), 0.01),
        "norm_g": 1.0 + nrm(4, (DEPTH, 2, D), 0.02),
        "final_g": 1.0 + nrm(5, (D,), 0.02),
        "sb_w_in": nrm(6, (N_SB, D, 3 * sb_w), D ** -0.5),
        "sb_w_out": nrm(7, (N_SB, sb_w, D), sb_w ** -0.5),
        "gla_w_in": nrm(8, (N_GLA, D, GLA_IN), D ** -0.5),
        "gla_w_gate_up": nrm(9, (N_GLA, GLA_GATE_RANK, gla_dqk), GLA_GATE_RANK ** -0.5),
        "gla_b_gate": nrm(10, (N_GLA, gla_dqk), 0.01),
        "gla_norm_g": 1.0 + nrm(11, (N_GLA, GLA_DV), 0.02),
        "gla_w_out": nrm(12, (N_GLA, gla_dv, D), gla_dv ** -0.5),
        "conv_w_in": nrm(13, (N_CONV, D, 3 * D), D ** -0.5),
        "conv_w": nrm(14, (N_CONV, CONV_WIDTH, D), CONV_WIDTH ** -0.5),
        "conv_b": nrm(15, (N_CONV, D), 0.01),
        "conv_w_out": nrm(16, (N_CONV, D, D), D ** -0.5),
        "dil_w_in": nrm(17, (N_DIL, D, DIL_GROUPS * 3 * dil_w), D ** -0.5),
        "dil_w_out": nrm(18, (N_DIL, dil_w, D), dil_w ** -0.5),
        "moe_w_grp": nrm(19, (DEPTH, D, MOE_GROUPS), D ** -0.5),
        "moe_b_grp": nrm(20, (DEPTH, MOE_GROUPS), 0.01),
        "moe_w_exp": nrm(21, (DEPTH, D, MOE_EXPERTS), D ** -0.5),
        "moe_b_exp": nrm(22, (DEPTH, MOE_EXPERTS), 0.01),
        "moe_w_gate": nrm(23, (DEPTH, MOE_EXPERTS, D, MOE_D_FF), D ** -0.5),
        "moe_w_up": nrm(24, (DEPTH, MOE_EXPERTS, D, MOE_D_FF), D ** -0.5),
        "moe_w_down": nrm(25, (DEPTH, MOE_EXPERTS, MOE_D_FF, D), MOE_D_FF ** -0.5),
    }

def first_block(x, c, ada_w, ada_b, norm_g, final_g, sb_w_in, sb_w_out, gla_w_in, gla_w_gate_up,
              gla_b_gate, gla_norm_g, gla_w_out, conv_w_in, conv_w, conv_b, conv_w_out,
              dil_w_in, dil_w_out, moe_w_grp, moe_b_grp, moe_w_exp, moe_b_exp, moe_w_gate,
              moe_w_up, moe_w_down):
    B, S, D = x.shape
    cond = jax.nn.silu(c)
    for i in range(DEPTH):
        mod = cond @ ada_w[i] + ada_b[i]
        sh1, sc1, g1, sh2, sc2, g2 = jnp.split(mod[:, None, :], N_MOD, axis=-1)

        h = rms_norm(x, norm_g[i, 0]) * (1.0 + sc1) + sh1
        kind, j = i % N_MIXERS, i // N_MIXERS
        if kind == 0:
            y = sb_mixer(h, sb_w_in[j], sb_w_out[j])
        elif kind == 1:
            y = gla_mixer(h, gla_w_in[j], gla_w_gate_up[j], gla_b_gate[j], gla_norm_g[j], gla_w_out[j])
        elif kind == 2:
            y = conv_mixer(h, conv_w_in[j], conv_w[j], conv_b[j], conv_w_out[j])
        else:
            y = dil_mixer(h, dil_w_in[j], dil_w_out[j])
        x = (x + g1 * y).astype(x.dtype)

        h = rms_norm(x, norm_g[i, 1]) * (1.0 + sc2) + sh2
        y = hier_moe(h.reshape(B * S, D), moe_w_grp[i], moe_b_grp[i], moe_w_exp[i], moe_b_exp[i],
                     moe_w_gate[i], moe_w_up[i], moe_w_down[i]).reshape(B, S, D)
        x = (x + g2 * y).astype(x.dtype)
    return rms_norm(x, final_g)


DEPTH_2 = 2

HEAD_DIM = 64
Q_BLOCK = 128
NEG_INF = -1e30
A_HEADS = 8
A_LATENT = 256
IDX_HEADS = 8
IDX_DIM = 64
TOPK_MAX = 256
B_HEADS = 4
C_HEADS = 16
REL_BUCKETS = 32
REL_MAX_DIST = 128
REL_HEADS = A_HEADS + B_HEADS
PEER_HEADS = 8
PEER_QDIM = 256
PEER_NKEYS = 128
PEER_EXPERTS = PEER_NKEYS * PEER_NKEYS
PEER_TOPK = 16
PEER_CHUNK = 128
EVEN_SIZES = (A_HEADS * HEAD_DIM, A_LATENT, IDX_HEADS * IDX_DIM, IDX_DIM, IDX_HEADS,
              B_HEADS * 2 * HEAD_DIM, B_HEADS * 2 * HEAD_DIM, B_HEADS * 2 * HEAD_DIM)
EVEN_IN = A_HEADS * HEAD_DIM + A_LATENT + IDX_HEADS * IDX_DIM + IDX_DIM + IDX_HEADS + 3 * B_HEADS * 2 * HEAD_DIM
EVEN_MIX = A_HEADS * HEAD_DIM + B_HEADS * 2 * HEAD_DIM
ODD_SIZES = (C_HEADS * HEAD_DIM, C_HEADS * HEAD_DIM, C_HEADS * HEAD_DIM, C_HEADS)
ODD_IN = 3 * C_HEADS * HEAD_DIM + C_HEADS
ODD_MIX = C_HEADS * HEAD_DIM


def rmsnorm(x, g):
    xf = x.astype(jnp.float32)
    y = xf * lax.rsqrt(jnp.mean(xf * xf, axis=-1, keepdims=True) + RMS_EPS)
    return (y * g.astype(jnp.float32)).astype(x.dtype)

def split_cols(p, sizes):
    points = np.cumsum(np.array(sizes))[:-1].tolist()
    return jnp.split(p, points, axis=-1)

def rel_bucket(dist):
    max_exact = REL_BUCKETS // 2
    d = jnp.maximum(dist, 0)
    df = jnp.maximum(d, 1).astype(jnp.float32)
    large = max_exact + (jnp.log(df / max_exact) / math.log(REL_MAX_DIST / max_exact)
                         * (REL_BUCKETS - max_exact)).astype(jnp.int32)
    large = jnp.minimum(large, REL_BUCKETS - 1)
    return jnp.where(d < max_exact, d, large)

def sweep_blocks(fn, batch, seq_len):
    n = seq_len // Q_BLOCK
    out = lax.map(fn, jnp.arange(n, dtype=jnp.int32) * Q_BLOCK)
    out = jnp.moveaxis(out, 0, 1)
    return out.reshape((batch, seq_len) + out.shape[3:])

def dsa_attention(q, ckv, q_idx, k_idx, w_idx, w_uk, w_uv, bias_a):
    B, S = q.shape[0], q.shape[1]
    topk = min(TOPK_MAX, S // 4)
    key_pos = jnp.arange(S, dtype=jnp.int32)
    scale = HEAD_DIM ** -0.5
    idx_scale = IDX_DIM ** -0.5
    q_lat = jnp.einsum('bthd,chd->bthc', q, w_uk)

    def block(start):
        qpos = start + jnp.arange(Q_BLOCK, dtype=jnp.int32)
        qi = lax.dynamic_slice_in_dim(q_idx, start, Q_BLOCK, axis=1)
        wi = lax.dynamic_slice_in_dim(w_idx, start, Q_BLOCK, axis=1)
        ql = lax.dynamic_slice_in_dim(q_lat, start, Q_BLOCK, axis=1)
        li = jnp.einsum('bthd,bsd->bths', qi, k_idx).astype(jnp.float32) * idx_scale
        iscore = jnp.einsum('bths,bth->bts', jax.nn.relu(li), wi.astype(jnp.float32))
        causal = key_pos[None, :] <= qpos[:, None]
        iscore = jnp.where(causal[None], iscore, -jnp.inf)
        _, sel = lax.top_k(iscore, topk)
        kv_sel = jax.vmap(lambda lat, ix: lat[ix])(ckv, sel)
        dist = qpos[None, :, None] - sel
        s = jnp.einsum('bthc,btkc->bthk', ql, kv_sel).astype(jnp.float32) * scale
        s = s + jnp.moveaxis(bias_a[rel_bucket(dist)], -1, 2).astype(jnp.float32)
        s = jnp.where((dist >= 0)[:, :, None, :], s, NEG_INF)
        p = jax.nn.softmax(s, axis=-1).astype(ckv.dtype)
        o_lat = jnp.einsum('bthk,btkc->bthc', p, kv_sel)
        o = jnp.einsum('bthc,chd->bthd', o_lat, w_uv)
        return o.reshape(B, Q_BLOCK, A_HEADS * HEAD_DIM)

    return sweep_blocks(block, B, S)

def diff_attention(q1, q2, k1, k2, v, lam, lam_init, subln_g, bias_b):
    B, S = q1.shape[0], q1.shape[1]
    key_pos = jnp.arange(S, dtype=jnp.int32)
    scale = HEAD_DIM ** -0.5

    def block(start):
        qpos = start + jnp.arange(Q_BLOCK, dtype=jnp.int32)
        causal = key_pos[None, :] <= qpos[:, None]
        bias = jnp.moveaxis(bias_b[rel_bucket(qpos[:, None] - key_pos[None, :])], -1, 0)
        bias = bias.astype(jnp.float32)

        def probs(q, k):
            qb = lax.dynamic_slice_in_dim(q, start, Q_BLOCK, axis=1)
            s = jnp.einsum('bthd,bshd->bhts', qb, k).astype(jnp.float32) * scale + bias
            return jax.nn.softmax(jnp.where(causal, s, NEG_INF), axis=-1)

        a = probs(q1, k1) - lam * probs(q2, k2)
        return jnp.einsum('bhts,bshe->bthe', a.astype(v.dtype), v)

    o = sweep_blocks(block, B, S)
    o = rmsnorm(o, subln_g) * (1.0 - lam_init)
    return o.reshape(B, S, B_HEADS * 2 * HEAD_DIM)

def forgetting_attention(q, k, v, f_logit):
    B, S = q.shape[0], q.shape[1]
    key_pos = jnp.arange(S, dtype=jnp.int32)
    scale = HEAD_DIM ** -0.5
    cum = jnp.moveaxis(jnp.cumsum(jax.nn.log_sigmoid(f_logit.astype(jnp.float32)), axis=1), -1, 1)

    def block(start):
        qpos = start + jnp.arange(Q_BLOCK, dtype=jnp.int32)
        causal = key_pos[None, :] <= qpos[:, None]
        qb = lax.dynamic_slice_in_dim(q, start, Q_BLOCK, axis=1)
        cq = lax.dynamic_slice_in_dim(cum, start, Q_BLOCK, axis=2)
        s = jnp.einsum('bthd,bshd->bhts', qb, k).astype(jnp.float32) * scale
        s = s + cq[..., :, None] - cum[..., None, :]
        p = jax.nn.softmax(jnp.where(causal, s, NEG_INF), axis=-1).astype(v.dtype)
        return jnp.einsum('bhts,bshd->bthd', p, v)

    return sweep_blocks(block, B, S).reshape(B, S, C_HEADS * HEAD_DIM)

def even_mixer(h, w_in, w_out, kv_norm, w_uk, w_uv, lam_vec, subln_g, rel_bias, lam_init):
    B, S, _ = h.shape
    q_a, ckv, q_i, k_i, w_i, q_b, k_b, v_b = split_cols(h @ w_in, EVEN_SIZES)
    q_a = q_a.reshape(B, S, A_HEADS, HEAD_DIM)
    ckv = rmsnorm(ckv, kv_norm)
    q_i = q_i.reshape(B, S, IDX_HEADS, IDX_DIM)
    w_i = w_i * (IDX_HEADS ** -0.5)
    o_a = dsa_attention(q_a, ckv, q_i, k_i, w_i, w_uk, w_uv, rel_bias[:, :A_HEADS])
    q_b = q_b.reshape(B, S, B_HEADS, 2, HEAD_DIM)
    k_b = k_b.reshape(B, S, B_HEADS, 2, HEAD_DIM)
    v_b = v_b.reshape(B, S, B_HEADS, 2 * HEAD_DIM)
    lv = lam_vec.astype(jnp.float32)
    lam = jnp.exp(jnp.sum(lv[0] * lv[1])) - jnp.exp(jnp.sum(lv[2] * lv[3])) + lam_init
    o_b = diff_attention(q_b[..., 0, :], q_b[..., 1, :], k_b[..., 0, :], k_b[..., 1, :],
                         v_b, lam, lam_init, subln_g, rel_bias[:, A_HEADS:])
    return jnp.concatenate([o_a, o_b], axis=-1) @ w_out

def odd_mixer(h, w_in, b_forget, w_out):
    B, S, _ = h.shape
    q, k, v, f = split_cols(h @ w_in, ODD_SIZES)
    shp = (B, S, C_HEADS, HEAD_DIM)
    o = forgetting_attention(q.reshape(shp), k.reshape(shp), v.reshape(shp), f + b_forget)
    return o @ w_out

def peer_ffn(h, w_q, sub_keys, u, v):
    B, S, D = h.shape
    T = B * S
    ht = h.reshape(T, D)
    q = (ht @ w_q).reshape(T, PEER_HEADS, 2, PEER_QDIM // 2)
    s = jnp.einsum('thpd,pnd->thpn', q, sub_keys).astype(jnp.float32)
    top_s, top_i = lax.top_k(s, PEER_TOPK)
    cand_s = top_s[:, :, 0, :, None] + top_s[:, :, 1, None, :]
    cand_i = top_i[:, :, 0, :, None] * PEER_NKEYS + top_i[:, :, 1, None, :]
    best_s, best_j = lax.top_k(cand_s.reshape(T, PEER_HEADS, -1), PEER_TOPK)
    experts = jnp.take_along_axis(cand_i.reshape(T, PEER_HEADS, -1), best_j, axis=-1)
    gates = jax.nn.softmax(best_s, axis=-1)
    n_chunks = T // PEER_CHUNK
    hk = PEER_HEADS * PEER_TOPK

    def chunk(args):
        xc, ec, gc = args
        act = jax.nn.gelu(jnp.einsum('cd,ced->ce', xc, u[ec]))
        return jnp.einsum('ce,ced->cd', gc.astype(xc.dtype) * act, v[ec])

    out = lax.map(chunk, (ht.reshape(n_chunks, PEER_CHUNK, D),
                          experts.reshape(n_chunks, PEER_CHUNK, hk),
                          gates.reshape(n_chunks, PEER_CHUNK, hk)))
    return out.reshape(B, S, D)

def second_inputs(seed: int = 0) -> dict:
    key = jax.random.key(seed)
    ks = jax.random.split(key, 24)
    n_even = (DEPTH_2 + 1) // 2
    n_odd = DEPTH_2 // 2

    def nrm(k, shape, scale):
        return jax.random.normal(k, shape, jnp.float32) * scale

    return {
        "x": nrm(ks[0], (BATCH, SEQ, D_MODEL), 1.0),
        "c": nrm(ks[1], (BATCH, D_MODEL), 1.0),
        "rel_bias": nrm(ks[2], (REL_BUCKETS, REL_HEADS), 0.5),
        "ada_w": nrm(ks[3], (DEPTH_2, D_MODEL, 6 * D_MODEL), 0.5 * D_MODEL ** -0.5),
        "ada_b": nrm(ks[4], (DEPTH_2, 6 * D_MODEL), 0.02),
        "norm_mix": 1.0 + nrm(ks[5], (DEPTH_2, D_MODEL), 0.02),
        "norm_ffn": 1.0 + nrm(ks[6], (DEPTH_2, D_MODEL), 0.02),
        "norm_final": 1.0 + nrm(ks[7], (D_MODEL,), 0.02),
        "even_w_in": nrm(ks[8], (n_even, D_MODEL, EVEN_IN), D_MODEL ** -0.5),
        "even_w_out": nrm(ks[9], (n_even, EVEN_MIX, D_MODEL), EVEN_MIX ** -0.5),
        "a_kv_norm": 1.0 + nrm(ks[10], (n_even, A_LATENT), 0.02),
        "a_w_uk": nrm(ks[11], (n_even, A_LATENT, A_HEADS, HEAD_DIM), A_LATENT ** -0.5),
        "a_w_uv": nrm(ks[12], (n_even, A_LATENT, A_HEADS, HEAD_DIM), A_LATENT ** -0.5),
        "b_lambda": nrm(ks[13], (n_even, 4, HEAD_DIM), 0.1),
        "b_subln": 1.0 + nrm(ks[14], (n_even, 2 * HEAD_DIM), 0.02),
        "odd_w_in": nrm(ks[15], (n_odd, D_MODEL, ODD_IN), D_MODEL ** -0.5),
        "odd_b_forget": 2.0 + nrm(ks[16], (n_odd, C_HEADS), 0.5),
        "odd_w_out": nrm(ks[17], (n_odd, ODD_MIX, D_MODEL), ODD_MIX ** -0.5),
        "peer_w_q": nrm(ks[18], (DEPTH_2, D_MODEL, PEER_HEADS * PEER_QDIM), D_MODEL ** -0.5),
        "peer_sub_keys": nrm(ks[19], (DEPTH_2, 2, PEER_NKEYS, PEER_QDIM // 2), (PEER_QDIM // 2) ** -0.5),
        "peer_u": nrm(ks[20], (DEPTH_2, PEER_EXPERTS, D_MODEL), D_MODEL ** -0.5),
        "peer_v": nrm(ks[21], (DEPTH_2, PEER_EXPERTS, D_MODEL), PEER_HEADS ** -0.5),
    }

def second_block(x, c, rel_bias, ada_w, ada_b, norm_mix, norm_ffn, norm_final,
              even_w_in, even_w_out, a_kv_norm, a_w_uk, a_w_uv, b_lambda, b_subln,
              odd_w_in, odd_b_forget, odd_w_out,
              peer_w_q, peer_sub_keys, peer_u, peer_v):
    c_act = jax.nn.silu(c)
    for layer in range(DEPTH_2):
        mod = (c_act @ ada_w[layer] + ada_b[layer])[:, None, :]
        sh1, sc1, g1, sh2, sc2, g2 = jnp.split(mod, 6, axis=-1)
        h = rmsnorm(x, norm_mix[layer]) * (1.0 + sc1) + sh1
        if layer % 2 == 0:
            e = layer // 2
            lam_init = 0.8 - 0.6 * math.exp(-0.3 * layer)
            y = even_mixer(h, even_w_in[e], even_w_out[e], a_kv_norm[e], a_w_uk[e], a_w_uv[e],
                           b_lambda[e], b_subln[e], rel_bias, lam_init)
        else:
            o = layer // 2
            y = odd_mixer(h, odd_w_in[o], odd_b_forget[o], odd_w_out[o])
        x = x + g1 * y
        h = rmsnorm(x, norm_ffn[layer]) * (1.0 + sc2) + sh2
        x = x + g2 * peer_ffn(h, peer_w_q[layer], peer_sub_keys[layer], peer_u[layer], peer_v[layer])
    return rmsnorm(x, norm_final)


def setup_inputs(seed=0):
    out = dict(first_inputs(seed))
    for name, value in second_inputs(seed + 1).items():
        if name != "x":
            out[name + "_2"] = value
    return out


def reference(
    x, c, ada_w, ada_b, norm_g, final_g, sb_w_in, sb_w_out, gla_w_in, gla_w_gate_up, gla_b_gate,
    gla_norm_g, gla_w_out, conv_w_in, conv_w, conv_b, conv_w_out, dil_w_in, dil_w_out,
    moe_w_grp, moe_b_grp, moe_w_exp, moe_b_exp, moe_w_gate, moe_w_up, moe_w_down, c_2,
    rel_bias_2, ada_w_2, ada_b_2, norm_mix_2, norm_ffn_2, norm_final_2, even_w_in_2,
    even_w_out_2, a_kv_norm_2, a_w_uk_2, a_w_uv_2, b_lambda_2, b_subln_2, odd_w_in_2,
    odd_b_forget_2, odd_w_out_2, peer_w_q_2, peer_sub_keys_2, peer_u_2, peer_v_2,
):
    x = first_block(
        x, c, ada_w, ada_b, norm_g, final_g, sb_w_in, sb_w_out, gla_w_in, gla_w_gate_up,
        gla_b_gate, gla_norm_g, gla_w_out, conv_w_in, conv_w, conv_b, conv_w_out, dil_w_in,
        dil_w_out, moe_w_grp, moe_b_grp, moe_w_exp, moe_b_exp, moe_w_gate, moe_w_up, moe_w_down,
    )
    return second_block(
        x, c_2, rel_bias_2, ada_w_2, ada_b_2, norm_mix_2, norm_ffn_2, norm_final_2, even_w_in_2,
        even_w_out_2, a_kv_norm_2, a_w_uk_2, a_w_uv_2, b_lambda_2, b_subln_2, odd_w_in_2,
        odd_b_forget_2, odd_w_out_2, peer_w_q_2, peer_sub_keys_2, peer_u_2, peer_v_2,
    )


_drawn_inputs = setup_inputs


def setup_inputs(seed=0):
    import zlib

    import numpy as np

    out = dict(_drawn_inputs(seed))
    spreads = {}
    factors = {'ada_b': 3.432,
     'norm_g': 3.775,
     'moe_b_grp': 8.0,
     'moe_b_exp': 8.0,
     'norm_mix_2': 5.2,
     'norm_ffn_2': 4.685,
     'norm_final_2': 2.81,
     'a_kv_norm_2': 8.0,
     'b_subln_2': 8.0}
    for name, (base, spread) in spreads.items():
        noise = np.random.default_rng([zlib.crc32(name.encode()), seed]).standard_normal(out[name].shape)
        drawn = base * np.exp(spread * noise) if base else spread * noise
        out[name] = __import__('jax').numpy.asarray(drawn.astype(out[name].dtype))
    for name, factor in factors.items():
        out[name] = (out[name] * factor).astype(out[name].dtype)
    return out
```

```python
import math
from contextlib import ExitStack

import concourse.bass as bass
from concourse import mybir

F32 = mybir.dt.float32
BF16 = mybir.dt.bfloat16
U32 = mybir.dt.uint32
I32 = mybir.dt.int32
ALU = mybir.AluOpType
ACT = mybir.ActivationFunctionType
AX_X = mybir.AxisListType.X

P = 128
D = 1024
KC = D // P
T = 256
NT = T // P
HALF = D // 2
EPS = 1e-6
NEG = -1e30
LOWEST = -3.0e38
TAKEN = -3.3e38

HEAD = 64
MAPS = 16
SCALE = HEAD ** -0.5
MAPW = 3 * P

IDX_HEADS = 8
DSA_TOP = 64
DSA_HEADS = 8
DIFF_HEADS = 4
LATENT = 256
REL_BUCKETS = 32
REL_HEADS = 12

GROUPS = 4
PER_GROUP = 8
EXPERTS = 32
FF = 512
SLOTS = 64

PEER_HEADS = 8
PEER_K = 16
NKEYS = 128
PEER_EXPERTS = NKEYS * NKEYS
RING = 8
BODY = 32


def rel_bucket_ranges():
    exact = REL_BUCKETS // 2
    bucket = []
    for d in range(T):
        if d < exact:
            bucket.append(d)
        else:
            bucket.append(min(REL_BUCKETS - 1, exact + int(math.log(d / exact) / math.log(128 / exact) * exact)))
    return [(b, bucket.index(b), T - 1 - bucket[::-1].index(b)) for b in sorted(set(bucket))]


def two_block_kernel(nc, I, out):
    with ExitStack() as ctx:
        def sb(name, shape, dt=F32):
            return ctx.enter_context(nc.sbuf_tensor("sb_" + name, shape, dt))

        def sem(name):
            return ctx.enter_context(nc.semaphore(name))

        ps = ctx.enter_context(nc.psum_tensor("psum", [P, 8, HALF], F32))
        mod_rows_d = nc.dram_tensor("mod_rows_d", [3, 2 * D], F32).ap()
        rel_rows_d = nc.dram_tensor("rel_rows_d", [REL_HEADS, P, MAPW], F32).ap()

        x = sb("x", [P, NT, D])
        row = sb("row", [P, D])
        ident = sb("ident", [P, P])
        iota = sb("iota", [P, P])
        ones = sb("ones", [P, P])
        zeros = sb("zeros", [P, P])
        neg_ones = sb("neg_ones", [P, P])
        neg_tri = sb("neg_tri", [P, P])
        before = sb("before", [P, P])
        causal_add = sb("causal_add", [P, MAPW])
        token_sel = sb("token_sel", [P, BODY], BF16)
        mod_cols = sb("mod_cols", [P, 3, 4, KC])
        gain_cols = sb("gain_cols", [P, 6, KC])
        c_cols = sb("c_cols", [P, 2, KC])
        c_silu = sb("c_silu", [P, 2, KC])
        a_cols = sb("a_cols", [P, KC])
        ssq = sb("ssq", [P, NT])
        var = sb("var", [P, NT])
        std = sb("std", [P, NT])
        rstd = sb("rstd", [P, NT])
        small = sb("small", [P, 256])
        peer_i = sb("peer_i", [P, T])
        peer_j = sb("peer_j", [P, T])
        peer_g = sb("peer_g", [P, T])
        peer_e = sb("peer_e", [P, T], U32)
        passes = sb("passes", [P, 1], I32)

        AREA = 47104
        area = sb("area", [P, AREA])

        def view(at, *shape, dt=F32):
            n = math.prod(shape)
            words = n if dt != BF16 else n // 2
            assert at + words <= AREA, (at, shape)
            v = area[:, at:at + words]
            if dt != F32:
                v = v.bitcast(dt)
            if len(shape) == 2:
                v = v.rearrange("p (a b) -> p a b", b=shape[1])
            if len(shape) == 3:
                v = v.rearrange("p (a b c) -> p a b c", b=shape[1], c=shape[2])
            return v

        hT = view(0, KC, T)
        xn = view(2048, NT, D)
        wring = [view(4096 + 4096 * i, KC, HALF) for i in range(3)]
        qkT = view(16384, MAPS, T)
        v_tok = view(20480, NT, D)
        oT = view(22528, KC, T)
        AT = 24576
        ada_ring = [view(22528 + 6144 * i, 6 * D) for i in range(2)]
        ada_acc = view(22528 + 12288, 6 * D)
        ada_bias = view(22528 + 18432, 6 * D)
        mod_row = view(20480, 2 * D)

        consts_made = sem("consts_made")
        vec_loaded = sem("vec_loaded")
        x_loaded = sem("x_loaded")
        x_done = sem("x_done")
        row_loaded = sem("row_loaded")
        ada_loaded = [sem(f"ada_loaded{i}") for i in range(2)]
        ada_bias_loaded = sem("ada_bias_loaded")
        ada_used = sem("ada_used")
        c_ready = sem("c_ready")
        ada_summed = sem("ada_summed")
        ada_psum = sem("ada_psum")
        ada_cols_out = sem("ada_cols_out")
        ada_row_out = sem("ada_row_out")
        mod_row_stored = sem("mod_row_stored")
        ssq_done = sem("ssq_done")
        var_done = sem("var_done")
        std_done = sem("std_done")
        xn_done = sem("xn_done")
        xt_done = sem("xt_done")
        hT_done = sem("hT_done")
        w_loaded = [sem(f"w_loaded{i}") for i in range(3)]
        proj_done = sem("proj_done")
        proj_out = sem("proj_out")
        score_done = sem("score_done")
        score_read = sem("score_read")
        av_done = sem("av_done")
        av_out = sem("av_out")
        dve_step = sem("dve_step")
        act_step = sem("act_step")
        pool_step = sem("pool_step")
        stored = sem("stored")
        sems = {}

        def named(name):
            if name not in sems:
                sems[name] = sem(name)
            return sems[name]

        def stepper(eng, step_sem):
            n = [0]

            def step(ins):
                n[0] += 1
                ins.then_inc(step_sem, 1)
                eng.wait_ge(step_sem, n[0])
            return step

        groups = []

        def group(stage, w, kind, src, dst, scale=1.0, by="act", dup=0):
            groups.append(dict(stage=stage, w=w, kind=kind, src=src, dst=dst, scale=scale, by=by, dup=dup))

        ckvT = view(AT, 2, T)
        ckv_tok = view(AT + 512, NT, LATENT)
        kidx = view(AT + 1024, T)
        widx = view(AT + 1280, NT, IDX_HEADS)
        qidx = view(AT + 1312, 4, T)
        EV = AT + 1312 + 1024
        f_cum = view(AT, T)

        def sb_groups():
            w = I["sb_w_in"][0]
            for g in range(4):
                group("mix1", w[:, g * HALF:(g + 1) * HALF], "F", hT, qkT[:, 4 * g:4 * g + 4, :], SCALE if g < 2 else 1.0)
            for g in range(2):
                group("mix1", w[:, (4 + g) * HALF:(5 + g) * HALF], "T", hT, v_tok[:, :, g * HALF:(g + 1) * HALF])
            for g in range(2):
                group("mix1", I["sb_w_out"][0][:, g * HALF:(g + 1) * HALF], "T", oT, g, by="residual")

        def even_groups():
            w = I["even_w_in_2"][0]
            a, i, kk = 512 + LATENT, 512 + LATENT + 512, 512 + LATENT + 512 + 64
            b = kk + 8
            group("even", w[:, 512:a], "T", hT, ckv_tok)
            group("even", w[:, a:i], "F", hT, qidx)
            group("even", w[:, i:b], "I", hT, None)
            group("even", w[:, 0:512], "F", hT, qkT[:, 0:4, :], SCALE)
            group("even", w[:, b:b + 512], "F", hT, qkT[:, 4:8, :], SCALE)
            group("even", w[:, b + 512:b + 1024], "F", hT, qkT[:, 12:16, :])
            group("even", w[:, b + 1024:b + 1536], "T", hT, v_tok[:, :, 512:1024])
            group("even", I["a_w_uk_2"][0].rearrange("c h d -> c (h d)"), "F", ckvT, qkT[:, 8:12, :])
            group("even", I["a_w_uv_2"][0].rearrange("c h d -> c (h d)"), "T", ckvT, v_tok[:, :, 0:512])
            for g in range(2):
                group("even", I["even_w_out_2"][0][:, g * HALF:(g + 1) * HALF], "T", oT, g, by="residual")

        def odd_groups():
            w = I["odd_w_in_2"][0]
            group("odd", w[:, 3072:3088], "C", hT, None, by="dve")
            for g in range(4):
                group("odd", w[:, g * HALF:(g + 1) * HALF], "F", hT, qkT[:, 4 * g:4 * g + 4, :], SCALE if g < 2 else 1.0)
            for g in range(2):
                group("odd", w[:, (4 + g) * HALF:(5 + g) * HALF], "T", hT, v_tok[:, :, g * HALF:(g + 1) * HALF])
            for g in range(2):
                group("odd", I["odd_w_out_2"][0][:, g * HALF:(g + 1) * HALF], "T", oT, g, by="residual")

        def peer_groups(layer):
            w = I["peer_w_q_2"][layer]
            for g in range(4):
                group(f"peer{layer}", w[:, g * HALF:(g + 1) * HALF], "F", hT, qkT[:, 4 * g:4 * g + 4, :])

        sb_groups()
        even_groups()
        peer_groups(0)
        odd_groups()
        peer_groups(1)

        def groups_of(stage):
            return [(n, g) for n, g in enumerate(groups) if g["stage"] == stage]

        def w_turns(n):
            return sum(32 if g["kind"] == "I" else 16 for g in groups[n % 3:n + 1:3])

        def x_updates(stage):
            return {"mix1": 0, "moe": 1, "fin1": 2, "even": 3, "peer0": 4, "odd": 5, "peer1": 6, "all": 7}[stage]

        NORM = {"mix1": (0, 0, 0), "moe": (1, 0, 2), "even": (2, 1, 0), "peer0": (3, 1, 2), "odd": (4, 2, 0), "peer1": (5, 2, 2)}
        GAINS = [I["norm_g"][0, 0], I["norm_g"][0, 1], I["norm_mix_2"][0], I["norm_ffn_2"][0], I["norm_mix_2"][1],
                 I["norm_ffn_2"][1]]
        h_tok = view(2048, NT, D)
        moe_w = [[view(4096 + 12288 * b + 4096 * i, (KC, KC, FF // P)[i], (FF, FF, D)[i]) for i in range(3)] for b in range(2)]
        M = 28672
        route_w = view(M, KC, GROUPS + EXPERTS)
        route_b = view(M + 288, GROUPS + EXPERTS)
        grp_logit = view(M + 352, NT, 8)
        exp_logit = view(M + 368, NT, EXPERTS)
        grp_top = view(M + 432, NT, 8)
        grp_at = view(M + 448, NT, 8, dt=U32)
        grp_num = view(M + 464, NT)
        grp_neg = view(M + 466, NT)
        grp_exp = view(M + 468, NT, GROUPS)
        grp_sum = view(M + 476, NT)
        grp_p = view(M + 478, NT)
        grp_hot = view(M + 480, NT, GROUPS)
        in_grp = view(M + 488, NT, PER_GROUP)
        in_top = view(M + 504, NT, 8)
        in_at = view(M + 520, NT, 8, dt=U32)
        in_num = view(M + 536, NT, 8)
        in_neg = view(M + 552, NT)
        in_exp = view(M + 554, NT)
        in_den = view(M + 556, NT)
        gate1 = view(M + 558, NT)
        gate2 = view(M + 560, NT)
        expert = view(M + 562, NT, 2)
        hot1 = view(M + 576, NT, EXPERTS)
        hot2 = view(M + 640, NT, EXPERTS)
        chosen = view(M + 704, NT, EXPERTS)
        RW = EXPERTS + 2
        weight = view(M + 768, NT, RW)
        rank = view(M + 836, NT, RW)
        most = view(M + 904, 8)
        disp = [view(M + 1024 + 128 * b, NT, SLOTS) for b in range(2)]
        comb = view(M + 1280, NT, 2 * SLOTS)
        xe = [view(M + 1536 + 512 * b, KC, SLOTS) for b in range(2)]
        silu_g = [view(M + 2560 + 256 * b, FF // P * SLOTS) for b in range(2)]
        act_e = [view(M + 3072 + 256 * b, FF // P, SLOTS) for b in range(2)]
        y_pair = view(M + 3584, D)
        combT = view(M + 4608, T)
        PAIRS = EXPERTS // 2

        def overflow(eng, one_pass):
            eng.wait_ge(named("passes_known"), 1)
            n = eng.value_load(passes[0:1, 0:1], min_val=1, max_val=T // SLOTS)
            with eng.If(n > 1):
                with eng.Fori(1, n) as p:
                    one_pass(p)
        idx_relu = [view(EV + MAPW * i, MAPW) for i in range(2)]
        idx_score = view(EV + 2 * MAPW, MAPW)
        idx_mask = view(EV + 3 * MAPW, MAPW)
        idx_top = view(EV + 4 * MAPW, 8)
        kv_ssq = view(EV + 1552, NT)
        kv_std = view(EV + 1554, NT)
        lam_prod = view(EV + 1556, 2, HEAD)
        lam_sum = view(EV + 1684, 2)
        lam_exp = view(EV + 1686, 2)
        neg_lam = view(EV + 1688, 1)
        subln_col = view(EV + 1689, 1)
        SM = EV + 1696
        sm_s = [view(SM + MAPW * i, MAPW) for i in range(2)]
        sm_p = [view(SM + MAPW * (2 + i), MAPW) for i in range(2)]
        sm_pT = [view(SM + MAPW * (4 + i), MAPW) for i in range(2)]
        sm_max = [view(SM + MAPW * 6 + 2 * i, 2) for i in range(2)]
        sm_sum = [view(SM + MAPW * 6 + 4 + 2 * i, 2) for i in range(2)]
        sm_inv = [view(SM + MAPW * 6 + 8 + 2 * i, 2) for i in range(2)]
        diff_sq = view(SM + MAPW * 6 + 16, DIFF_HEADS, T)
        diff_std = view(SM + MAPW * 6 + 16 + DIFF_HEADS * T, DIFF_HEADS, T)
        LAM_INIT = 0.8 - 0.6 * math.exp(0.0)

        C_HEADS = MAPS
        f_logit = view(AT + T, T)
        f_abs = view(AT + 2 * T, T)
        f_log = view(AT + 3 * T, T)
        neg_ident = view(AT + 4 * T, C_HEADS)
        forget_col = view(AT + 4 * T + C_HEADS, 1)

        SOFTMAX = {"even": [], "odd": []}
        for m in range(MAPS):
            if m < DSA_HEADS:
                SOFTMAX["even"].append(dict(m=m, kind="head", n=m, turn=m, av=MAPS + m))
            else:
                hb = (m - DSA_HEADS) // 2
                SOFTMAX["even"].append(dict(m=m, kind="second" if m % 2 else "first", n=m, turn=DSA_HEADS + hb, hb=hb))
            SOFTMAX["odd"].append(dict(m=m, kind="head", n=MAPS + m, turn=DSA_HEADS + DIFF_HEADS + m, av=MAPS + DSA_HEADS + m))

        def both_tiles(t, nt):
            return t[:, 0:P] if nt == 0 else t[:, P:MAPW]

        def wait_read(eng, d):
            if d["kind"] == "head":
                eng.wait_ge(av_done, d["av"] + 1)
            else:
                eng.wait_ge(named("diff_av"), d["hb"] + 1)
        C_WORDS = NKEYS * T
        coef_all = view(0, T, NKEYS)
        UV = C_WORDS
        u_rows = [view(UV + D * s, D) for s in range(RING)]
        VI = 4
        v_rows = [view(UV + VI * D * s, VI, D) for s in range(2)]
        h_parts = view(UV + RING * D, 8, D, dt=BF16)
        AB = UV + RING * D + 4 * D
        hot_i = [view(AB + 4 * P * s, 4, P) for s in range(2)]
        hot_j = [view(AB + 4 * P * (2 + s), 4, P) for s in range(2)]
        coef_ring = [view(AB + VI * T * s, VI, T) for s in range(2)]
        keys_raw = view(AB, 2, P)
        keysT = view(AB + 2 * P, 2, P)
        part_hi = view(UV, NT, D, dt=BF16)
        part_mid = view(UV + D, NT, D, dt=BF16)
        part_lo = view(UV + 2 * D, NT, D, dt=BF16)
        part_rest = view(UV + 3 * D, NT, D)
        K = 20480
        HP = 2 * PEER_HEADS
        key_top = view(K, NT * HP, PEER_K)
        key_at = view(K + 512, NT * HP, PEER_K, dt=U32)
        key_num = view(K + 1024, NT * HP, PEER_K)
        key_left = view(K + 1536, 4, NKEYS)
        cand = view(K + 2048, PEER_HEADS, PEER_K * PEER_K)
        cand_left = view(K + 4096, PEER_HEADS, PEER_K * PEER_K)
        best = view(K + 6144, NT * PEER_HEADS, PEER_K)
        best_at = view(K + 6400, NT * PEER_HEADS, PEER_K, dt=U32)
        best_hi = view(K + 6656, P, dt=U32)
        best_lo = view(K + 6784, P, dt=U32)
        best_row = view(K + 6912, P)
        best_col = view(K + 7040, P)
        match = view(K + 7168, P, PEER_K)
        pick_i = view(K + 9216, NT, P)
        pick_j = view(K + 9472, NT, P)
        gate = view(K + 9728, NT * PEER_HEADS, PEER_K)
        gate_sum = view(K + 9984, NT * PEER_HEADS)
        peer_num = small
        dots = small[:, 0:BODY]
        gelu = small[:, BODY:2 * BODY]
        coef = small[:, 2 * BODY:3 * BODY]
        idx_ring = [small[:, 3 * BODY + 8 * s:3 * BODY + 8 * s + 8].bitcast(U32) for s in range(2)]
        BODIES = T // BODY
        SUB = BODY // 4
        CHUNKS = NKEYS // VI

        def layer_of(stage):
            return int(stage[-1])
        block = ctx.enter_context(nc.Block())
        ADA = [(I["ada_w"][0], I["ada_b"][0:1, :], 0), (I["ada_w_2"][0], I["ada_b_2"][0:1, :], 1),
               (I["ada_w_2"][1], I["ada_b_2"][1:2, :], 1)]
        ROWS = [("mix1", 0, 0), ("moe", 0, 1), ("fin1", None, I["final_g"]), ("even", 1, 0), ("peer0", 1, 1),
                ("odd", 2, 0), ("peer1", 2, 1), ("all", None, I["norm_final_2"])]

        st_abs = [view(AT + MAPW * i, MAPW) for i in range(2)]
        st_exp = [view(AT + MAPW * (2 + i), MAPW) for i in range(2)]
        st_ln = [view(AT + MAPW * (4 + i), MAPW) for i in range(2)]
        st_keep = [view(AT + MAPW * (6 + i), MAPW) for i in range(2)]
        st_a = [view(AT + MAPW * (8 + i), MAPW) for i in range(2)]

        RB = 36864
        rel_maps = view(RB, REL_HEADS, MAPW)
        lam_vec = view(RB + REL_HEADS * MAPW, 4, HEAD)
        kv_gain = view(RB + REL_HEADS * MAPW + 256, LATENT // P)
        subln_raw = view(RB + REL_HEADS * MAPW + 258, 1)
        rel_heads, rel_near, rel_far = small[:, 0:REL_BUCKETS], peer_i, peer_j

        def map_q(m):
            lo = HEAD * (m % 2)
            return qkT[lo:lo + HEAD, m // 2, :], qkT[lo:lo + HEAD, MAPS // 2 + m // 2, :]

        def diag_blocks(t):
            return t.rearrange("p (b c) -> p b c", c=P)[:, 0:3:2, :]

        @block.sync
        def _(sp):
            def load_row(stage):
                r = [s for s, _, _ in ROWS].index(stage)
                _, a, v = ROWS[r]
                if r:
                    sp.wait_ge(x_done, r)
                if a is None:
                    src = v.rearrange("(a n) -> a n", a=1)
                else:
                    sp.wait_ge(mod_row_stored, 16 * (a + 1))
                    src = mod_rows_d[a:a + 1, v * D:(v + 1) * D]
                sp.dma_start(row[:, :], src.broadcast_to([P, D])).then_inc(row_loaded, 16)

            def load_group(n, g, first):
                if first and n:
                    sp.wait_ge(x_done, x_updates(g["stage"]))
                if n >= 3:
                    sp.wait_ge(proj_done, n - 2)
                cols = g["w"].shape[1]
                nk = g["w"].shape[0] // P
                w = g["w"].rearrange("(k p) n -> p k n", p=P)
                slot = wring[n % 3]
                if g["kind"] == "I":
                    sp.dma_start(slot[:, 0:nk, 0:64], w[:, :, 0:64]).then_inc(w_loaded[n % 3], 16)
                    sp.dma_start(slot[:, 0:nk, 64:64 + cols], w).then_inc(w_loaded[n % 3], 16)
                else:
                    sp.dma_start(slot[:, 0:nk, 0:cols], w).then_inc(w_loaded[n % 3], 16)

            def load_stage(stage):
                for i, (n, g) in enumerate(groups_of(stage)):
                    load_group(n, g, i == 0)
                    if i == 2:
                        load_row(stage)

            sp.dma_start(x[:, :, :], I["x"][0].rearrange("(t p) d -> p t d", p=P)).then_inc(x_loaded, 16)
            for i, c in enumerate((I["c"], I["c_2"])):
                sp.dma_start(c_cols[:, i, :], c[0].rearrange("(k p) -> p k", p=P),
                             allow_slow_non_contiguous=True).then_inc(vec_loaded, 16)
            for i, gain in enumerate(GAINS):
                sp.dma_start(gain_cols[:, i, :], gain.rearrange("(k p) -> p k", p=P),
                             allow_slow_non_contiguous=True).then_inc(vec_loaded, 16)
            sp.dma_start(rel_heads[0:REL_HEADS, :], I["rel_bias_2"].rearrange("b h -> h b"),
                         allow_slow_non_contiguous=True).then_inc(named("rel_heads_loaded"), 16)
            for a, (w, b, _) in enumerate(ADA):
                if a:
                    sp.wait_ge(ada_psum, a)
                sp.dma_start(ada_bias[0:1, :], b).then_inc(ada_bias_loaded, 16)
                for k in range(KC):
                    n = a * KC + k
                    if n >= 2:
                        sp.wait_ge(ada_summed, n - 1)
                    sp.dma_start(ada_ring[n % 2][:, :], w[k * P:(k + 1) * P, :]).then_inc(ada_loaded[n % 2], 16)
            load_stage("mix1")
            sp.wait_ge(ada_psum, 3)
            sp.dma_start(lam_vec.rearrange("p a d -> p (a d)"), I["b_lambda_2"].rearrange("e a d -> e (a d)").broadcast_to([P, 4 * HEAD])
                         ).then_inc(named("even_vec_loaded"), 16)
            sp.dma_start(kv_gain, I["a_kv_norm_2"][0].rearrange("(k p) -> p k", p=P),
                         allow_slow_non_contiguous=True).then_inc(named("even_vec_loaded"), 16)
            sp.dma_start(subln_raw, I["b_subln_2"][0].rearrange("(p a) -> p a", a=1)).then_inc(named("even_vec_loaded"), 16)
            sp.wait_ge(named("rel_made"), 1)
            for part, cols in ((rel_near, slice(0, T)), (rel_far, slice(T, MAPW))):
                width = cols.stop - cols.start
                sp.dma_start(rel_rows_d[:, :, cols], part[0:REL_HEADS, 0:width].unsqueeze(1).broadcast_to([REL_HEADS, P, width])
                             ).then_inc(named("rel_stored"), 16)
            sp.wait_ge(named("rel_stored"), 32)
            rows = rel_rows_d.tensor
            sp.dma_start(rel_maps[:, :, P:MAPW], bass.AP(rows, P - 1, [[MAPW - 1, P], [P * MAPW, REL_HEADS], [1, T]])
                         ).then_inc(named("rel_loaded"), 16)
            sp.dma_start(rel_maps[:, :, 0:P], bass.AP(rows, 2 * P - 1, [[MAPW - 1, P], [P * MAPW, REL_HEADS], [1, P]])
                         ).then_inc(named("rel_loaded"), 16)
            def load_expert(e, b):
                for i, w in enumerate((I["moe_w_gate"], I["moe_w_up"], I["moe_w_down"])):
                    src = w[0, bass.ds(e, 1)].rearrange("e (k p) f -> p (e k) f", p=P)
                    sp.dma_start(moe_w[b][i], src).then_inc(named(f"expert_loaded{b}"), 16)

            def load_pass(p):
                for b in range(2):
                    load_expert(b, b)
                with sp.Fori(1, PAIRS) as i:
                    for b in range(2):
                        sp.wait_ge(named("y_done"), p * EXPERTS + 2 * i + (b - 1))
                        load_expert(2 * i + b, b)

            def load_overflow(p):
                sp.wait_ge(named("comb_done"), p * PAIRS + 1)
                load_pass(p)

            sp.wait_ge(x_done, x_updates("moe"))
            with nc.allow_non_contiguous_dma(reason="a router's few columns"):
                sp.dma_start(route_w[:, :, 0:GROUPS], I["moe_w_grp"][0].rearrange("(k p) n -> p k n", p=P)
                             ).then_inc(named("route_loaded"), 16)
                sp.dma_start(route_w[:, :, GROUPS:], I["moe_w_exp"][0].rearrange("(k p) n -> p k n", p=P)
                             ).then_inc(named("route_loaded"), 16)
            sp.dma_start(route_b[0:1, 0:GROUPS], I["moe_b_grp"][0:1, :]).then_inc(named("route_loaded"), 16)
            sp.dma_start(route_b[0:1, GROUPS:], I["moe_b_exp"][0:1, :]).then_inc(named("route_loaded"), 16)
            load_row("moe")
            load_pass(0)
            overflow(sp, load_overflow)
            load_row("fin1")
            load_stage("even")
            def peer(stage):
                L = layer_of(stage)
                sp.wait_ge(x_done, x_updates(stage))
                sp.dma_start(keys_raw[:, :, :], I["peer_sub_keys_2"][L].rearrange("a n d -> n a d")).then_inc(named("keys_loaded"), 16)
                load_stage(stage)
                sp.wait_ge(named("parts_made"), L + 1)
                for q in range(8):
                    lo = 32 * (q % 4)
                    for n, part in enumerate((part_hi, part_mid, part_lo)):
                        sp.dma_start(h_parts[32 * n:32 * n + 32, q, :], part[lo:lo + 32, q // 4, :]).then_inc(named("h_parts_loaded"), 16)
                sp.wait_ge(named("dots_done"), RING + T * (L + 1))
                v = I["peer_v_2"][L].rearrange("(i j) d -> j i d", j=NKEYS)

                def load_v(c, s):
                    sp.dma_start(v_rows[s], v[:, bass.ds(c * VI, VI), :]).then_inc(named(f"v_loaded{s}"), 16)

                for s in range(2):
                    load_v(s, s)
                with sp.Fori(1, CHUNKS // 2) as m:
                    for s in range(2):
                        sp.wait_ge(named("v_used"), 2 * m + (L * CHUNKS + s - 1))
                        load_v(2 * m + s, s)

            peer("peer0")
            sp.wait_ge(x_done, x_updates("odd"))
            sp.dma_start(forget_col[0:C_HEADS, :], I["odd_b_forget_2"][0].rearrange("(h a) -> h a", a=1)).then_inc(named("forget_loaded"), 16)
            load_stage("odd")
            peer("peer1")
            load_row("all")
            sp.wait_ge(x_done, x_updates("all") + 1)
            sp.dma_start(out[0].rearrange("(t p) d -> p t d", p=P), x[:, :, :]).then_inc(stored, 16)
            sp.wait_ge(stored, 16)

        @block.gpsimd
        def _(pool):
            step = stepper(pool, pool_step)
            step(pool.memset(ident[:, :], 0.0))
            step(pool.memset(ones[:, :], 1.0))
            step(pool.memset(neg_ones[:, :], -1.0))
            step(pool.memset(zeros[:, :], 0.0))
            step(pool.memset(causal_add[:, :], 0.0))
            step(pool.iota(iota[:, :], [[1, P]], base=0, channel_multiplier=0, allow_small_or_imprecise_dtypes=True))
            step(pool.affine_select(out=ident[:, :], in_=ident[:, :], compare_op=ALU.not_equal, fill=1.0,
                                    base=0, pattern=[[-1, P]], channel_multiplier=1))
            step(pool.affine_select(out=before[:, :], in_=ones[:, :], compare_op=ALU.is_gt, fill=0.0,
                                    base=0, pattern=[[1, P]], channel_multiplier=-1))
            step(pool.affine_select(out=neg_tri[:, :], in_=neg_ones[:, :], compare_op=ALU.is_ge, fill=0.0,
                                    base=0, pattern=[[-1, P]], channel_multiplier=1))
            step(pool.affine_select(out=diag_blocks(causal_add[:, :]), in_=diag_blocks(causal_add[:, :]),
                                    compare_op=ALU.is_ge, fill=NEG, base=0, pattern=[[0, 2], [-1, P]],
                                    channel_multiplier=1))
            step(pool.memset(token_sel[:, :], 0.0))
            for quadrant in range(3):
                part = token_sel[:, :]
                step(pool.affine_select(out=part, in_=part, compare_op=ALU.not_equal, fill=1.0,
                                        base=-BODY * quadrant, pattern=[[-1, BODY]], channel_multiplier=1))
            pool.sem_inc(consts_made, 1)

            pool.wait_ge(named("rel_heads_loaded"), 16)
            step(pool.memset(rel_far[0:REL_HEADS, :], NEG))
            for b, first, last in rel_bucket_ranges():
                step(pool.tensor_copy(rel_near[0:REL_HEADS, T - 1 - last:T - first],
                                      rel_heads[0:REL_HEADS, b:b + 1].broadcast_to([REL_HEADS, last - first + 1])))
            pool.sem_inc(named("rel_made"), 1)

            for h in range(MAPS):
                pool.wait_ge(named("stick_exp"), h + 1)
                a = diag_blocks(st_a[h % 2])
                pool.affine_select(out=a, in_=a, compare_op=ALU.is_gt, fill=0.0, base=0,
                                   pattern=[[0, 2], [1, P]], channel_multiplier=-1).then_inc(named("stick_mask"), 1)
            pool.wait_ge(named("idx_summed"), IDX_HEADS)
            pool.affine_select(out=diag_blocks(idx_score), in_=diag_blocks(idx_score), compare_op=ALU.is_ge, fill=LOWEST,
                               base=0, pattern=[[0, 2], [-1, P]], channel_multiplier=1).then_inc(named("idx_causal"), 1)
            def peer(stage):
                L = layer_of(stage)
                u = I["peer_u_2"].rearrange("l e d -> (l e) d")
                pool.wait_ge(x_done, x_updates(stage))
                step(pool.memset(h_parts[96:128, :, :], 0.0))
                pool.sem_inc(named("h_parts_cleared"), 1)
                pool.wait_ge(named("experts_made"), L + 1)
                pool.wait_ge(named("h_parts_loaded"), 24 * 16 * (L + 1))
                with pool.Fori(0, BODIES) as g:
                    for b in range(BODY // RING):
                        at = g * BODY + b * RING
                        pool.tensor_copy(idx_ring[b % 2], peer_e[:, bass.ds(at, RING)]).then_inc(named("idx_copied"), 1)
                        pool.wait_ge(named("idx_copied"), g * (BODY // RING) + (L * T // RING + b + 1))
                        for s in range(RING):
                            pool.wait_ge(named("dots_done"), at + (L * T + s + 1))
                            pool.sem_inc(named("gathers_begun"), 1)
                            pool.indirect_dma_start(u_rows[s], None, u, bass.IndirectOffsetOnAxis(ap=idx_ring[b % 2][:, s:s + 1], axis=0)
                                                    ).then_inc(named(f"u_loaded{s}"), 16)

            peer("peer0")
            peer("peer1")

        @block.scalar
        def _(act):
            step = stepper(act, act_step)

            def norm(stage):
                n = x_updates(stage)
                if n:
                    act.wait_ge(x_done, n)
                else:
                    act.wait_ge(x_loaded, 16)
                for t in range(NT):
                    act.activation(xn[:, t, :], x[:, t, :], ACT.Square, accum_out=ssq[:, t:t + 1]).then_inc(ssq_done, 1)
                act.wait_ge(var_done, n + 1)
                act.activation(std[:, :], var[:, :], ACT.Sqrt).then_inc(std_done, 1)

            def take(n, g):
                if g["by"] != "act":
                    return
                act.wait_ge(proj_done, n + 1)
                b = 2 * (n % 2)
                cols = g["w"].shape[1]
                if g["kind"] == "F":
                    src = ps[:, b:b + 2, :].rearrange("p b (f t) -> p (b f) t", t=T)
                    act.activation(g["dst"], src, ACT.Copy, scale=g["scale"]).then_inc(proj_out, 1)
                elif g["kind"] == "T":
                    act.activation(g["dst"], ps[:, b:b + 2, 0:cols], ACT.Copy, scale=g["scale"]).then_inc(proj_out, 1)
                else:
                    step(act.activation(kidx[:, :], ps[:, b, 0:T], ACT.Copy))
                    act.activation(widx[:, :, :], ps[:, b + 1, 0:16].rearrange("p (t h) -> p t h", t=NT), ACT.Copy,
                                   scale=IDX_HEADS ** -0.5).then_inc(proj_out, 1)

            def take_av(h, n):
                act.wait_ge(av_done, n + 1)
                lo = HEAD * (h % 2)
                act.activation(oT[lo:lo + HEAD, h // 2, :], ps[lo:lo + HEAD, 6 + (h // 2) % 2, 0:T],
                               ACT.Copy).then_inc(av_out, 1)

            act.wait_ge(vec_loaded, 128)
            act.activation(c_silu[:, :, :], c_cols[:, :, :], ACT.Silu).then_inc(c_ready, 1)
            for a in range(3):
                act.wait_ge(ada_psum, a + 1)
                act.activation(mod_cols[:, a, :, :], ps[:, 4, 0:4 * KC].rearrange("p (v k) -> p v k", k=KC),
                               ACT.Copy).then_inc(ada_cols_out, 1)
                if a:
                    act.wait_ge(mod_row_stored, 16 * a)
                act.activation(mod_row[0:1, :], ps[0:1, 0:4, :].rearrange("p b n -> p (b n)"),
                               ACT.Copy).then_inc(ada_row_out, 1)
                act.wait_ge(ada_row_out, a + 1)
                act.dma_start(mod_rows_d[a:a + 1, :], mod_row[0:1, :]).then_inc(mod_row_stored, 16)
            act.wait_ge(mod_row_stored, 48)

            norm("mix1")
            for n, g in groups_of("mix1"):
                take(n, g)

            def stick_keep(h):
                act.wait_ge(score_done, h + 1)
                step(act.activation(st_abs[h % 2], ps[:, 4 + h % 2, 0:MAPW], ACT.Abs))
                step(act.activation(st_exp[h % 2], st_abs[h % 2], ACT.Exp, scale=-1.0))
                if h >= 2:
                    act.wait_ge(named("stick_kept"), h - 1)
                act.activation(st_ln[h % 2], st_exp[h % 2], ACT.Ln, bias=1.0).then_inc(named("stick_ln"), 1)

            def stick_weight(h):
                act.wait_ge(named("stick_sum"), h + 1)
                if h >= 2:
                    act.wait_ge(av_done, h - 1)
                act.activation(st_a[h % 2], ps[:, 4 + h % 2, 0:MAPW], ACT.Exp).then_inc(named("stick_exp"), 1)

            for i in range(MAPS + 2):
                if i < MAPS:
                    stick_keep(i)
                if 1 <= i <= MAPS:
                    stick_weight(i - 1)
                if i >= 2:
                    take_av(i - 2, i - 2)
            def moe_pass(p):
                def take_xe(e, b):
                    act.wait_ge(named("xe_psum"), p * (EXPERTS + 1) + e + 2)
                    act.activation(xe[b], ps[:, 4, :].rearrange("p (k s) -> p k s", s=SLOTS), ACT.Copy).then_inc(named("xe_ready"), 1)

                take_xe(0, 0)
                with act.Fori(0, PAIRS) as i:
                    for b in range(2):
                        n = p * EXPERTS + 2 * i + b
                        act.wait_ge(named("gu_done"), n + 1)
                        act.activation(silu_g[b], ps[:, 5, 0:HALF // 2], ACT.Silu).then_inc(named("silu_done"), 1)
                        take_xe(2 * i + 1 + b, 1 - b)
                        act.wait_ge(named("y_done"), n + 1)
                        act.wait_ge(named("comb_done"), p * PAIRS + i + 1)
                        rows = slice(SLOTS * b, SLOTS * (b + 1))
                        act.activation(y_pair[rows, :], ps[rows, 6:8, :].rearrange("p b n -> p (b n)"),
                                       ACT.Copy).then_inc(named("y_ready"), 1)

            norm("moe")
            for b in range(4):
                act.wait_ge(named("ht_psum"), b + 1)
                act.activation(h_tok[:, b // 2, (b % 2) * HALF:(b % 2 + 1) * HALF], ps[:, b, :],
                               ACT.Copy).then_inc(named("h_tok_ready"), 1)
            act.sem_inc(named("xe_ready"), 1)
            act.sem_inc(named("y_ready"), 1)
            act.wait_ge(named("grp_neg_made"), 1)
            for t in range(NT):
                act.activation(grp_exp[:, t, :], grp_logit[:, t, 0:GROUPS], ACT.Exp, bias=grp_neg[:, t:t + 1],
                               accum_out=grp_sum[:, t:t + 1]).then_inc(named("grp_exp_done"), 1)
            act.wait_ge(named("in_neg_made"), 1)
            for t in range(NT):
                act.activation(in_exp[:, t:t + 1], in_top[:, t, 1:2], ACT.Exp,
                               bias=in_neg[:, t:t + 1]).then_inc(named("in_exp_done"), 1)
            moe_pass(0)
            overflow(act, moe_pass)
            norm("fin1")
            def softmax_attention(stage):
                maps = SOFTMAX[stage]

                def exps(i):
                    d = maps[i]
                    act.wait_ge(named("max_made"), d["n"] + 1)
                    if i >= 2:
                        if maps[i - 2]["kind"] == "first":
                            act.wait_ge(named("probs_ready"), maps[i - 2]["turn"] + 1)
                        else:
                            act.wait_ge(named("probs_turned"), maps[i - 2]["turn"] + 1)
                    b = i % 2
                    for t in range(NT):
                        act.activation(both_tiles(sm_p[b], t), both_tiles(sm_s[b], t), ACT.Exp, bias=sm_max[b][:, t:t + 1],
                                       accum_out=sm_sum[b][:, t:t + 1]).then_inc(named("exp_done"), 1)

                def take_turned(d, before_last):
                    act.wait_ge(named("probs_turned"), d["turn"] + 1)
                    if before_last:
                        wait_read(act, before_last)
                    act.activation(sm_pT[d["turn"] % 2], ps[:, d["turn"] % 2, 0:MAPW], ACT.Copy).then_inc(named("turned_out"), 1)

                turned = [d for d in maps if d["kind"] != "first"]
                for i in range(MAPS + 2):
                    if i < MAPS:
                        exps(i)
                    if 1 <= i <= MAPS and maps[i - 1]["kind"] != "first":
                        j = turned.index(maps[i - 1])
                        take_turned(maps[i - 1], turned[j - 2] if j >= 2 else None)
                    if i >= 2 and maps[i - 2]["kind"] == "head":
                        take_av(maps[i - 2]["m"], maps[i - 2]["av"])

            norm("even")
            even = groups_of("even")
            take(*even[0])
            act.wait_ge(proj_out, even[0][0] + 1)
            for t in range(NT):
                act.activation(idx_relu[t][:, 0:LATENT], ckv_tok[:, t, :], ACT.Square,
                               accum_out=kv_ssq[:, t:t + 1]).then_inc(named("kv_ssq_done"), 1)
            act.wait_ge(named("kv_var_done"), 1)
            act.activation(kv_std, kv_std, ACT.Sqrt).then_inc(named("kv_std_done"), 1)
            take(*even[1])
            take(*even[2])
            act.wait_ge(named("lam_sum_made"), 1)
            act.activation(lam_exp, lam_sum, ACT.Exp).then_inc(named("lam_exp_done"), 1)

            def idx_relus(h):
                act.wait_ge(score_done, MAPS + h + 1)
                if h >= 2:
                    act.wait_ge(named("idx_summed"), h - 1)
                act.activation(idx_relu[h % 2], ps[:, 4 + h % 2, 0:MAPW], ACT.Relu, scale=HEAD ** -0.5).then_inc(named("idx_relu_done"), 1)

            act.wait_ge(named("kv_scaled"), 1)
            for i in range(4):
                idx_relus(2 * i)
                idx_relus(2 * i + 1)
                take(*even[3 + i])
            for n, g in even[7:9]:
                take(n, g)
            softmax_attention("even")
            act.wait_ge(named("diff_av"), DIFF_HEADS)
            act.activation(diff_sq.rearrange("p h t -> p (h t)"), ps[:, 2:4, :].rearrange("p b n -> p (b n)"),
                           ACT.Square).then_inc(named("diff_sq_done"), 1)
            act.wait_ge(named("diff_var_done"), 1)
            act.activation(diff_std[:, :, :], diff_std[:, :, :], ACT.Sqrt).then_inc(named("diff_std_done"), 1)
            def peer(stage):
                L = layer_of(stage)
                norm(stage)
                for b in range(4):
                    act.wait_ge(named("ht_psum"), 4 * (L + 1) + b + 1)
                    act.activation(h_tok[:, b // 2, (b % 2) * HALF:(b % 2 + 1) * HALF], ps[:, b, :],
                                   ACT.Copy).then_inc(named("h_tok_ready"), 1)
                act.wait_ge(named("keys_psum"), L + 1)
                act.activation(keysT.rearrange("p a n -> p (a n)"), ps[:, 4, 0:2 * P], ACT.Copy).then_inc(named("keysT_ready"), 1)
                for n, g in groups_of(stage):
                    take(n, g)
                act.wait_ge(named("gate_diff"), L + 1)
                act.activation(gate[:, :, :], gate[:, :, :], ACT.Exp).then_inc(named("gate_exp"), 1)

                def take_coef(g, m):
                    act.wait_ge(named("spread_done"), g * SUB + (2 + L * T // 4 + m + 1))
                    act.sem_inc(named("coef_begun"), 1)
                    act.activation(coef_all[:, bass.ds(g * BODY + 4 * m, 4), :], ps[:, 4 + m % 2, :].rearrange("p (t i) -> p t i", i=P),
                                   ACT.Copy).then_inc(named("coef_out"), 1)

                with act.Fori(0, BODIES) as g:
                    for b in range(BODY // RING + 1):
                        if b < BODY // RING:
                            act.wait_ge(named("dots_done"), g * BODY + (RING + L * T + (b + 1) * RING))
                            cols = slice(b * RING, (b + 1) * RING)
                            act.activation(gelu[:, cols], dots[:, cols], ACT.Gelu_apprx_tanh).then_inc(named("gelu_done"), 1)
                        if b >= 1:
                            for m in range(2 * (b - 1), 2 * b):
                                take_coef(g, m)

                by_key = coef_all.rearrange("p t i -> p i t")
                act.wait_ge(named("coef_out"), 2 + T // 4 * (L + 1))

                def take_keys(c, s):
                    act.activation(coef_ring[s], by_key[:, bass.ds(c * VI, VI), :], ACT.Copy).then_inc(named("keys_out"), 1)

                act.wait_ge(named("spread_done"), 2 + T // 4 * (L + 1))
                for s in range(2):
                    take_keys(s, s)
                with act.Fori(1, CHUNKS // 2) as m:
                    for s in range(2):
                        act.wait_ge(named("v_used"), 2 * m + (L * CHUNKS + s - 1))
                        act.sem_inc(named("keys_begun"), 1)
                        take_keys(2 * m + s, s)

            act.sem_inc(named("coef_out"), 2)
            peer("peer0")
            norm("odd")
            act.wait_ge(named("f_made"), 1)
            step(act.activation(f_abs[0:C_HEADS, :], f_logit[0:C_HEADS, :], ACT.Abs))
            step(act.activation(f_log[0:C_HEADS, :], f_abs[0:C_HEADS, :], ACT.Exp, scale=-1.0))
            act.activation(f_log[0:C_HEADS, :], f_log[0:C_HEADS, :], ACT.Ln, bias=1.0).then_inc(named("f_log_done"), 1)
            for n, g in groups_of("odd"):
                take(n, g)
            softmax_attention("odd")
            peer("peer1")
            norm("all")

        @block.tensor
        def _(pe):
            def project(n, g):
                pe.wait_ge(w_loaded[n % 3], w_turns(n))
                if n >= 2:
                    pe.wait_ge(proj_out, n - 1)
                w = wring[n % 3]
                nk = g["w"].shape[0] // P
                cols = g["w"].shape[1]
                b = 2 * (n % 2)
                src = g["src"]
                if g["kind"] == "F":
                    for f in range(cols // P):
                        for k in range(nk):
                            last = pe.matmul(ps[:, b + f // 2, (f % 2) * T:(f % 2 + 1) * T], w[:, k, f * P:(f + 1) * P],
                                             src[:, k, :], start=(k == 0), stop=(k == nk - 1))
                elif g["kind"] == "T":
                    for t in range(NT):
                        for k in range(nk):
                            last = pe.matmul(ps[:, b + t, 0:cols], src[:, k, t * P:(t + 1) * P], w[:, k, 0:cols],
                                             start=(k == 0), stop=(k == nk - 1))
                elif g["kind"] == "I":
                    for k in range(nk):
                        pe.matmul(ps[:, b, 0:T], w[:, k, 0:P], src[:, k, :], start=(k == 0), stop=(k == nk - 1))
                    for t in range(NT):
                        for k in range(nk):
                            last = pe.matmul(ps[:, b + 1, t * 8:(t + 1) * 8], src[:, k, t * P:(t + 1) * P], w[:, k, P:P + 8],
                                             start=(k == 0), stop=(k == nk - 1))
                else:
                    for k in range(nk):
                        last = pe.matmul(ps[0:cols, b, 0:T], w[:, k, 0:cols], src[:, k, :],
                                         start=(k == 0), stop=(k == nk - 1))
                last.then_inc(proj_done, 1)

            def transpose_norm(stage):
                n = NORM[stage][0]
                for b in range(4):
                    t, half = b // 2, b % 2
                    pe.wait_ge(xn_done, NT * n + t + 1)
                    for k in range(4):
                        last = pe.transpose(ps[:, b, k * P:(k + 1) * P], xn[:, t, (4 * half + k) * P:(4 * half + k + 1) * P],
                                            ident[:, :])
                    last.then_inc(xt_done, 1)
                pe.wait_ge(hT_done, 4 * (n + 1))

            def values(h, n, pT):
                if n >= 4:
                    pe.wait_ge(av_out, n - 3)
                lo = HEAD * (h % 2)
                o = ps[lo:lo + HEAD, 6 + (h // 2) % 2, 0:T]
                pe.matmul(o, v_tok[:, 0, h * HEAD:(h + 1) * HEAD], pT[:, 0:T], start=True, stop=False, skip_group_check=True)
                pe.matmul(ps[lo:lo + HEAD, 6 + (h // 2) % 2, P:T], v_tok[:, 1, h * HEAD:(h + 1) * HEAD], pT[:, T:MAPW],
                          start=False, stop=True, skip_group_check=True).then_inc(av_done, 1)

            pe.wait_ge(consts_made, 1)
            for a in range(3):
                pe.wait_ge(ada_summed, KC * (a + 1))
                pe.wait_ge(ada_bias_loaded, 16 * (a + 1))
                if a:
                    pe.wait_ge(ada_cols_out, a)
                    pe.wait_ge(ada_row_out, a)
                for vi, v in enumerate((0, 1, 3, 4)):
                    for k in range(KC):
                        o = ps[:, 4, vi * KC + k:vi * KC + k + 1]
                        cols = slice(v * D + k * P, v * D + (k + 1) * P)
                        pe.matmul(o, ada_acc[:, cols], ones[:, 0:1], start=True, stop=False)
                        pe.matmul(o, ada_bias[0:1, cols], ones[0:1, 0:1], start=False, stop=True)
                for vi, v in enumerate((2, 5)):
                    for half in range(2):
                        o = ps[0:1, 2 * vi + half, :]
                        cols = slice(v * D + half * HALF, v * D + (half + 1) * HALF)
                        pe.matmul(o, ones[:, 0:1], ada_acc[:, cols], start=True, stop=False)
                        last = pe.matmul(o, ones[0:1, 0:1], ada_bias[0:1, cols], start=False, stop=True)
                last.then_inc(ada_psum, 1)
            pe.wait_ge(ada_row_out, 3)
            pe.wait_ge(ada_cols_out, 3)

            transpose_norm("mix1")
            for n, g in groups_of("mix1")[:-2]:
                project(n, g)
            pe.wait_ge(proj_out, 6)

            def stick_scores(h):
                if h >= 2:
                    pe.wait_ge(named("stick_exp"), h - 1)
                q, k = map_q(h)
                z = ps[:, 4 + h % 2, :]
                pe.matmul(z[:, 0:T], k[:, 0:P], q, start=True, stop=False, skip_group_check=True)
                pe.matmul(z[:, T:MAPW], k[:, P:T], q[:, P:T], start=False, stop=True,
                          skip_group_check=True).then_inc(score_done, 1)

            def stick_sums(h):
                pe.wait_ge(named("stick_kept"), h + 1)
                z = ps[:, 4 + h % 2, :]
                keep = st_keep[h % 2]
                pe.matmul(z[:, 0:T], neg_tri[:, :], keep[:, 0:T], start=False, stop=False, skip_group_check=True)
                pe.matmul(z[:, P:T], neg_ones[:, :], keep[:, T:MAPW], start=False, stop=False, skip_group_check=True)
                pe.matmul(z[:, T:MAPW], neg_tri[:, :], keep[:, T:MAPW], start=False, stop=True,
                          skip_group_check=True).then_inc(named("stick_sum"), 1)

            for i in range(MAPS + 2):
                if i < MAPS:
                    stick_scores(i)
                if 1 <= i <= MAPS:
                    stick_sums(i - 1)
                if i >= 2:
                    pe.wait_ge(named("stick_mask"), i - 1)
                    values(i - 2, i - 2, st_a[i % 2])
            pe.wait_ge(av_out, MAPS)
            for n, g in groups_of("mix1")[-2:]:
                project(n, g)
            def moe_pass(p):
                def dispatch(e, b):
                    xi = p * (EXPERTS + 1) + e
                    pe.wait_ge(named("disp_made"), xi + 1)
                    pe.wait_ge(named("xe_ready"), xi + 1)
                    for k in range(KC):
                        for t in range(NT):
                            last = pe.matmul(ps[:, 4, k * SLOTS:(k + 1) * SLOTS], h_tok[:, t, k * P:(k + 1) * P], disp[b][:, t, :],
                                             start=(t == 0), stop=(t == NT - 1))
                    last.then_inc(named("xe_psum"), 1)

                pe.wait_ge(named("combT_ready"), p * PAIRS + 1)
                dispatch(0, 0)
                with pe.Fori(0, PAIRS) as i:
                    for b in range(2):
                        n = p * EXPERTS + 2 * i + b
                        e = 2 * i + b
                        pe.wait_ge(named(f"expert_loaded{b}"), (p * PAIRS + i) * 48 + 48)
                        pe.wait_ge(named("xe_ready"), p * (EXPERTS + 1) + e + 2)
                        pe.wait_ge(named("act_done"), n + 1)
                        for m in range(2):
                            for f in range(FF // P):
                                o = ps[:, 5, (m * 4 + f) * SLOTS:(m * 4 + f + 1) * SLOTS]
                                for k in range(KC):
                                    last = pe.matmul(o, moe_w[b][m][:, k, f * P:(f + 1) * P], xe[b][:, k, :],
                                                     start=(k == 0), stop=(k == KC - 1))
                        last.then_inc(named("gu_done"), 1)
                        if b == 1:
                            pe.wait_ge(named("combT_ready"), p * PAIRS + i + 2)
                        dispatch(e + 1, 1 - b)
                        pe.wait_ge(named("act_done"), n + 2)
                        pe.wait_ge(named("y_ready"), n + 1)
                        for half in range(2):
                            for f in range(FF // P):
                                last = pe.matmul(ps[SLOTS * b:SLOTS * (b + 1), 6 + half, :], act_e[b][:, f, :],
                                                 moe_w[b][2][:, f, half * HALF:(half + 1) * HALF],
                                                 start=(f == 0), stop=(f == FF // P - 1))
                        last.then_inc(named("y_done"), 1)
                        if b == 0:
                            pe.wait_ge(named("xe_ready"), p * (EXPERTS + 1) + e + 3)
                            for t in range(NT):
                                last = pe.transpose(ps[:, 4, t * P:(t + 1) * P], comb[:, t, :], ident[:, :])
                            last.then_inc(named("combT_psum"), 1)
                    pe.wait_ge(named("y_ready"), p * EXPERTS + 2 * i + 3)
                    for t in range(NT):
                        for half in range(2):
                            last = pe.matmul(ps[:, 2 * t + half, :], combT[:, t * P:(t + 1) * P], y_pair[:, half * HALF:(half + 1) * HALF],
                                             start=False, stop=True, skip_group_check=True)
                    last.then_inc(named("comb_done"), 1)

            transpose_norm("moe")
            for b in range(4):
                for k in range(4):
                    last = pe.transpose(ps[:, b, k * P:(k + 1) * P], hT[:, 4 * (b % 2) + k, (b // 2) * P:(b // 2 + 1) * P],
                                        ident[:, :])
                last.then_inc(named("ht_psum"), 1)
            pe.wait_ge(named("route_loaded"), 64)
            for t in range(NT):
                o = ps[:, 4, t * 64:t * 64 + GROUPS + EXPERTS]
                for k in range(KC):
                    pe.matmul(o, hT[:, k, t * P:(t + 1) * P], route_w[:, k, :], start=(k == 0), stop=False)
                last = pe.matmul(o, ones[0:1, :], route_b[0:1, :], start=False, stop=True)
            last.then_inc(named("logits_done"), 1)
            pe.wait_ge(named("chosen_made"), 1)
            pe.matmul(ps[:, 5, 0:EXPERTS], before[:, :], chosen[:, 0, :], start=True, stop=True)
            pe.matmul(ps[:, 5, 64:64 + EXPERTS], ones[:, :], chosen[:, 0, :], start=True, stop=False)
            pe.matmul(ps[:, 5, 64:64 + EXPERTS], before[:, :], chosen[:, 1, :], start=False, stop=True)
            pe.matmul(ps[:, 5, 128:128 + EXPERTS], ones[:, :], chosen[:, 0, :], start=True, stop=False)
            pe.matmul(ps[:, 5, 128:128 + EXPERTS], ones[:, :], chosen[:, 1, :], start=False, stop=True
                      ).then_inc(named("ranks_done"), 1)
            pe.wait_ge(named("h_tok_ready"), 4)
            for b in range(4):
                pe.matmul(ps[:, b, :], zeros[:, :], x[:, 0, 0:HALF], start=True, stop=False, skip_group_check=True)
            pe.sem_inc(named("comb_done"), 1)
            pe.sem_inc(named("xe_psum"), 1)
            pe.wait_ge(named("rank_made"), 1)
            moe_pass(0)
            overflow(pe, moe_pass)
            pe.matmul(ps[:, 0, :], zeros[:, :], x[:, 0, 0:HALF], start=False, stop=True,
                      skip_group_check=True).then_inc(named("moe_combined"), 1)
            def softmax_attention(stage):
                maps = SOFTMAX[stage]

                def scores(i):
                    d = maps[i]
                    if i >= 2:
                        pe.wait_ge(score_read, d["n"] - 1)
                    q, k = map_q(d["m"])
                    z = ps[:, 4 + i % 2, :]
                    forget = stage == "odd"
                    pe.matmul(z[:, 0:P], q[:, 0:P], k[:, 0:P], start=True, stop=False, skip_group_check=True)
                    last = pe.matmul(z[:, P:MAPW], q[:, P:T], k[:, 0:T], start=False, stop=not forget, skip_group_check=True)
                    if forget:
                        pick = neg_ident[0:C_HEADS, d["m"]:d["m"] + 1].broadcast_to([C_HEADS, P])
                        pe.matmul(z[:, 0:P], pick, f_cum[0:C_HEADS, 0:P], start=False, stop=False, skip_group_check=True)
                        last = pe.matmul(z[:, P:MAPW], pick, f_cum[0:C_HEADS, :], start=False, stop=True, skip_group_check=True)
                    last.then_inc(score_done, 1)

                def turn(d, before_last):
                    pe.wait_ge(named("probs_ready"), d["turn"] + 1)
                    if before_last:
                        pe.wait_ge(named("turned_out"), before_last["turn"] + 1)
                    p = sm_p[d["m"] % 2]
                    for c in range(3):
                        last = pe.transpose(ps[:, d["turn"] % 2, c * P:(c + 1) * P], p[:, c * P:(c + 1) * P], ident[:, :])
                    last.then_inc(named("probs_turned"), 1)

                def weigh(d):
                    pe.wait_ge(named("turned_out"), d["turn"] + 1)
                    pT = sm_pT[d["turn"] % 2]
                    if d["kind"] == "head":
                        values(d["m"], d["av"], pT)
                        return
                    v = v_tok[:, :, DSA_HEADS * HEAD + 2 * HEAD * d["hb"]:DSA_HEADS * HEAD + 2 * HEAD * (d["hb"] + 1)]
                    o = ps[:, 2 + d["hb"] // 2, (d["hb"] % 2) * T:(d["hb"] % 2 + 1) * T]
                    pe.matmul(o, v[:, 0, :], pT[:, 0:T], start=True, stop=False, skip_group_check=True)
                    pe.matmul(o[:, P:T], v[:, 1, :], pT[:, T:MAPW], start=False, stop=True,
                              skip_group_check=True).then_inc(named("diff_av"), 1)

                turned = [d for d in maps if d["kind"] != "first"]
                for i in range(MAPS + 2):
                    if i < MAPS:
                        scores(i)
                    if 1 <= i <= MAPS and maps[i - 1]["kind"] != "first":
                        j = turned.index(maps[i - 1])
                        turn(maps[i - 1], turned[j - 2] if j >= 2 else None)
                    if i >= 2 and maps[i - 2]["kind"] != "first":
                        weigh(maps[i - 2])

            transpose_norm("even")
            even = groups_of("even")
            project(*even[0])
            project(*even[1])
            project(*even[2])
            pe.wait_ge(named("kv_scaled"), 1)
            for c in range(LATENT // P):
                for t in range(NT):
                    last = pe.transpose(ps[:, 6, c * T + t * P:c * T + (t + 1) * P], ckv_tok[:, t, c * P:(c + 1) * P], ident[:, :])
            last.then_inc(named("kv_turned"), 1)

            def idx_scores(h):
                if h >= 2:
                    pe.wait_ge(named("idx_relu_done"), h - 1)
                lo = HEAD * (h % 2)
                q, k = qidx[lo:lo + HEAD, h // 2, :], kidx[lo:lo + HEAD, :]
                z = ps[:, 4 + h % 2, :]
                pe.matmul(z[:, 0:P], q[:, 0:P], k[:, 0:P], start=True, stop=False, skip_group_check=True)
                pe.matmul(z[:, P:MAPW], q[:, P:T], k[:, 0:T], start=False, stop=True, skip_group_check=True).then_inc(score_done, 1)

            pe.wait_ge(proj_out, even[2][0] + 1)
            for i in range(4):
                idx_scores(2 * i)
                idx_scores(2 * i + 1)
                project(*even[3 + i])
            pe.wait_ge(named("ckvT_ready"), 1)
            project(*even[7])
            project(*even[8])
            pe.wait_ge(proj_out, even[8][0] + 1)
            pe.wait_ge(named("idx_relu_done"), IDX_HEADS)
            softmax_attention("even")
            pe.wait_ge(named("diff_sq_done"), 1)
            pe.wait_ge(score_read, MAPS)
            for half in range(2):
                last = pe.matmul(ps[:, 4 + half, :], ones[:, :], diff_sq[:, 2 * half:2 * half + 2, :].rearrange("p h t -> p (h t)"),
                                 start=True, stop=True)
            last.then_inc(named("diff_summed"), 1)
            pe.wait_ge(named("diff_out"), 1)
            pe.wait_ge(av_out, MAPS + DSA_HEADS)
            for n, g in even[-2:]:
                project(n, g)
            def peer(stage):
                L = layer_of(stage)
                transpose_norm(stage)
                for b in range(4):
                    for k in range(4):
                        last = pe.transpose(ps[:, b, k * P:(k + 1) * P], hT[:, 4 * (b % 2) + k, (b // 2) * P:(b // 2 + 1) * P],
                                            ident[:, :])
                    last.then_inc(named("ht_psum"), 1)
                pe.wait_ge(named("keys_loaded"), 16 * (L + 1))
                for a in range(2):
                    last = pe.transpose(ps[:, 4, a * P:(a + 1) * P], keys_raw[:, a, :], ident[:, :])
                last.then_inc(named("keys_psum"), 1)
                pe.wait_ge(named("h_tok_ready"), 4 * (L + 2))
                for n, g in groups_of(stage):
                    project(n, g)
                pe.wait_ge(proj_out, groups_of(stage)[-1][0] + 1)
                pe.wait_ge(named("keysT_ready"), L + 1)
                for t in range(NT):
                    for q in range(HP):
                        last = pe.matmul(ps[:, (4 + 4 * t + q // 4) % 8, (q % 4) * P:(q % 4 + 1) * P], qkT[:, q, t * P:(t + 1) * P],
                                         keysT[:, q % 2, :], start=True, stop=True)
                        if q % 4 == 3:
                            last.then_inc(named("key_scores"), 1)
                pe.wait_ge(named("picks_made"), L + 1)
                for n, (bank, pick) in enumerate(((4, pick_i), (4, pick_j), (5, gate))):
                    for t in range(NT):
                        src = pick[:, t, :] if n < 2 else pick[:, t * PEER_HEADS:(t + 1) * PEER_HEADS, :].rearrange("p h k -> p (h k)")
                        last = pe.transpose(ps[:, bank, ((n % 2) * NT + t) * P:((n % 2) * NT + t + 1) * P], src, ident[:, :])
                last.then_inc(named("picks_psum"), 1)
                pe.wait_ge(named("h_parts_loaded"), 24 * 16 * (L + 1))
                pe.wait_ge(named("h_parts_cleared"), L + 1)
                pe.wait_ge(named("experts_made"), L + 1)

                def spread(g, m):
                    pe.wait_ge(named("hots_made"), g * SUB + (L * T // 4 + m + 1))
                    pe.wait_ge(named("coef_out"), g * SUB + (L * T // 4 + m + 1))
                    for j in range(4):
                        last = pe.matmul(ps[:, 4 + m % 2, j * P:(j + 1) * P], hot_j[m % 2][:, j, :], hot_i[m % 2][:, j, :],
                                         start=True, stop=True)
                    last.then_inc(named("spread_done"), 1)

                with pe.Fori(0, BODIES) as g:
                    for b in range(BODY // RING + 1):
                        if b < BODY // RING:
                            for s in range(RING):
                                i = b * RING + s
                                pe.wait_ge(named("dots_done"), g * BODY + (L * T + i + RING - 1))
                                for half in range(2):
                                    last = pe.matmul(ps[:, 2 * (i % 2) + half, :], token_sel[:, i:i + 1].broadcast_to([P, P]),
                                                     h_parts[:, bass.ds(g, 1), half * HALF:(half + 1) * HALF].rearrange("p g n -> p (g n)"),
                                                     start=True, stop=True)
                                last.then_inc(named("row_spread"), 1)
                        if b >= 1:
                            for m in range(2 * (b - 1), 2 * b):
                                spread(g, m)

                pe.wait_ge(named("dots_done"), RING + T * (L + 1))
                for b in range(4):
                    pe.matmul(ps[:, b, :], zeros[:, :], x[:, 0, 0:HALF], start=True, stop=False, skip_group_check=True)
                with pe.Fori(0, CHUNKS // 2) as m:
                    for s in range(2):
                        pe.wait_ge(named(f"v_loaded{s}"), m * 16 + (L * CHUNKS // 2 + 1) * 16)
                        pe.wait_ge(named("keys_out"), 2 * m + (L * CHUNKS + s + 1))
                        for i in range(VI):
                            for t in range(NT):
                                for half in range(2):
                                    last = pe.matmul(ps[:, 2 * t + half, :], coef_ring[s][:, i, t * P:(t + 1) * P],
                                                     v_rows[s][:, i, half * HALF:(half + 1) * HALF], start=False, stop=True,
                                                     skip_group_check=True)
                        last.then_inc(named("v_used"), 1)

            pe.sem_inc(named("spread_done"), 2)
            peer("peer0")
            transpose_norm("odd")
            odd = groups_of("odd")
            for n, g in odd[:-2]:
                project(n, g)
            pe.wait_ge(proj_out, odd[-3][0] + 1)
            pe.wait_ge(named("f_summed"), 1)
            softmax_attention("odd")
            pe.wait_ge(av_out, MAPS + DSA_HEADS + MAPS)
            for n, g in odd[-2:]:
                project(n, g)
            peer("peer1")

        @block.vector
        def _(dve):
            step = stepper(dve, dve_step)

            def rms(stage):
                n = x_updates(stage)
                dve.wait_ge(ssq_done, NT * (n + 1))
                dve.tensor_scalar(var[:, :], ssq[:, :], 1.0 / D, EPS, ALU.mult, ALU.add).then_inc(var_done, 1)
                dve.wait_ge(std_done, n + 1)
                step(dve.reciprocal(rstd[:, :], std[:, :]))

            def norm(stage):
                rms(stage)
                n, a, v = NORM[stage]
                for t in range(NT):
                    dve.tensor_scalar(xn[:, t, :], x[:, t, :], rstd[:, t:t + 1], None, ALU.mult).then_inc(xn_done, 1)
                if n == 0:
                    dve.wait_ge(vec_loaded, 128)
                step(dve.scalar_tensor_tensor(a_cols[:, :], mod_cols[:, a, v + 1, :], 1.0, gain_cols[:, n, :],
                                              ALU.add, ALU.mult))
                for b in range(4):
                    t, half = b // 2, b % 2
                    dve.wait_ge(xt_done, 4 * n + b + 1)
                    for j in range(4):
                        k = 4 * half + j
                        last = dve.tensor_scalar(hT[:, k, t * P:(t + 1) * P], ps[:, b, j * P:(j + 1) * P], a_cols[:, k:k + 1],
                                                 mod_cols[:, a, v, k:k + 1], ALU.mult, ALU.add)
                    last.then_inc(hT_done, 1)

            def residual(stage):
                r = x_updates(stage)
                dve.wait_ge(row_loaded, 16 * (r + 1))
                for half, (n, g) in enumerate(groups_of(stage)[-2:]):
                    dve.wait_ge(proj_done, n + 1)
                    b = 2 * (n % 2)
                    cols = slice(half * HALF, (half + 1) * HALF)
                    dve.tensor_tensor(xn[:, :, cols], ps[:, b:b + 2, :], row[:, cols].unsqueeze(1).broadcast_to([P, NT, HALF]),
                                      ALU.mult).then_inc(proj_out, 1)
                    dve.wait_ge(proj_out, n + 1)
                    if half == 0:
                        step(dve.tensor_tensor(x[:, :, cols], x[:, :, cols], xn[:, :, cols], ALU.add))
                    else:
                        dve.tensor_tensor(x[:, :, cols], x[:, :, cols], xn[:, :, cols], ALU.add).then_inc(x_done, 1)
                        dve.wait_ge(x_done, r + 1)

            dve.wait_ge(c_ready, 1)
            for a, (_, _, ci) in enumerate(ADA):
                if a:
                    dve.wait_ge(ada_psum, a)
                for k in range(KC):
                    n = a * KC + k
                    dve.wait_ge(ada_loaded[n % 2], 16 * (n // 2 + 1))
                    w = ada_ring[n % 2][:, :]
                    if k == 0:
                        dve.tensor_scalar(ada_acc[:, :], w, c_silu[:, ci, k:k + 1], None, ALU.mult).then_inc(ada_summed, 1)
                    else:
                        dve.scalar_tensor_tensor(ada_acc[:, :], w, c_silu[:, ci, k:k + 1], ada_acc[:, :], ALU.mult,
                                                 ALU.add).then_inc(ada_summed, 1)
                    dve.wait_ge(ada_summed, n + 1)
            dve.wait_ge(ada_cols_out, 3)
            dve.wait_ge(consts_made, 1)

            norm("mix1")
            for h in range(MAPS):
                dve.wait_ge(named("stick_ln"), h + 1)
                keep = st_keep[h % 2]
                step(dve.scalar_tensor_tensor(keep, ps[:, 4 + h % 2, 0:MAPW], 0.0, st_ln[h % 2], ALU.max, ALU.add))
                dve.tensor_tensor(diag_blocks(keep), diag_blocks(keep), before[:, :].unsqueeze(1).broadcast_to([P, 2, P]),
                                  ALU.mult).then_inc(named("stick_kept"), 1)
            residual("mix1")
            def moe_pass(p):
                def places(e, b):
                    xi = p * (EXPERTS + 1) + e
                    for t in range(NT):
                        dve.tensor_scalar(comb[:, t, SLOTS * b:SLOTS * (b + 1)], iota[:, 0:SLOTS], rank[:, t, bass.ds(e, 1)],
                                          weight[:, t, bass.ds(e, 1)], ALU.is_equal, ALU.mult)
                    for t in range(NT):
                        last = dve.tensor_scalar(disp[b][:, t, :], iota[:, 0:SLOTS], rank[:, t, bass.ds(e, 1)], None, ALU.is_equal)
                    last.then_inc(named("disp_made"), 1)

                places(0, 0)
                with dve.Fori(0, PAIRS) as i:
                    for b in range(2):
                        n = p * EXPERTS + 2 * i + b
                        if b == 1:
                            dve.wait_ge(named("combT_psum"), p * PAIRS + i + 1)
                            dve.wait_ge(named("comb_done"), p * PAIRS + i + 1)
                            dve.tensor_copy(combT, ps[:, 4, 0:T]).then_inc(named("combT_ready"), 1)
                        dve.wait_ge(named("xe_psum"), p * (EXPERTS + 1) + 2 * i + b + 1)
                        places(2 * i + b + 1, 1 - b)
                        dve.wait_ge(named("silu_done"), n + 1)
                        dve.tensor_tensor(act_e[b].rearrange("p f s -> p (f s)"), silu_g[b], ps[:, 5, HALF // 2:HALF],
                                          ALU.mult).then_inc(named("act_done"), 1)

            def moe_overflow(p):
                dve.wait_ge(named("comb_done"), p * PAIRS + 1)
                step_rank = named("rank_moved")
                dve.wait_ge(named("xe_psum"), p * (EXPERTS + 1) + 1)
                dve.tensor_scalar(rank[:, :, :], rank[:, :, :], -float(SLOTS), None, ALU.add).then_inc(step_rank, 1)
                dve.wait_ge(step_rank, p)
                moe_pass(p)

            def moe_route():
                step(dve.memset(grp_logit[:, :, :], LOWEST))
                step(dve.memset(weight[:, :, :], 0.0))
                step(dve.memset(rank[:, :, :], -1.0))
                dve.wait_ge(named("logits_done"), 1)
                logits = ps[:, 4, 0:128].rearrange("p (t n) -> p t n", t=NT)
                step(dve.tensor_copy(grp_logit[:, :, 0:GROUPS], logits[:, :, 0:GROUPS]))
                step(dve.tensor_copy(exp_logit[:, :, :], logits[:, :, GROUPS:GROUPS + EXPERTS]))
                for t in range(NT):
                    step(dve.max(grp_top[:, t, :], grp_logit[:, t, :]))
                    step(dve.max_index(grp_at[:, t, :], grp_top[:, t, :], grp_logit[:, t, :]))
                step(dve.tensor_copy(grp_num, grp_at[:, :, 0]))
                dve.tensor_scalar(grp_neg, grp_top[:, :, 0], -1.0, None, ALU.mult).then_inc(named("grp_neg_made"), 1)
                for t in range(NT):
                    step(dve.tensor_scalar(grp_hot[:, t, :], iota[:, 0:GROUPS], grp_num[:, t:t + 1], None, ALU.is_equal))
                    for g in range(GROUPS):
                        part = exp_logit[:, t, g * PER_GROUP:(g + 1) * PER_GROUP]
                        if g == 0:
                            step(dve.tensor_scalar(in_grp[:, t, :], part, grp_hot[:, t, 0:1], None, ALU.mult))
                        else:
                            step(dve.scalar_tensor_tensor(in_grp[:, t, :], part, grp_hot[:, t, g:g + 1], in_grp[:, t, :],
                                                          ALU.mult, ALU.add))
                    step(dve.max(in_top[:, t, :], in_grp[:, t, :]))
                    step(dve.max_index(in_at[:, t, :], in_top[:, t, :], in_grp[:, t, :]))
                dve.tensor_scalar(in_neg, in_top[:, :, 0], -1.0, None, ALU.mult).then_inc(named("in_neg_made"), 1)
                step(dve.tensor_copy(in_num[:, :, :], in_at[:, :, :]))
                for t in range(NT):
                    step(dve.scalar_tensor_tensor(expert[:, t, :], grp_num[:, t:t + 1].broadcast_to([P, 2]), float(PER_GROUP),
                                                  in_num[:, t, 0:2], ALU.mult, ALU.add))
                dve.wait_ge(named("grp_exp_done"), NT)
                step(dve.reciprocal(grp_p, grp_sum))
                dve.wait_ge(named("in_exp_done"), NT)
                step(dve.tensor_scalar(in_den, in_exp, 1.0, None, ALU.add))
                step(dve.reciprocal(in_den, in_den))
                step(dve.tensor_tensor(gate1, grp_p, in_den, ALU.mult))
                step(dve.tensor_tensor(gate2, gate1, in_exp, ALU.mult))
                for t in range(NT):
                    step(dve.tensor_scalar(hot1[:, t, :], iota[:, 0:EXPERTS], expert[:, t, 0:1], None, ALU.is_equal))
                    step(dve.tensor_scalar(hot2[:, t, :], iota[:, 0:EXPERTS], expert[:, t, 1:2], None, ALU.is_equal))
                dve.tensor_tensor(chosen[:, :, :], hot1[:, :, :], hot2[:, :, :], ALU.add).then_inc(named("chosen_made"), 1)
                dve.wait_ge(named("chosen_made"), 1)
                for t in range(NT):
                    step(dve.tensor_scalar(hot1[:, t, :], hot1[:, t, :], gate1[:, t:t + 1], None, ALU.mult))
                    step(dve.scalar_tensor_tensor(weight[:, t, 0:EXPERTS], hot2[:, t, :], gate2[:, t:t + 1], hot1[:, t, :],
                                                  ALU.mult, ALU.add))
                dve.wait_ge(named("ranks_done"), 1)
                counted = ps[:, 5, 0:128].rearrange("p (t n) -> p t n", t=NT)[:, :, 0:EXPERTS]
                step(dve.scalar_tensor_tensor(rank[:, :, 0:EXPERTS], counted, 1.0, chosen[:, :, :], ALU.add, ALU.mult))
                step(dve.tensor_scalar(rank[:, :, 0:EXPERTS], rank[:, :, 0:EXPERTS], -1.0, None, ALU.add))
                step(dve.tensor_reduce(most[:, 0:1], ps[:, 5, 128:128 + EXPERTS], AX_X, ALU.max))
                step(dve.tensor_scalar(most[:, 1:2], most[:, 0:1], SLOTS + 0.5, 1.0, ALU.is_gt, ALU.add))
                for more in range(2, T // SLOTS):
                    step(dve.scalar_tensor_tensor(most[:, more:more + 1], most[:, 0:1], more * SLOTS + 0.5, most[:, more - 1:more],
                                                  ALU.is_gt, ALU.add))
                dve.tensor_copy(passes[:, :], most[:, T // SLOTS - 1:T // SLOTS]).then_inc(named("passes_known"), 1)
                dve.sem_inc(named("rank_made"), 1)

            def residual_banks(stage, done):
                r = x_updates(stage)
                dve.wait_ge(row_loaded, 16 * (r + 1))
                for t in range(NT):
                    step(dve.tensor_tensor(xn[:, t, :], ps[:, 2 * t:2 * t + 2, :].rearrange("p b n -> p (b n)"), row[:, :], ALU.mult))
                dve.tensor_tensor(x[:, :, :], x[:, :, :], xn[:, :, :], ALU.add).then_inc(x_done, 1)
                dve.wait_ge(x_done, r + 1)

            def norm_rows(stage):
                rms(stage)
                r = x_updates(stage)
                dve.wait_ge(row_loaded, 16 * (r + 1))
                for t in range(NT):
                    last = dve.scalar_tensor_tensor(x[:, t, :], x[:, t, :], rstd[:, t:t + 1], row[:, :], ALU.mult, ALU.mult)
                    if t < NT - 1:
                        step(last)
                last.then_inc(x_done, 1)
                dve.wait_ge(x_done, r + 1)

            norm("moe")
            moe_route()
            dve.sem_inc(named("act_done"), 1)
            dve.sem_inc(named("combT_ready"), 1)
            moe_pass(0)
            overflow(dve, moe_overflow)
            dve.wait_ge(named("moe_combined"), 1)
            residual_banks("moe", None)
            norm_rows("fin1")
            def softmax_attention(stage, add):
                maps = SOFTMAX[stage]

                def scored(i):
                    d = maps[i]
                    b = i % 2
                    dve.wait_ge(score_done, MAPS + IDX_HEADS + d["n"] + 1)
                    dve.tensor_tensor(sm_s[b], ps[:, 4 + b, 0:MAPW], add(d["m"]), ALU.add).then_inc(score_read, 1)
                    dve.wait_ge(score_read, d["n"] + 1)
                    for t in range(NT):
                        last = dve.tensor_reduce(sm_max[b][:, t:t + 1], both_tiles(sm_s[b], t), AX_X, ALU.max, negate=True)
                    last.then_inc(named("max_made"), 1)

                def normed(i):
                    d = maps[i]
                    b = i % 2
                    dve.wait_ge(named("exp_done"), NT * (d["n"] + 1))
                    step(dve.reciprocal(sm_inv[b], sm_sum[b]))
                    if d["kind"] == "second":
                        step(dve.tensor_scalar(sm_inv[b], sm_inv[b], neg_lam[:, 0:1], None, ALU.mult))
                        for t in range(NT):
                            last = dve.scalar_tensor_tensor(both_tiles(sm_p[b], t), both_tiles(sm_p[b], t), sm_inv[b][:, t:t + 1],
                                                            both_tiles(sm_p[1 - b], t), ALU.mult, ALU.add)
                    else:
                        for t in range(NT):
                            last = dve.tensor_scalar(both_tiles(sm_p[b], t), both_tiles(sm_p[b], t), sm_inv[b][:, t:t + 1], None, ALU.mult)
                    if d["kind"] == "first":
                        step(last)
                    else:
                        last.then_inc(named("probs_ready"), 1)

                for i in range(MAPS + 1):
                    if i < MAPS:
                        scored(i)
                    if i >= 1:
                        normed(i - 1)

            norm("even")
            dve.wait_ge(named("kv_ssq_done"), NT)
            dve.tensor_scalar(kv_std, kv_ssq, 1.0 / LATENT, EPS, ALU.mult, ALU.add).then_inc(named("kv_var_done"), 1)
            dve.wait_ge(named("kv_std_done"), 1)
            step(dve.reciprocal(kv_std, kv_std))
            for t in range(NT):
                last = dve.tensor_scalar(ckv_tok[:, t, :], ckv_tok[:, t, :], kv_std[:, t:t + 1], None, ALU.mult)
            last.then_inc(named("kv_scaled"), 1)
            dve.wait_ge(named("even_vec_loaded"), 16 * 3)
            lam_pairs = lam_vec.rearrange("p (a b) d -> p a b d", b=2)
            step(dve.tensor_tensor(lam_prod[:, :, :], lam_pairs[:, :, 0, :], lam_pairs[:, :, 1, :], ALU.mult))
            dve.tensor_reduce(lam_sum, lam_prod[:, :, :], AX_X, ALU.add).then_inc(named("lam_sum_made"), 1)
            step(dve.tensor_scalar(subln_col, subln_raw, 1.0 - LAM_INIT, None, ALU.mult))
            dve.wait_ge(named("lam_exp_done"), 1)
            step(dve.tensor_tensor(neg_lam, lam_exp[:, 1:2], lam_exp[:, 0:1], ALU.subtract))
            step(dve.tensor_scalar(neg_lam, neg_lam, -LAM_INIT, None, ALU.add))
            dve.wait_ge(named("kv_turned"), 1)
            for c in range(LATENT // P):
                last = dve.tensor_scalar(ckvT[:, c, :], ps[:, 6, c * T:(c + 1) * T], kv_gain[:, c:c + 1], None, ALU.mult)
            last.then_inc(named("ckvT_ready"), 1)
            dve.wait_ge(proj_out, groups_of("even")[2][0] + 1)
            for h in range(IDX_HEADS):
                dve.wait_ge(named("idx_relu_done"), h + 1)
                if h == 0:
                    for t in range(NT):
                        last = dve.tensor_scalar(both_tiles(idx_score, t), both_tiles(idx_relu[0], t), widx[:, t, 0:1], 0.0, ALU.mult, ALU.add)
                else:
                    for t in range(NT):
                        last = dve.scalar_tensor_tensor(both_tiles(idx_score, t), both_tiles(idx_relu[h % 2], t), widx[:, t, h:h + 1],
                                                        both_tiles(idx_score, t), ALU.mult, ALU.add)
                last.then_inc(named("idx_summed"), 1)
                dve.wait_ge(named("idx_summed"), h + 1)
            dve.wait_ge(named("idx_causal"), 1)
            for r in range(DSA_TOP // 8):
                for t in range(NT):
                    step(dve.max(idx_top, both_tiles(idx_score, t)))
                    step(dve.match_replace(both_tiles(idx_score, t), idx_top, both_tiles(idx_score, t), TAKEN))
            step(dve.tensor_scalar(idx_mask, idx_score, TAKEN, NEG, ALU.not_equal, ALU.mult))
            dve.wait_ge(named("rel_loaded"), 32)
            dsa_maps = rel_maps[:, 0:DSA_HEADS, :]
            step(dve.tensor_tensor(dsa_maps, dsa_maps, idx_mask.unsqueeze(1).broadcast_to([P, DSA_HEADS, MAPW]), ALU.add))
            softmax_attention("even", lambda m: rel_maps[:, m if m < DSA_HEADS else (m + DSA_HEADS) // 2, :])
            dve.wait_ge(named("diff_summed"), 1)
            dve.tensor_scalar(diff_std.rearrange("p h t -> p (h t)"), ps[:, 4:6, :].rearrange("p b n -> p (b n)"), 0.5 / HEAD, EPS,
                              ALU.mult, ALU.add).then_inc(named("diff_var_done"), 1)
            dve.wait_ge(named("diff_std_done"), 1)
            step(dve.reciprocal(diff_std[:, :, :], diff_std[:, :, :]))
            dve.scalar_tensor_tensor(oT[:, 4:8, :].rearrange("p h t -> p (h t)"), ps[:, 2:4, :].rearrange("p b n -> p (b n)"),
                                     subln_col[:, 0:1], diff_std.rearrange("p h t -> p (h t)"), ALU.mult, ALU.mult
                                     ).then_inc(named("diff_out"), 1)
            residual("even")
            def peer(stage):
                L = layer_of(stage)
                norm(stage)
                dve.wait_ge(named("h_tok_ready"), 4 * (L + 2))
                step(dve.tensor_copy(part_hi[:, :, :], h_tok[:, :, :]))
                step(dve.tensor_tensor(part_rest[:, :, :], h_tok[:, :, :], part_hi[:, :, :], ALU.subtract))
                step(dve.tensor_copy(part_mid[:, :, :], part_rest[:, :, :]))
                dve.tensor_tensor(part_lo[:, :, :], part_rest[:, :, :], part_mid[:, :, :], ALU.subtract).then_inc(named("parts_made"), 1)
                for f in range(NT * HP // 4):
                    dve.wait_ge(named("key_scores"), NT * HP // 4 * L + f + 1)
                    rows = [(4 * f + j, ps[:, (4 + f) % 8, j * P:(j + 1) * P], key_left[:, j, :]) for j in range(4)]
                    for r, s, _ in rows:
                        last = dve.max(key_top[:, r, 0:8], s)
                    step(last)
                    for r, s, left in rows:
                        dve.max_index(key_at[:, r, 0:8], key_top[:, r, 0:8], s)
                        last = dve.match_replace(left, key_top[:, r, 0:8], s, LOWEST)
                    step(last)
                    for r, _, left in rows:
                        last = dve.max(key_top[:, r, 8:16], left)
                    step(last)
                    for r, _, left in rows:
                        last = dve.max_index(key_at[:, r, 8:16], key_top[:, r, 8:16], left)
                    step(last)
                step(dve.tensor_copy(key_num[:, :, :], key_at[:, :, :]))
                for t in range(NT):
                    first = slice(t * HP, (t + 1) * HP, 2)
                    second = slice(t * HP + 1, (t + 1) * HP, 2)
                    square = [P, PEER_HEADS, PEER_K, PEER_K]
                    step(dve.tensor_tensor(cand.rearrange("p h (a b) -> p h a b", b=PEER_K),
                                           key_top[:, first, :].unsqueeze(3).broadcast_to(square),
                                           key_top[:, second, :].unsqueeze(2).broadcast_to(square), ALU.add))
                    heads = [(t * PEER_HEADS + h, cand[:, h, :], cand_left[:, h, :]) for h in range(PEER_HEADS)]
                    for r, s, _ in heads:
                        last = dve.max(best[:, r, 0:8], s)
                    step(last)
                    for r, s, left in heads:
                        dve.max_index(best_at[:, r, 0:8], best[:, r, 0:8], s)
                        last = dve.match_replace(left, best[:, r, 0:8], s, LOWEST)
                    step(last)
                    for r, _, left in heads:
                        last = dve.max(best[:, r, 8:16], left)
                    step(last)
                    for r, _, left in heads:
                        last = dve.max_index(best_at[:, r, 8:16], best[:, r, 8:16], left)
                    step(last)
                    flat = best_at[:, t * PEER_HEADS:(t + 1) * PEER_HEADS, :].rearrange("p h k -> p (h k)")
                    dve.tensor_scalar(best_hi, flat, 4, None, ALU.logical_shift_right)
                    step(dve.tensor_scalar(best_lo, flat, PEER_K - 1, None, ALU.bitwise_and))
                    dve.tensor_copy(best_row, best_hi)
                    step(dve.tensor_copy(best_col, best_lo))
                    for side, place, pick in ((first, best_row, pick_i), (second, best_col, pick_j)):
                        step(dve.tensor_tensor(match[:, :, :], iota[:, 0:PEER_K].unsqueeze(1).broadcast_to([P, P, PEER_K]),
                                               place.unsqueeze(2).broadcast_to([P, P, PEER_K]), ALU.is_equal))
                        as_heads = match.rearrange("p (h k) m -> p h k m", h=PEER_HEADS)
                        step(dve.tensor_tensor(as_heads, as_heads, key_num[:, side, :].unsqueeze(2).broadcast_to(square), ALU.mult))
                        step(dve.tensor_reduce(pick[:, t, :], match[:, :, :], AX_X, ALU.add))
                full = [P, NT * PEER_HEADS, PEER_K]
                dve.tensor_tensor(gate[:, :, :], best[:, :, :], best[:, :, 0:1].broadcast_to(full), ALU.subtract
                                  ).then_inc(named("gate_diff"), 1)
                dve.wait_ge(named("gate_exp"), L + 1)
                step(dve.tensor_reduce(gate_sum, gate[:, :, :], AX_X, ALU.add))
                step(dve.reciprocal(gate_sum, gate_sum))
                dve.tensor_tensor(gate[:, :, :], gate[:, :, :], gate_sum.unsqueeze(2).broadcast_to(full), ALU.mult
                                  ).then_inc(named("picks_made"), 1)
                dve.wait_ge(named("picks_psum"), L + 1)
                dve.tensor_copy(peer_i[:, :], ps[:, 4, 0:T])
                dve.tensor_copy(peer_j[:, :], ps[:, 4, T:2 * T])
                step(dve.tensor_copy(peer_g[:, :], ps[:, 5, 0:T]))
                step(dve.scalar_tensor_tensor(peer_num[:, :], peer_i[:, :], float(NKEYS), peer_j[:, :], ALU.mult, ALU.add))
                dve.tensor_scalar(peer_e[:, :], peer_num[:, :], float(L * PEER_EXPERTS), None, ALU.add).then_inc(named("experts_made"), 1)

                def hots(g, b):
                    n = g * (BODY // RING) + (L * T // RING + b + 1)
                    cols = slice(b * RING, (b + 1) * RING)
                    dve.wait_ge(named("gelu_done"), n)
                    dve.tensor_tensor(coef[:, cols], gelu[:, cols], peer_g[:, bass.ds(g * BODY + b * RING, RING)], ALU.mult
                                      ).then_inc(named("coef_made"), 1)
                    dve.wait_ge(named("coef_made"), n)
                    for m in range(2 * b, 2 * b + 2):
                        dve.wait_ge(named("spread_done"), g * SUB + (L * T // 4 + m + 1))
                        for j in range(4):
                            i = 4 * m + j
                            dve.tensor_scalar(hot_i[m % 2][:, j, :], iota[:, :], peer_i[:, bass.ds(g * BODY + i, 1)], coef[:, i:i + 1],
                                              ALU.is_equal, ALU.mult)
                            last = dve.tensor_scalar(hot_j[m % 2][:, j, :], iota[:, :], peer_j[:, bass.ds(g * BODY + i, 1)], None,
                                                     ALU.is_equal)
                        last.then_inc(named("hots_made"), 1)

                with dve.Fori(0, BODIES) as g:
                    for b in range(BODY // RING + 1):
                        if b < BODY // RING:
                            for s in range(RING):
                                i = b * RING + s
                                dve.wait_ge(named(f"u_loaded{s}"), g * (16 * BODY // RING) + (L * T // RING + b + 1) * 16)
                                dve.wait_ge(named("row_spread"), g * BODY + (L * T + i + 1))
                                dve.tensor_tensor_reduce(u_rows[s], u_rows[s], ps[:, 2 * (i % 2):2 * (i % 2) + 2, :].rearrange(
                                    "p b n -> p (b n)"), 1.0, 0.0, ALU.mult, ALU.add, dots[:, i:i + 1]).then_inc(named("dots_done"), 1)
                        if b >= 1:
                            hots(g, b - 1)
                dve.wait_ge(named("v_used"), CHUNKS * (L + 1))
                residual_banks(stage, None)

            dve.sem_inc(named("dots_done"), RING)
            peer("peer0")
            norm("odd")
            n = groups_of("odd")[0][0]
            dve.wait_ge(proj_done, n + 1)
            dve.wait_ge(named("forget_loaded"), 16)
            step(dve.tensor_scalar(f_logit[0:C_HEADS, :], ps[0:C_HEADS, 2 * (n % 2), 0:T], forget_col[0:C_HEADS, 0:1], None, ALU.add))
            dve.sem_inc(proj_out, 1)
            dve.sem_inc(named("f_made"), 1)
            dve.wait_ge(named("f_log_done"), 1)
            step(dve.scalar_tensor_tensor(f_log[0:C_HEADS, :], f_logit[0:C_HEADS, :], 0.0, f_log[0:C_HEADS, :], ALU.min, ALU.subtract))
            step(dve.tensor_tensor_scan(f_cum[0:C_HEADS, :], ones[0:C_HEADS, 0:1].broadcast_to([C_HEADS, T]), f_log[0:C_HEADS, :],
                                        0.0, ALU.mult, ALU.add))
            dve.tensor_scalar(neg_ident[0:C_HEADS, :], ident[0:C_HEADS, 0:C_HEADS], -1.0, None, ALU.mult).then_inc(named("f_summed"), 1)
            softmax_attention("odd", lambda m: causal_add[:, :])
            residual("odd")
            peer("peer1")
            norm_rows("all")


INPUTS = [
    "x", "c", "ada_w", "ada_b", "norm_g", "final_g", "sb_w_in", "sb_w_out", "moe_w_grp", "moe_b_grp", "moe_w_exp",
    "moe_b_exp", "moe_w_gate", "moe_w_up", "moe_w_down", "c_2", "rel_bias_2", "ada_w_2", "ada_b_2", "norm_mix_2",
    "norm_ffn_2", "norm_final_2", "even_w_in_2", "even_w_out_2", "a_kv_norm_2", "a_w_uk_2", "a_w_uv_2", "b_lambda_2",
    "b_subln_2", "odd_w_in_2", "odd_b_forget_2", "odd_w_out_2", "peer_w_q_2", "peer_sub_keys_2", "peer_u_2", "peer_v_2",
]


def kernel(**inputs):
    import numpy as np
    import concourse.bacc as bacc
    from concourse.bass_utils import run_bass_kernel_spmd

    nc = bacc.Bacc("TRN2", target_bir_lowering=False, num_devices=1)
    arrays, args = {}, {}
    for name in INPUTS:
        a = np.ascontiguousarray(inputs[name])
        arrays["in_" + name] = a
        args[name] = nc.dram_tensor("in_" + name, a.shape, mybir.dt.from_np(a.dtype), kind="ExternalInput").ap()
    out = nc.dram_tensor("out_x", (1, T, D), F32, kind="ExternalOutput").ap()
    two_block_kernel(nc, args, out)
    r = run_bass_kernel_spmd(nc, [arrays], core_ids=[0])
    return r.results[0]["out_x"]
```

```python
import math
from contextlib import ExitStack

import concourse.bass as bass
from concourse import mybir

F32 = mybir.dt.float32
BF16 = mybir.dt.bfloat16
U32 = mybir.dt.uint32
I32 = mybir.dt.int32
ALU = mybir.AluOpType
ACT = mybir.ActivationFunctionType
AX_X = mybir.AxisListType.X

P = 128
D = 1024
KC = D // P
T = 256
NT = T // P
HALF = D // 2
EPS = 1e-6
NEG = -1e30
LOWEST = -3.0e38
TAKEN = -3.3e38

HEAD = 64
MAPS = 16
SCALE = HEAD ** -0.5
MAPW = 3 * P

IDX_HEADS = 8
DSA_TOP = 64
DSA_HEADS = 8
DIFF_HEADS = 4
LATENT = 256
REL_BUCKETS = 32
REL_HEADS = 12

GROUPS = 4
PER_GROUP = 8
EXPERTS = 32
FF = 512
SLOTS = 64

PEER_HEADS = 8
PEER_K = 16
NKEYS = 128
PEER_EXPERTS = NKEYS * NKEYS
RING = 8
BODY = 32


def rel_bucket_ranges():
    exact = REL_BUCKETS // 2
    bucket = []
    for d in range(T):
        if d < exact:
            bucket.append(d)
        else:
            bucket.append(min(REL_BUCKETS - 1, exact + int(math.log(d / exact) / math.log(128 / exact) * exact)))
    return [(b, bucket.index(b), T - 1 - bucket[::-1].index(b)) for b in sorted(set(bucket))]


def two_block_kernel(nc, I, out):
    with ExitStack() as ctx:
        def sb(name, shape, dt=F32):
            return ctx.enter_context(nc.sbuf_tensor("sb_" + name, shape, dt))

        def sem(name):
            return ctx.enter_context(nc.semaphore(name))

        ps = ctx.enter_context(nc.psum_tensor("psum", [P, 8, HALF], F32))
        rel_rows_d = nc.dram_tensor("rel_rows_d", [REL_HEADS, P, MAPW], F32).ap()

        x = sb("x", [P, NT, D])
        row = sb("row", [P, D])
        ident = sb("ident", [P, P])
        iota = sb("iota", [P, P])
        ones = sb("ones", [P, P])
        zeros = sb("zeros", [P, P])
        neg_ones = sb("neg_ones", [P, P])
        neg_tri = sb("neg_tri", [P, P])
        before = sb("before", [P, P])
        causal_add = sb("causal_add", [P, MAPW])
        token_sel = sb("token_sel", [P, BODY], BF16)
        vec_cols = sb("vec_cols", [P, 2, 112])
        mod_cols = sb("mod_cols", [P, 3, 6, KC])
        c_silu = sb("c_silu", [P, 2 * KC])
        a_cols = sb("a_cols", [P, KC])
        ssq = sb("ssq", [P, NT])
        var = sb("var", [P, NT])
        std = sb("std", [P, NT])
        rstd = sb("rstd", [P, NT])
        small = sb("small", [P, 256])
        peer_i = sb("peer_i", [P, T])
        peer_neg_j = sb("peer_neg_j", [P, T])
        peer_g = sb("peer_g", [P, T])
        peer_e = sb("peer_e", [P, T], U32)
        passes = sb("passes", [P, 1], I32)

        AREA = 47104
        area = sb("area", [P, AREA])

        def view(at, *shape, dt=F32):
            n = math.prod(shape)
            words = n if dt != BF16 else n // 2
            assert at + words <= AREA, (at, shape)
            v = area[:, at:at + words]
            if dt != F32:
                v = v.bitcast(dt)
            if len(shape) == 2:
                v = v.rearrange("p (a b) -> p a b", b=shape[1])
            if len(shape) == 3:
                v = v.rearrange("p (a b c) -> p a b c", b=shape[1], c=shape[2])
            return v

        hT = view(0, KC, T)
        xn = view(2048, NT, D)
        wring = [view(4096 + 4096 * i, KC, HALF) for i in range(3)]
        qkT = view(16384, MAPS, T)
        v_tok = view(20480, NT, D)
        oT = view(22528, KC, T)
        AT = 24576
        vec_raw = view(2048, 2, P)
        THIRD = 2 * D
        PIECES = 9 * KC
        EARLY = 6 * KC
        ADA_AT = 28416
        ada_acc = {"mix1": [view(ADA_AT + THIRD * i, THIRD) for i in range(2)]}
        ada_ring = {"mix1": [view(ADA_AT + THIRD * (2 + i), THIRD) for i in range(6)]}

        def ada_stage(n):
            return ("mix1", n) if n < EARLY else ("even", n - EARLY)

        consts_made = sem("consts_made")
        vec_loaded = sem("vec_loaded")
        x_loaded = sem("x_loaded")
        x_done = sem("x_done")
        row_loaded = sem("row_loaded")
        ada_loaded = [sem(f"ada_loaded{i}") for i in range(6)]
        ada_used = sem("ada_used")
        c_ready = sem("c_ready")
        ada_sums = sem("ada_sums")
        mod_made = sem("mod_made")
        ident_made = sem("ident_made")
        ssq_done = sem("ssq_done")
        var_done = sem("var_done")
        std_done = sem("std_done")
        xn_done = sem("xn_done")
        xt_done = sem("xt_done")
        hT_done = sem("hT_done")
        w_loaded = [sem(f"w_loaded{i}") for i in range(3)]
        proj_done = sem("proj_done")
        proj_out = sem("proj_out")
        score_done = sem("score_done")
        score_read = sem("score_read")
        av_done = sem("av_done")
        av_out = sem("av_out")
        dve_step = sem("dve_step")
        act_step = sem("act_step")
        pool_step = sem("pool_step")
        stored = sem("stored")
        sems = {}

        def named(name):
            if name not in sems:
                sems[name] = sem(name)
            return sems[name]

        def stepper(eng, step_sem):
            n = [0]

            def step(ins):
                n[0] += 1
                ins.then_inc(step_sem, 1)
                eng.wait_ge(step_sem, n[0])
            return step

        groups = []

        def group(stage, w, kind, src, dst, scale=1.0, by="act", dup=0):
            groups.append(dict(stage=stage, w=w, kind=kind, src=src, dst=dst, scale=scale, by=by, dup=dup))

        ckvT = view(AT, 2, T)
        ckv_tok = view(AT + 512, NT, LATENT)
        kidx = view(AT + 1024, T)
        widx = view(AT + 1280, NT, IDX_HEADS)
        qidx = view(AT + 1312, 4, T)
        EV = AT + 1312 + 1024
        f_cum = view(AT, T)

        def sb_groups():
            w = I["sb_w_in"][0]
            for g in range(4):
                group("mix1", w[:, g * HALF:(g + 1) * HALF], "F", hT, qkT[:, 4 * g:4 * g + 4, :], SCALE if g < 2 else 1.0)
            for g in range(2):
                group("mix1", w[:, (4 + g) * HALF:(5 + g) * HALF], "T", hT, v_tok[:, :, g * HALF:(g + 1) * HALF])
            for g in range(2):
                group("mix1", I["sb_w_out"][0][:, g * HALF:(g + 1) * HALF], "T", oT, g, by="residual")

        def even_groups():
            w = I["even_w_in_2"][0]
            a, i, kk = 512 + LATENT, 512 + LATENT + 512, 512 + LATENT + 512 + 64
            b = kk + 8
            group("even", w[:, 512:a], "T", hT, ckv_tok)
            group("even", w[:, a:i], "F", hT, qidx)
            group("even", w[:, i:b], "I", hT, None)
            group("even", w[:, 0:512], "F", hT, qkT[:, 0:4, :], SCALE)
            group("even", w[:, b:b + 512], "F", hT, qkT[:, 4:8, :], SCALE)
            group("even", w[:, b + 512:b + 1024], "F", hT, qkT[:, 12:16, :])
            group("even", w[:, b + 1024:b + 1536], "T", hT, v_tok[:, :, 512:1024])
            group("even", I["a_w_uk_2"][0].rearrange("c h d -> c (h d)"), "F", ckvT, qkT[:, 8:12, :])
            group("even", I["a_w_uv_2"][0].rearrange("c h d -> c (h d)"), "T", ckvT, v_tok[:, :, 0:512])
            for g in range(2):
                group("even", I["even_w_out_2"][0][:, g * HALF:(g + 1) * HALF], "T", oT, g, by="residual")

        def odd_groups():
            w = I["odd_w_in_2"][0]
            group("odd", w[:, 3072:3088], "C", hT, None, by="dve")
            for g in range(4):
                group("odd", w[:, g * HALF:(g + 1) * HALF], "F", hT, qkT[:, 4 * g:4 * g + 4, :], SCALE if g < 2 else 1.0)
            for g in range(2):
                group("odd", w[:, (4 + g) * HALF:(5 + g) * HALF], "T", hT, v_tok[:, :, g * HALF:(g + 1) * HALF])
            for g in range(2):
                group("odd", I["odd_w_out_2"][0][:, g * HALF:(g + 1) * HALF], "T", oT, g, by="residual")

        def peer_groups(layer):
            w = I["peer_w_q_2"][layer]
            for g in range(4):
                group(f"peer{layer}", w[:, g * HALF:(g + 1) * HALF], "F", hT, qkT[:, 4 * g:4 * g + 4, :])

        sb_groups()
        even_groups()
        peer_groups(0)
        odd_groups()
        peer_groups(1)

        def groups_of(stage):
            return [(n, g) for n, g in enumerate(groups) if g["stage"] == stage]

        def w_turns(n):
            return sum(32 if g["kind"] == "I" else 16 for g in groups[n % 3:n + 1:3])

        def x_updates(stage):
            return {"mix1": 0, "moe": 1, "fin1": 2, "even": 3, "peer0": 4, "odd": 5, "peer1": 6, "all": 7}[stage]

        NORM = {"mix1": (0, 0, 0), "moe": (1, 0, 3), "even": (2, 1, 0), "peer0": (3, 1, 3), "odd": (4, 2, 0), "peer1": (5, 2, 3)}
        GAINS = [I["norm_g"][0, 0], I["norm_g"][0, 1], I["norm_mix_2"][0], I["norm_ffn_2"][0], I["norm_mix_2"][1],
                 I["norm_ffn_2"][1]]
        h_tok = view(2048, NT, D)
        moe_at = ((24576, 24576 + 4096, 24576 + 8192), (36864, 36864 + 4096, 4096))
        moe_w = [[view(moe_at[b][i], (KC, KC, FF // P)[i], (FF, FF, D)[i]) for i in range(3)] for b in range(2)]
        M = 8192
        route_w = view(M, KC, GROUPS + EXPERTS)
        route_b = view(M + 288, GROUPS + EXPERTS)
        grp_logit = view(M + 352, NT, 8)
        exp_logit = view(M + 368, NT, EXPERTS)
        grp_top = view(M + 432, NT, 8)
        grp_at = view(M + 448, NT, 8, dt=U32)
        grp_num = view(M + 464, NT)
        grp_neg = view(M + 466, NT)
        grp_exp = view(M + 468, NT, GROUPS)
        grp_sum = view(M + 476, NT)
        grp_p = view(M + 478, NT)
        grp_hot = view(M + 480, NT, GROUPS)
        in_grp = view(M + 488, NT, PER_GROUP)
        in_top = view(M + 504, NT, 8)
        in_at = view(M + 520, NT, 8, dt=U32)
        in_num = view(M + 536, NT, 8)
        in_neg = view(M + 552, NT)
        in_exp = view(M + 554, NT)
        in_den = view(M + 556, NT)
        gate1 = view(M + 558, NT)
        gate2 = view(M + 560, NT)
        expert = view(M + 562, NT, 2)
        hot1 = view(M + 576, NT, EXPERTS)
        hot2 = view(M + 640, NT, EXPERTS)
        chosen = view(M + 704, NT, EXPERTS)
        RW = EXPERTS + 4
        weight = view(M + 768, NT, RW)
        rank = view(M + 768 + NT * RW, NT, RW)
        most = view(M + 768 + 2 * NT * RW, 8)
        disp = view(M + 1024, NT, 2 * SLOTS)
        comb = [view(M + 1280 + 256 * b, NT, 2 * SLOTS) for b in range(2)]
        xe = [view(M + 1792 + 1024 * b, KC, 2 * SLOTS) for b in range(2)]
        silu_g = [view(M + 3840 + 256 * b, FF // 2) for b in range(2)]
        act_e = [view(M + 4352 + 256 * b, FF // 2) for b in range(2)]
        turned = [view(M + 4864 + 512 * b, 4, P) for b in range(2)]
        y_e = [view(M + 5888 + 512 * b, HALF) for b in range(2)]
        PAIRS = EXPERTS // 2
        SENT = PAIRS + 1
        PLACED = PAIRS + 2

        def overflow(eng, one_pass):
            eng.wait_ge(named("passes_known"), 1)
            n = eng.value_load(passes[0:1, 0:1], min_val=1, max_val=T // SLOTS)
            with eng.If(n > 1):
                with eng.Fori(1, n) as p:
                    one_pass(p)
        idx_relu = [view(EV + MAPW * i, MAPW) for i in range(2)]
        idx_score = view(EV + 2 * MAPW, MAPW)
        idx_mask = view(EV + 3 * MAPW, MAPW)
        idx_top = view(EV + 4 * MAPW, 8)
        kv_ssq = view(EV + 1552, NT)
        kv_std = view(EV + 1554, NT)
        lam_prod = view(EV + 1556, 2, HEAD)
        lam_sum = view(EV + 1684, 2)
        lam_exp = view(EV + 1686, 2)
        neg_lam = view(EV + 1688, 1)
        subln_col = view(EV + 1689, 1)
        SM = EV + 1696
        sm_s = [view(SM + MAPW * i, MAPW) for i in range(2)]
        sm_p = [view(SM + MAPW * (2 + i), MAPW) for i in range(2)]
        sm_pT = [view(SM + MAPW * (4 + i), MAPW) for i in range(2)]
        sm_max = [view(SM + MAPW * 6 + 2 * i, 2) for i in range(2)]
        sm_sum = [view(SM + MAPW * 6 + 4 + 2 * i, 2) for i in range(2)]
        sm_inv = [view(SM + MAPW * 6 + 8 + 2 * i, 2) for i in range(2)]
        diff_sq = view(SM + MAPW * 6 + 16, DIFF_HEADS, T)
        diff_std = view(SM + MAPW * 6 + 16 + DIFF_HEADS * T, DIFF_HEADS, T)
        ada_acc["even"] = [view(SM + MAPW * 6 + 16, THIRD), view(SM + MAPW * 6 + 16 + THIRD, THIRD)]
        ada_ring["even"] = [view(SM + MAPW * 6 + 16 + THIRD * (2 + i), THIRD) for i in range(3)]
        LAM_INIT = 0.8 - 0.6 * math.exp(0.0)

        C_HEADS = MAPS
        f_logit = view(AT + T, T)
        f_abs = view(AT + 2 * T, T)
        f_log = view(AT + 3 * T, T)
        neg_ident = view(AT + 4 * T, C_HEADS)
        forget_col = view(AT + 4 * T + C_HEADS, 1)

        SOFTMAX = {"even": [], "odd": []}
        for m in range(MAPS):
            if m < DSA_HEADS:
                SOFTMAX["even"].append(dict(m=m, kind="head", n=m, turn=m, av=MAPS + m))
            else:
                hb = (m - DSA_HEADS) // 2
                SOFTMAX["even"].append(dict(m=m, kind="second" if m % 2 else "first", n=m, turn=DSA_HEADS + hb, hb=hb))
            SOFTMAX["odd"].append(dict(m=m, kind="head", n=MAPS + m, turn=DSA_HEADS + DIFF_HEADS + m, av=MAPS + DSA_HEADS + m))

        def both_tiles(t, nt):
            return t[:, 0:P] if nt == 0 else t[:, P:MAPW]

        def wait_read(eng, d):
            if d["kind"] == "head":
                eng.wait_ge(av_done, d["av"] + 1)
            else:
                eng.wait_ge(named("diff_av"), d["hb"] + 1)
        C_WORDS = NKEYS * T
        coef_all = view(0, T, NKEYS)
        UV = C_WORDS
        u_rows = [view(UV + D * s, D) for s in range(RING)]
        VI = 4
        v_rows = [view(UV + VI * D * s, VI, D) for s in range(2)]
        h_parts = view(UV + RING * D, 8, D, dt=BF16)
        AB = UV + RING * D + 4 * D
        hot_i = [view(AB + 4 * P * s, 4, P) for s in range(2)]
        hot_j = [view(AB + 4 * P * (2 + s), 4, P) for s in range(2)]
        coef_ring = [view(AB + VI * T * s, VI, T) for s in range(2)]
        keys_raw = view(AB, 2, P)
        keysT = view(AB + 2 * P, 2, P)
        part_hi = view(UV, NT, D, dt=BF16)
        part_mid = view(UV + D, NT, D, dt=BF16)
        part_lo = view(UV + 2 * D, NT, D, dt=BF16)
        part_rest = view(UV + 3 * D, NT, D)
        K = 20480
        HP = 2 * PEER_HEADS
        GQ = HP // 4
        GH = GQ // 2
        key_top = view(K, NT * HP, PEER_K)
        key_at = view(K + 512, NT * HP, PEER_K, dt=U32)
        key_num = view(K + 1024, NT * HP, PEER_K)
        key_left = view(K + 1536, NT * GQ, NKEYS)
        cand = view(K + 2560, NT * GH, PEER_K * PEER_K)
        cand_left = view(K + 3584, NT * GH, PEER_K * PEER_K)
        best = view(K + 6144, NT * PEER_HEADS, PEER_K)
        best_at = view(K + 6400, NT * PEER_HEADS, PEER_K, dt=U32)
        GK = GH * PEER_K
        best_hi = view(K + 6656, NT, GK, dt=U32)
        best_lo = view(K + 6784, NT, GK, dt=U32)
        best_row = view(K + 6912, NT, GK)
        best_col = view(K + 7040, NT, GK)
        match = [view(K + 7168 + GK * PEER_K * i, GK, PEER_K) for i in range(4)]
        pick_i = view(K + 9216, NT, P)
        pick_j = view(K + 9472, NT, P)
        gate = view(K + 9728, NT * PEER_HEADS, PEER_K)
        gate_sum = view(K + 9984, NT * PEER_HEADS)
        peer_num = small
        dots = small[:, 0:BODY]
        gelu = small[:, BODY:2 * BODY]
        coef = small[:, 2 * BODY:3 * BODY]
        idx_ring = [small[:, 3 * BODY + 8 * s:3 * BODY + 8 * s + 8].bitcast(U32) for s in range(2)]
        BODIES = T // BODY
        SUB = BODY // 4
        CHUNKS = NKEYS // VI

        def layer_of(stage):
            return int(stage[-1])
        block = ctx.enter_context(nc.Block())
        ADA = [(I["ada_w"][0], 0), (I["ada_w_2"][0], KC), (I["ada_w_2"][1], KC)]
        BIAS_AT = [(0, 64), (1, 0), (1, 48)]

        st_abs = [view(AT + MAPW * i, MAPW) for i in range(2)]
        st_exp = [view(AT + MAPW * (2 + i), MAPW) for i in range(2)]
        st_ln = [view(AT + MAPW * (4 + i), MAPW) for i in range(2)]
        st_keep = [view(AT + MAPW * (6 + i), MAPW) for i in range(2)]
        st_a = [view(AT + MAPW * (8 + i), MAPW) for i in range(2)]

        RB = AREA - REL_HEADS * MAPW - 4 * HEAD - 3
        rel_maps = view(RB, REL_HEADS, MAPW)
        lam_vec = view(RB + REL_HEADS * MAPW, 4, HEAD)
        kv_gain = view(RB + REL_HEADS * MAPW + 4 * HEAD, LATENT // P)
        subln_raw = view(RB + REL_HEADS * MAPW + 4 * HEAD + 2, 1)
        rel_heads, rel_near, rel_far = small[:, 0:REL_BUCKETS], peer_i, peer_neg_j

        def map_q(m):
            lo = HEAD * (m % 2)
            return qkT[lo:lo + HEAD, m // 2, :], qkT[lo:lo + HEAD, MAPS // 2 + m // 2, :]

        def diag_blocks(t):
            return t.rearrange("p (b c) -> p b c", c=P)[:, 0:3:2, :]

        ROW_TURN = {"mix1": 1, "moe": 2, "even": 3, "peer0": 4, "odd": 5, "peer1": 6}

        @block.sync
        def _(sp):
            def load_row(stage, vector):
                sp.wait_ge(x_done, x_updates(stage))
                sp.dma_start(row[:, :], vector.rearrange("(a n) -> a n", a=1).broadcast_to([P, D])).then_inc(row_loaded, 16)

            def load_piece(n):
                stage, i = ada_stage(n)
                ring = ada_ring[stage]
                if i >= len(ring):
                    sp.wait_ge(ada_used, n - len(ring) + 1)
                third = n // KC
                k = n % KC
                w = ADA[third // 3][0]
                sp.dma_start(ring[i % len(ring)], w[k * P:(k + 1) * P, third % 3 * THIRD:(third % 3 + 1) * THIRD]
                             ).then_inc(ada_loaded[i % len(ring)], 16)

            def load_mixer(stage, first, pieces):
                n = first
                for i, (j, g) in enumerate(groups_of(stage)):
                    load_group(j, g, i == 0)
                    for _ in range(pieces[i]):
                        load_piece(n)
                        n += 1

            def load_group(n, g, first):
                if first and n:
                    sp.wait_ge(x_done, x_updates(g["stage"]))
                if n >= 3:
                    sp.wait_ge(proj_done, n - 2)
                cols = g["w"].shape[1]
                nk = g["w"].shape[0] // P
                w = g["w"].rearrange("(k p) n -> p k n", p=P)
                slot = wring[n % 3]
                if g["kind"] == "I":
                    sp.dma_start(slot[:, 0:nk, 0:64], w[:, :, 0:64]).then_inc(w_loaded[n % 3], 16)
                    sp.dma_start(slot[:, 0:nk, 64:64 + cols], w).then_inc(w_loaded[n % 3], 16)
                else:
                    sp.dma_start(slot[:, 0:nk, 0:cols], w).then_inc(w_loaded[n % 3], 16)

            def load_stage(stage):
                for i, (n, g) in enumerate(groups_of(stage)):
                    load_group(n, g, i == 0)

            VECS = [(I["c"][0], 0, 0), (I["c_2"][0], 0, KC)] + [(gain, 0, KC * (2 + i)) for i, gain in enumerate(GAINS)]
            VECS += [(I["ada_b"][0], *BIAS_AT[0]), (I["ada_b_2"][0], *BIAS_AT[1]), (I["ada_b_2"][1], *BIAS_AT[2])]
            for vector, half, at in VECS:
                rows = vector.shape[0] // P
                sp.dma_start(vec_raw[at:at + rows, half, :], vector.rearrange("(k p) -> k p", p=P)).then_inc(vec_loaded, 16)
            sp.dma_start(rel_heads[0:REL_HEADS, :], I["rel_bias_2"].rearrange("b h -> h b"),
                          allow_slow_non_contiguous=True).then_inc(named("rel_heads_loaded"), 16)
            for n in range(KC):
                load_piece(n)
            sp.dma_start(x[:, :, :], I["x"][0].rearrange("(t p) d -> p t d", p=P)).then_inc(x_loaded, 16)
            load_mixer("mix1", KC, [3, 2, 3, 3, 3, 3, 3, 20])
            sp.wait_ge(named("rel_made"), 1)
            for part, cols in ((rel_near, slice(0, T)), (rel_far, slice(T, MAPW))):
                width = cols.stop - cols.start
                sp.dma_start(rel_rows_d[:, :, cols], part[0:REL_HEADS, 0:width].unsqueeze(1).broadcast_to([REL_HEADS, P, width])
                             ).then_inc(named("rel_stored"), 16)
            def load_expert(e, b, part):
                for i, w in ((0, I["moe_w_gate"]), (1, I["moe_w_up"]), (2, I["moe_w_down"])):
                    if part == i // 2:
                        src = w[0, bass.ds(e, 1)].rearrange("e (k p) f -> p (e k) f", p=P)
                        sp.dma_start(moe_w[b][i], src).then_inc(named(("gu_loaded", "down_loaded")[part] + str(b)), 16)

            def load_pass(p):
                with sp.Fori(1, PAIRS) as i:
                    for b in range(2):
                        sp.wait_ge(named("gu_done"), p * EXPERTS + 2 * i + (b - 1))
                        load_expert(2 * i + b, b, 0)
                        sp.wait_ge(named("y_done"), p * EXPERTS + 2 * i + (b - 1))
                        load_expert(2 * i + b, b, 1)

            def load_overflow(p):
                sp.wait_ge(named("comb_done"), p * (EXPERTS + 1))
                for b in range(2):
                    for part in range(2):
                        load_expert(b, b, part)
                load_pass(p)

            sp.wait_ge(av_out, MAPS)
            sp.wait_ge(ada_sums, EARLY // KC)
            load_expert(0, 0, 0)
            load_expert(0, 0, 1)
            load_expert(1, 1, 0)
            sp.wait_ge(x_done, x_updates("moe"))
            with nc.allow_non_contiguous_dma(reason="a router's few columns"):
                sp.dma_start(route_w[:, :, 0:GROUPS], I["moe_w_grp"][0].rearrange("(k p) n -> p k n", p=P)
                             ).then_inc(named("route_loaded"), 16)
                sp.dma_start(route_w[:, :, GROUPS:], I["moe_w_exp"][0].rearrange("(k p) n -> p k n", p=P)
                             ).then_inc(named("route_loaded"), 16)
            sp.dma_start(route_b[0:1, 0:GROUPS], I["moe_b_grp"][0:1, :]).then_inc(named("route_loaded"), 16)
            sp.dma_start(route_b[0:1, GROUPS:], I["moe_b_exp"][0:1, :]).then_inc(named("route_loaded"), 16)
            load_expert(1, 1, 1)
            load_pass(0)
            overflow(sp, load_overflow)
            load_row("fin1", I["final_g"])
            sp.wait_ge(x_done, x_updates("even"))
            sp.dma_start(lam_vec.rearrange("p a d -> p (a d)"), I["b_lambda_2"].rearrange("e a d -> e (a d)").broadcast_to([P, 4 * HEAD])
                         ).then_inc(named("even_vec_loaded"), 16)
            sp.dma_start(kv_gain, I["a_kv_norm_2"][0].rearrange("(k p) -> p k", p=P),
                         allow_slow_non_contiguous=True).then_inc(named("even_vec_loaded"), 16)
            sp.dma_start(subln_raw, I["b_subln_2"][0].rearrange("(p a) -> p a", a=1)).then_inc(named("even_vec_loaded"), 16)
            sp.wait_ge(named("rel_stored"), 32)
            rows = rel_rows_d.tensor
            sp.dma_start(rel_maps[:, :, P:MAPW], bass.AP(rows, P - 1, [[MAPW - 1, P], [P * MAPW, REL_HEADS], [1, T]])
                         ).then_inc(named("rel_loaded"), 16)
            sp.dma_start(rel_maps[:, :, 0:P], bass.AP(rows, 2 * P - 1, [[MAPW - 1, P], [P * MAPW, REL_HEADS], [1, P]])
                         ).then_inc(named("rel_loaded"), 16)
            load_mixer("even", EARLY, [0, 0, 3, 2, 3, 3, 3, 2, 1, 1, 6])
            def peer(stage):
                L = layer_of(stage)
                sp.wait_ge(x_done, x_updates(stage))
                sp.dma_start(keys_raw[:, :, :], I["peer_sub_keys_2"][L].rearrange("a n d -> n a d")).then_inc(named("keys_loaded"), 16)
                load_stage(stage)
                sp.wait_ge(named("parts_made"), L + 1)
                for q in range(8):
                    lo = 32 * (q % 4)
                    for n, part in enumerate((part_hi, part_mid, part_lo)):
                        sp.dma_start(h_parts[32 * n:32 * n + 32, q, :], part[lo:lo + 32, q // 4, :]).then_inc(named("h_parts_loaded"), 16)
                sp.wait_ge(named("dots_done"), RING + T * (L + 1))
                v = I["peer_v_2"][L].rearrange("(i j) d -> j i d", j=NKEYS)

                def load_v(c, s):
                    sp.dma_start(v_rows[s], v[:, bass.ds(c * VI, VI), :]).then_inc(named(f"v_loaded{s}"), 16)

                for s in range(2):
                    load_v(s, s)
                with sp.Fori(1, CHUNKS // 2) as m:
                    for s in range(2):
                        sp.wait_ge(named("v_used"), 2 * m + (L * CHUNKS + s - 1))
                        load_v(2 * m + s, s)

            peer("peer0")
            sp.wait_ge(x_done, x_updates("odd"))
            sp.dma_start(forget_col[0:C_HEADS, :], I["odd_b_forget_2"][0].rearrange("(h a) -> h a", a=1)).then_inc(named("forget_loaded"), 16)
            load_stage("odd")
            peer("peer1")
            load_row("all", I["norm_final_2"])
            sp.wait_ge(named("rel_stored"), 32)
            sp.wait_ge(x_done, x_updates("all") + 1)
            sp.dma_start(out[0].rearrange("(t p) d -> p t d", p=P), x[:, :, :]).then_inc(stored, 16)
            sp.wait_ge(stored, 16)

        @block.gpsimd
        def _(pool):
            step = stepper(pool, pool_step)
            step(pool.memset(ident[:, :], 0.0))
            step(pool.affine_select(out=ident[:, :], in_=ident[:, :], compare_op=ALU.not_equal, fill=1.0,
                                    base=0, pattern=[[-1, P]], channel_multiplier=1))
            pool.sem_inc(ident_made, 1)
            step(pool.memset(ones[:, :], 1.0))
            step(pool.memset(neg_ones[:, :], -1.0))
            step(pool.memset(zeros[:, :], 0.0))
            step(pool.memset(causal_add[:, :], 0.0))
            step(pool.iota(iota[:, :], [[1, P]], base=0, channel_multiplier=0, allow_small_or_imprecise_dtypes=True))
            step(pool.affine_select(out=before[:, :], in_=ones[:, :], compare_op=ALU.is_gt, fill=0.0,
                                    base=0, pattern=[[1, P]], channel_multiplier=-1))
            step(pool.affine_select(out=neg_tri[:, :], in_=neg_ones[:, :], compare_op=ALU.is_ge, fill=0.0,
                                    base=0, pattern=[[-1, P]], channel_multiplier=1))
            step(pool.affine_select(out=diag_blocks(causal_add[:, :]), in_=diag_blocks(causal_add[:, :]),
                                    compare_op=ALU.is_ge, fill=NEG, base=0, pattern=[[0, 2], [-1, P]],
                                    channel_multiplier=1))
            step(pool.memset(token_sel[:, :], 0.0))
            for quadrant in range(3):
                part = token_sel[:, :]
                step(pool.affine_select(out=part, in_=part, compare_op=ALU.not_equal, fill=1.0,
                                        base=-BODY * quadrant, pattern=[[-1, BODY]], channel_multiplier=1))
            pool.sem_inc(consts_made, 1)

            pool.wait_ge(named("rel_heads_loaded"), 16)
            step(pool.memset(rel_far[0:REL_HEADS, :], NEG))
            for b, first, last in rel_bucket_ranges():
                step(pool.tensor_copy(rel_near[0:REL_HEADS, T - 1 - last:T - first],
                                      rel_heads[0:REL_HEADS, b:b + 1].broadcast_to([REL_HEADS, last - first + 1])))
            pool.sem_inc(named("rel_made"), 1)

            for h in range(MAPS):
                pool.wait_ge(named("stick_exp"), h + 1)
                a = diag_blocks(st_a[h % 2])
                pool.affine_select(out=a, in_=a, compare_op=ALU.is_gt, fill=0.0, base=0,
                                   pattern=[[0, 2], [1, P]], channel_multiplier=-1).then_inc(named("stick_mask"), 1)
            pool.wait_ge(named("idx_summed"), IDX_HEADS)
            pool.affine_select(out=diag_blocks(idx_score), in_=diag_blocks(idx_score), compare_op=ALU.is_ge, fill=LOWEST,
                               base=0, pattern=[[0, 2], [-1, P]], channel_multiplier=1).then_inc(named("idx_causal"), 1)
            def peer(stage):
                L = layer_of(stage)
                u = I["peer_u_2"].rearrange("l e d -> (l e) d")
                pool.wait_ge(x_done, x_updates(stage))
                step(pool.memset(h_parts[96:128, :, :], 0.0))
                pool.sem_inc(named("h_parts_cleared"), 1)
                pool.wait_ge(named("experts_made"), L + 1)
                pool.wait_ge(named("h_parts_loaded"), 24 * 16 * (L + 1))
                with pool.Fori(0, BODIES) as g:
                    for b in range(BODY // RING):
                        at = g * BODY + b * RING
                        pool.tensor_copy(idx_ring[b % 2], peer_e[:, bass.ds(at, RING)]).then_inc(named("idx_copied"), 1)
                        pool.wait_ge(named("idx_copied"), g * (BODY // RING) + (L * T // RING + b + 1))
                        for s in range(RING):
                            pool.wait_ge(named("dots_done"), at + (L * T + s + 1))
                            pool.sem_inc(named("gathers_begun"), 1)
                            pool.indirect_dma_start(u_rows[s], None, u, bass.IndirectOffsetOnAxis(ap=idx_ring[b % 2][:, s:s + 1], axis=0)
                                                    ).then_inc(named(f"u_loaded{s}"), 16)

            peer("peer0")
            peer("peer1")

        @block.scalar
        def _(act):
            step = stepper(act, act_step)

            def norm(stage):
                n = x_updates(stage)
                if n:
                    act.wait_ge(x_done, n)
                else:
                    act.wait_ge(x_loaded, 16)
                for t in range(NT):
                    act.activation(xn[:, t, :], x[:, t, :], ACT.Square, accum_out=ssq[:, t:t + 1]).then_inc(ssq_done, 1)
                act.wait_ge(var_done, n + 1)
                act.activation(std[:, :], var[:, :], ACT.Sqrt).then_inc(std_done, 1)

            def take(n, g):
                if g["by"] != "act":
                    return
                act.wait_ge(proj_done, n + 1)
                b = 2 * (n % 2)
                cols = g["w"].shape[1]
                if g["kind"] == "F":
                    src = ps[:, b:b + 2, :].rearrange("p b (f t) -> p (b f) t", t=T)
                    act.activation(g["dst"], src, ACT.Copy, scale=g["scale"]).then_inc(proj_out, 1)
                elif g["kind"] == "T":
                    act.activation(g["dst"], ps[:, b:b + 2, 0:cols], ACT.Copy, scale=g["scale"]).then_inc(proj_out, 1)
                else:
                    step(act.activation(kidx[:, :], ps[:, b, 0:T], ACT.Copy))
                    act.activation(widx[:, :, :], ps[:, b + 1, 0:16].rearrange("p (t h) -> p t h", t=NT), ACT.Copy,
                                   scale=IDX_HEADS ** -0.5).then_inc(proj_out, 1)

            def take_av(h, n):
                act.wait_ge(av_done, n + 1)
                lo = HEAD * (h % 2)
                act.activation(oT[lo:lo + HEAD, h // 2, :], ps[lo:lo + HEAD, 6, 0:T],
                               ACT.Copy).then_inc(av_out, 1)

            def take_row(stage, bank):
                act.wait_ge(named("row_made"), ROW_TURN[stage])
                act.activation(row[:, :], ps[:, bank:bank + 2, :].rearrange("p b n -> p (b n)"), ACT.Copy).then_inc(row_loaded, 16)

            act.wait_ge(named("vec_turned"), 1)
            act.activation(c_silu[:, :], ps[:, 5, 0:2 * KC], ACT.Silu).then_inc(c_ready, 1)
            act.activation(vec_cols[:, 0, :], ps[:, 5, 0:112], ACT.Copy)
            act.activation(vec_cols[:, 1, 0:96], ps[:, 5, P:P + 96], ACT.Copy).then_inc(named("vec_ready"), 1)

            norm("mix1")
            for n, g in groups_of("mix1"):
                take(n, g)

            def stick_keep(h):
                act.wait_ge(score_done, h + 1)
                step(act.activation(st_abs[h % 2], ps[:, 4 + h % 2, 0:MAPW], ACT.Abs))
                step(act.activation(st_exp[h % 2], st_abs[h % 2], ACT.Exp, scale=-1.0))
                if h >= 2:
                    act.wait_ge(named("stick_kept"), h - 1)
                act.activation(st_ln[h % 2], st_exp[h % 2], ACT.Ln, bias=1.0).then_inc(named("stick_ln"), 1)

            def stick_weight(h):
                act.wait_ge(named("stick_sum"), h + 1)
                if h >= 2:
                    act.wait_ge(av_done, h - 1)
                act.activation(st_a[h % 2], ps[:, 4 + h % 2, 0:MAPW], ACT.Exp).then_inc(named("stick_exp"), 1)

            for i in range(MAPS + 2):
                if i < MAPS:
                    stick_keep(i)
                if 1 <= i <= MAPS:
                    stick_weight(i - 1)
                if i >= 2:
                    take_av(i - 2, i - 2)
            take_row("mix1", 4)
            def moe_pass(p):
                def take_xe(j, buf):
                    act.wait_ge(named("xe_psum"), p * SENT + j + 1)
                    act.activation(xe[buf].rearrange("p k s -> p (k s)"), ps[:, 4:6, :].rearrange("p b n -> p (b n)"),
                                   ACT.Copy).then_inc(named("xe_ready"), 1)

                take_xe(0, 0)
                with act.Fori(0, PAIRS // 2) as i:
                    for h in range(2):
                        for b in range(2):
                            act.wait_ge(named("gu_done"), p * EXPERTS + 4 * i + (2 * h + b + 1))
                            act.activation(silu_g[b], ps[:, 6 + b, 0:FF // 2], ACT.Silu).then_inc(named("silu_done"), 1)
                            if b == 0:
                                take_xe(2 * i + (h + 1), 1 - h)
                        for b in range(2):
                            act.wait_ge(named("y_done"), p * EXPERTS + 4 * i + (2 * h + b + 1))
                            act.activation(y_e[b], ps[:, 6 + b, :], ACT.Copy).then_inc(named("y_ready"), 1)

            norm("moe")
            take_row("moe", 6)
            for b in range(4):
                act.wait_ge(named("ht_psum"), b + 1)
                act.activation(h_tok[:, b // 2, (b % 2) * HALF:(b % 2 + 1) * HALF], ps[:, b, :],
                               ACT.Copy).then_inc(named("h_tok_ready"), 1)
            act.sem_inc(named("y_ready"), 2)
            act.wait_ge(named("grp_neg_made"), 1)
            for t in range(NT):
                act.activation(grp_exp[:, t, :], grp_logit[:, t, 0:GROUPS], ACT.Exp, bias=grp_neg[:, t:t + 1],
                               accum_out=grp_sum[:, t:t + 1]).then_inc(named("grp_exp_done"), 1)
            act.wait_ge(named("in_neg_made"), 1)
            for t in range(NT):
                act.activation(in_exp[:, t:t + 1], in_top[:, t, 1:2], ACT.Exp,
                               bias=in_neg[:, t:t + 1]).then_inc(named("in_exp_done"), 1)
            moe_pass(0)
            overflow(act, moe_pass)
            norm("fin1")
            def softmax_attention(stage):
                maps = SOFTMAX[stage]

                def exps(i):
                    d = maps[i]
                    act.wait_ge(named("max_made"), d["n"] + 1)
                    if i >= 2:
                        if maps[i - 2]["kind"] == "first":
                            act.wait_ge(named("probs_ready"), maps[i - 2]["turn"] + 1)
                        else:
                            act.wait_ge(named("probs_turned"), maps[i - 2]["turn"] + 1)
                    b = i % 2
                    for t in range(NT):
                        act.activation(both_tiles(sm_p[b], t), both_tiles(sm_s[b], t), ACT.Exp, bias=sm_max[b][:, t:t + 1],
                                       accum_out=sm_sum[b][:, t:t + 1]).then_inc(named("exp_done"), 1)

                def take_turned(d, before_last):
                    act.wait_ge(named("probs_turned"), d["turn"] + 1)
                    if before_last:
                        wait_read(act, before_last)
                    act.activation(sm_pT[d["turn"] % 2], ps[:, d["turn"] % 2, 0:MAPW], ACT.Copy).then_inc(named("turned_out"), 1)

                turned = [d for d in maps if d["kind"] != "first"]
                for i in range(MAPS + 2):
                    if i < MAPS:
                        exps(i)
                    if 1 <= i <= MAPS and maps[i - 1]["kind"] != "first":
                        j = turned.index(maps[i - 1])
                        take_turned(maps[i - 1], turned[j - 2] if j >= 2 else None)
                    if i >= 2 and maps[i - 2]["kind"] == "head":
                        take_av(maps[i - 2]["m"], maps[i - 2]["av"])

            norm("even")
            take_row("even", 4)
            even = groups_of("even")
            take(*even[0])
            act.wait_ge(proj_out, even[0][0] + 1)
            for t in range(NT):
                act.activation(idx_relu[t][:, 0:LATENT], ckv_tok[:, t, :], ACT.Square,
                               accum_out=kv_ssq[:, t:t + 1]).then_inc(named("kv_ssq_done"), 1)
            act.wait_ge(named("kv_var_done"), 1)
            act.activation(kv_std, kv_std, ACT.Sqrt).then_inc(named("kv_std_done"), 1)
            take(*even[1])
            take(*even[2])
            act.wait_ge(named("lam_sum_made"), 1)
            act.activation(lam_exp, lam_sum, ACT.Exp).then_inc(named("lam_exp_done"), 1)

            def idx_relus(h):
                act.wait_ge(score_done, MAPS + h + 1)
                if h >= 2:
                    act.wait_ge(named("idx_summed"), h - 1)
                act.activation(idx_relu[h % 2], ps[:, 4 + h % 2, 0:MAPW], ACT.Relu, scale=HEAD ** -0.5).then_inc(named("idx_relu_done"), 1)

            act.wait_ge(named("kv_scaled"), 1)
            for i in range(4):
                idx_relus(2 * i)
                idx_relus(2 * i + 1)
                take(*even[3 + i])
            for n, g in even[7:9]:
                take(n, g)
            softmax_attention("even")
            act.wait_ge(named("diff_av"), DIFF_HEADS)
            act.wait_ge(ada_sums, 9)
            act.activation(diff_sq.rearrange("p h t -> p (h t)"), ps[:, 2:4, :].rearrange("p b n -> p (b n)"),
                           ACT.Square).then_inc(named("diff_sq_done"), 1)
            act.wait_ge(named("diff_var_done"), 1)
            act.activation(diff_std[:, :, :], diff_std[:, :, :], ACT.Sqrt).then_inc(named("diff_std_done"), 1)
            def peer(stage):
                L = layer_of(stage)
                norm(stage)
                take_row(stage, 6)
                for b in range(4):
                    act.wait_ge(named("ht_psum"), 4 * (L + 1) + b + 1)
                    act.activation(h_tok[:, b // 2, (b % 2) * HALF:(b % 2 + 1) * HALF], ps[:, b, :],
                                   ACT.Copy).then_inc(named("h_tok_ready"), 1)
                act.wait_ge(named("keys_psum"), L + 1)
                act.activation(keysT.rearrange("p a n -> p (a n)"), ps[:, 4, 0:2 * P], ACT.Copy).then_inc(named("keysT_ready"), 1)
                for n, g in groups_of(stage):
                    take(n, g)
                act.wait_ge(named("gate_diff"), L + 1)
                act.activation(gate[:, :, :], gate[:, :, :], ACT.Exp).then_inc(named("gate_exp"), 1)

                def take_coef(g, m):
                    act.wait_ge(named("spread_done"), g * SUB + (2 + L * T // 4 + m + 1))
                    act.sem_inc(named("coef_begun"), 1)
                    act.activation(coef_all[:, bass.ds(g * BODY + 4 * m, 4), :], ps[:, 4 + m % 2, :].rearrange("p (t i) -> p t i", i=P),
                                   ACT.Copy).then_inc(named("coef_out"), 1)

                def second_hots(g, m):
                    n = g * SUB + (L * T // 4 + m + 1)
                    act.wait_ge(named("spread_done"), n)
                    act.sem_inc(named("hots_j_begun"), 1)
                    for j in range(4):
                        last = act.activation(hot_j[m % 2][:, j, :], iota[:, :], ACT.Abs,
                                              bias=peer_neg_j[:, bass.ds(g * BODY + 4 * m + j, 1)])
                    last.then_inc(named("hots_j_apart"), 1)
                    act.wait_ge(named("hots_j_apart"), n)
                    act.activation(hot_j[m % 2], hot_j[m % 2], ACT.Relu, scale=-1.0, bias=1.0).then_inc(named("hots_j_made"), 1)

                with act.Fori(0, BODIES) as g:
                    for b in range(BODY // RING):
                        if b >= 2:
                            take_coef(g, 2 * (b - 2) + 1)
                        if b >= 1:
                            take_coef(g, 2 * (b - 1))
                        act.wait_ge(named("dots_done"), g * BODY + (RING + L * T + (b + 1) * RING))
                        cols = slice(b * RING, (b + 1) * RING)
                        act.activation(gelu[:, cols], dots[:, cols], ACT.Gelu_apprx_tanh).then_inc(named("gelu_done"), 1)
                        for m in range(2 * b, 2 * b + 2):
                            second_hots(g, m)
                    for m in range(SUB - 3, SUB):
                        take_coef(g, m)

                by_key = coef_all.rearrange("p t i -> p i t")
                act.wait_ge(named("coef_out"), 2 + T // 4 * (L + 1))

                def take_keys(c, s):
                    act.activation(coef_ring[s], by_key[:, bass.ds(c * VI, VI), :], ACT.Copy).then_inc(named("keys_out"), 1)

                act.wait_ge(named("spread_done"), 2 + T // 4 * (L + 1))
                for s in range(2):
                    take_keys(s, s)
                with act.Fori(1, CHUNKS // 2) as m:
                    for s in range(2):
                        act.wait_ge(named("v_used"), 2 * m + (L * CHUNKS + s - 1))
                        act.sem_inc(named("keys_begun"), 1)
                        take_keys(2 * m + s, s)

            act.sem_inc(named("coef_out"), 2)
            peer("peer0")
            norm("odd")
            take_row("odd", 4)
            act.wait_ge(named("f_made"), 1)
            step(act.activation(f_abs[0:C_HEADS, :], f_logit[0:C_HEADS, :], ACT.Abs))
            step(act.activation(f_log[0:C_HEADS, :], f_abs[0:C_HEADS, :], ACT.Exp, scale=-1.0))
            act.activation(f_log[0:C_HEADS, :], f_log[0:C_HEADS, :], ACT.Ln, bias=1.0).then_inc(named("f_log_done"), 1)
            for n, g in groups_of("odd"):
                take(n, g)
            softmax_attention("odd")
            peer("peer1")
            norm("all")

        @block.tensor
        def _(pe):
            def project(n, g):
                pe.wait_ge(w_loaded[n % 3], w_turns(n))
                if n >= 2:
                    pe.wait_ge(proj_out, n - 1)
                w = wring[n % 3]
                nk = g["w"].shape[0] // P
                cols = g["w"].shape[1]
                b = 2 * (n % 2)
                src = g["src"]
                if g["kind"] == "F":
                    for f in range(cols // P):
                        for k in range(nk):
                            last = pe.matmul(ps[:, b + f // 2, (f % 2) * T:(f % 2 + 1) * T], w[:, k, f * P:(f + 1) * P],
                                             src[:, k, :], start=(k == 0), stop=(k == nk - 1))
                elif g["kind"] == "T":
                    for t in range(NT):
                        for k in range(nk):
                            last = pe.matmul(ps[:, b + t, 0:cols], src[:, k, t * P:(t + 1) * P], w[:, k, 0:cols],
                                             start=(k == 0), stop=(k == nk - 1))
                elif g["kind"] == "I":
                    for k in range(nk):
                        pe.matmul(ps[:, b, 0:T], w[:, k, 0:P], src[:, k, :], start=(k == 0), stop=(k == nk - 1))
                    for t in range(NT):
                        for k in range(nk):
                            last = pe.matmul(ps[:, b + 1, t * 8:(t + 1) * 8], src[:, k, t * P:(t + 1) * P], w[:, k, P:P + 8],
                                             start=(k == 0), stop=(k == nk - 1))
                else:
                    for k in range(nk):
                        last = pe.matmul(ps[0:cols, b, 0:T], w[:, k, 0:cols], src[:, k, :],
                                         start=(k == 0), stop=(k == nk - 1))
                last.then_inc(proj_done, 1)

            def transpose_norm(stage):
                n = NORM[stage][0]
                for b in range(4):
                    t, half = b // 2, b % 2
                    pe.wait_ge(xn_done, NT * n + t + 1)
                    for k in range(4):
                        last = pe.transpose(ps[:, b, k * P:(k + 1) * P], xn[:, t, (4 * half + k) * P:(4 * half + k + 1) * P],
                                            ident[:, :])
                    last.then_inc(xt_done, 1)
                pe.wait_ge(hT_done, 4 * (n + 1))

            def values(h, n, pT):
                if n >= 2:
                    pe.wait_ge(av_out, n - 1)
                lo = HEAD * (h % 2)
                o = ps[lo:lo + HEAD, 6, 0:T]
                pe.matmul(o, v_tok[:, 0, h * HEAD:(h + 1) * HEAD], pT[:, 0:T], start=True, stop=False, skip_group_check=True)
                pe.matmul(ps[lo:lo + HEAD, 6, P:T], v_tok[:, 1, h * HEAD:(h + 1) * HEAD], pT[:, T:MAPW],
                          start=False, stop=True, skip_group_check=True).then_inc(av_done, 1)

            def sum_third(n):
                stage, i = ada_stage(n * KC)
                pe.wait_ge(ada_used, KC * (n + 1))
                if n:
                    pe.wait_ge(mod_made, n)
                for j in range(THIRD // P):
                    last = pe.matmul(ps[:, 7, j:j + 1], ada_acc[stage][n % 2][:, j * P:(j + 1) * P],
                                     ones[:, 0:1], start=True, stop=True)
                last.then_inc(ada_sums, 1)

            def make_row(stage, bank):
                _, a, v = NORM[stage]
                v += 2
                pe.wait_ge(mod_made, 3 * a + v // 2 + 1)
                for k in range(KC):
                    last = pe.matmul(ps[:, bank + k // 4, k % 4 * P:(k % 4 + 1) * P], mod_cols[:, a, v, k:k + 1].broadcast_to([P, P]),
                                     ident[:, :], start=True, stop=True)
                last.then_inc(named("row_made"), 1)

            pe.wait_ge(ident_made, 1)
            pe.wait_ge(vec_loaded, 16 * 11)
            pe.transpose(ps[:, 5, 0:112], vec_raw[0:112, 0, :], ident[0:112, 0:112])
            pe.transpose(ps[:, 5, P:P + 96], vec_raw[0:96, 1, :], ident[0:96, 0:96]).then_inc(named("vec_turned"), 1)
            pe.wait_ge(consts_made, 1)
            sum_third(0)

            transpose_norm("mix1")
            for i, (n, g) in enumerate(groups_of("mix1")[:-2]):
                project(n, g)
                if i == 3:
                    sum_third(1)
            sum_third(2)
            pe.wait_ge(proj_out, 6)

            def stick_scores(h):
                if h >= 2:
                    pe.wait_ge(named("stick_exp"), h - 1)
                q, k = map_q(h)
                z = ps[:, 4 + h % 2, :]
                pe.matmul(z[:, 0:T], k[:, 0:P], q, start=True, stop=False, skip_group_check=True)
                pe.matmul(z[:, T:MAPW], k[:, P:T], q[:, P:T], start=False, stop=True,
                          skip_group_check=True).then_inc(score_done, 1)

            def stick_sums(h):
                pe.wait_ge(named("stick_kept"), h + 1)
                z = ps[:, 4 + h % 2, :]
                keep = st_keep[h % 2]
                pe.matmul(z[:, 0:T], neg_tri[:, :], keep[:, 0:T], start=False, stop=False, skip_group_check=True)
                pe.matmul(z[:, P:T], neg_ones[:, :], keep[:, T:MAPW], start=False, stop=False, skip_group_check=True)
                pe.matmul(z[:, T:MAPW], neg_tri[:, :], keep[:, T:MAPW], start=False, stop=True,
                          skip_group_check=True).then_inc(named("stick_sum"), 1)

            for i in range(MAPS + 2):
                if i < MAPS:
                    stick_scores(i)
                if 1 <= i <= MAPS:
                    stick_sums(i - 1)
                if i >= 2:
                    pe.wait_ge(named("stick_mask"), i - 1)
                    values(i - 2, i - 2, st_a[i % 2])
                if i in (4, 10):
                    sum_third(3 + i // 6)
            sum_third(5)
            pe.wait_ge(named("stick_exp"), MAPS)
            make_row("mix1", 4)
            pe.wait_ge(av_out, MAPS)
            for n, g in groups_of("mix1")[-2:]:
                project(n, g)
            def moe_pass(p):
                def dispatch(j, first=False):
                    pe.wait_ge(named("disp_made"), p * PLACED + j + 1)
                    if not first:
                        pe.wait_ge(named("operands_out"), p * EXPERTS + 2 * j - 1)
                    for k in range(KC):
                        for t in range(NT):
                            last = pe.matmul(ps[:, 4 + k // 4, k % 4 * P:(k % 4 + 1) * P], h_tok[:, t, k * P:(k + 1) * P],
                                             disp[:, t, :], start=(t == 0), stop=(t == NT - 1))
                    last.then_inc(named("xe_psum"), 1)

                with_pass = p * EXPERTS

                def gate_up(i, h, b):
                    pe.wait_ge(named(f"gu_loaded{b}"), p * (PAIRS * 32) + 64 * i + 32 * (h + 1))
                    pe.wait_ge(named("xe_ready"), p * SENT + 2 * i + (h + 1))
                    pe.wait_ge(named("y_ready"), with_pass + 4 * i + (2 * h + b + 1))
                    for m in range(2):
                        for k in range(KC):
                            for half in range(2):
                                last = pe.matmul(ps[SLOTS * half:SLOTS * (half + 1), 6 + b, m * FF // 2:(m + 1) * FF // 2],
                                                 xe[h][:, k, SLOTS * b:SLOTS * (b + 1)],
                                                 moe_w[b][m][:, k, half * FF // 2:(half + 1) * FF // 2],
                                                 start=(k == 0), stop=(k == KC - 1), skip_group_check=True)
                    last.then_inc(named("gu_done"), 1)

                def turn_places(i, h, b):
                    pe.wait_ge(named("comb_made"), with_pass + 4 * i + (2 * h + b + 1))
                    pe.wait_ge(named("xe_ready"), p * SENT + 2 * i + (h + 2))
                    for t in range(NT):
                        pe.transpose(ps[:, 4 + b, (2 + t) * P:(3 + t) * P], comb[b][:, t, :], ident[:, :])

                def turn_act(i, h, b):
                    pe.wait_ge(named("act_done"), with_pass + 4 * i + (2 * h + b + 1))
                    for c in range(2):
                        last = pe.transpose(ps[:, 4 + b, c * P:(c + 1) * P], act_e[b][:, c * P:(c + 1) * P], ident[:, :])
                    last.then_inc(named("operands_made"), 1)

                def down(i, h, b):
                    pe.wait_ge(named(f"down_loaded{b}"), p * (PAIRS * 16) + 32 * i + 16 * (h + 1))
                    pe.wait_ge(named("operands_out"), with_pass + 4 * i + (2 * h + b + 2))
                    for f in range(FF // P):
                        for half in range(2):
                            last = pe.matmul(ps[SLOTS * half:SLOTS * (half + 1), 6 + b, :],
                                             turned[b][:, f % 2, SLOTS * (f // 2):SLOTS * (f // 2 + 1)],
                                             moe_w[b][2][:, f, half * HALF:(half + 1) * HALF],
                                             start=(f == 0), stop=(f == FF // P - 1), skip_group_check=True)
                    last.then_inc(named("y_done"), 1)

                def combine(b, ready):
                    pe.wait_ge(named("y_ready"), ready)
                    for t in range(NT):
                        for half in range(2):
                            rows = slice(SLOTS * half, SLOTS * (half + 1))
                            last = pe.matmul(ps[:, 2 * t + half, :], turned[b][rows, 2 + t, :], y_e[b][rows, :],
                                             start=False, stop=True, skip_group_check=True)
                    last.then_inc(named("comb_done"), 1)

                dispatch(0, first=True)
                with pe.Fori(0, PAIRS // 2) as i:
                    for h in range(2):
                        gate_up(i, h, 0)
                        dispatch(2 * i + (h + 1))
                        combine(1, with_pass + 4 * i + (2 * h + 2))
                        gate_up(i, h, 1)
                        turn_places(i, h, 0)
                        turn_act(i, h, 0)
                        turn_places(i, h, 1)
                        turn_act(i, h, 1)
                        down(i, h, 0)
                        down(i, h, 1)
                        combine(0, with_pass + 4 * i + (2 * h + 3))
                combine(1, with_pass + (EXPERTS + 2))

            transpose_norm("moe")
            make_row("moe", 6)
            for b in range(4):
                for k in range(4):
                    last = pe.transpose(ps[:, b, k * P:(k + 1) * P], hT[:, 4 * (b % 2) + k, (b // 2) * P:(b // 2 + 1) * P],
                                        ident[:, :])
                last.then_inc(named("ht_psum"), 1)
            pe.wait_ge(named("route_loaded"), 64)
            for t in range(NT):
                o = ps[:, 4, t * 64:t * 64 + GROUPS + EXPERTS]
                for k in range(KC):
                    pe.matmul(o, hT[:, k, t * P:(t + 1) * P], route_w[:, k, :], start=(k == 0), stop=False)
                last = pe.matmul(o, ones[0:1, :], route_b[0:1, :], start=False, stop=True)
            last.then_inc(named("logits_done"), 1)
            pe.wait_ge(named("chosen_made"), 1)
            pe.matmul(ps[:, 5, 0:EXPERTS], before[:, :], chosen[:, 0, :], start=True, stop=True)
            pe.matmul(ps[:, 5, 64:64 + EXPERTS], ones[:, :], chosen[:, 0, :], start=True, stop=False)
            pe.matmul(ps[:, 5, 64:64 + EXPERTS], before[:, :], chosen[:, 1, :], start=False, stop=True)
            pe.matmul(ps[:, 5, 128:128 + EXPERTS], ones[:, :], chosen[:, 0, :], start=True, stop=False)
            pe.matmul(ps[:, 5, 128:128 + EXPERTS], ones[:, :], chosen[:, 1, :], start=False, stop=True
                      ).then_inc(named("ranks_done"), 1)
            pe.wait_ge(named("h_tok_ready"), 4)
            for b in range(4):
                pe.matmul(ps[:, b, :], zeros[:, :], x[:, 0, 0:HALF], start=True, stop=False, skip_group_check=True)
            pe.wait_ge(named("rank_made"), 1)
            moe_pass(0)
            overflow(pe, moe_pass)
            pe.matmul(ps[:, 0, :], zeros[:, :], x[:, 0, 0:HALF], start=False, stop=True,
                      skip_group_check=True).then_inc(named("moe_combined"), 1)
            def softmax_attention(stage):
                maps = SOFTMAX[stage]

                def scores(i):
                    d = maps[i]
                    if i >= 2:
                        pe.wait_ge(score_read, d["n"] - 1)
                    q, k = map_q(d["m"])
                    z = ps[:, 4 + i % 2, :]
                    forget = stage == "odd"
                    pe.matmul(z[:, 0:P], q[:, 0:P], k[:, 0:P], start=True, stop=False, skip_group_check=True)
                    last = pe.matmul(z[:, P:MAPW], q[:, P:T], k[:, 0:T], start=False, stop=not forget, skip_group_check=True)
                    if forget:
                        pick = neg_ident[0:C_HEADS, d["m"]:d["m"] + 1].broadcast_to([C_HEADS, P])
                        pe.matmul(z[:, 0:P], pick, f_cum[0:C_HEADS, 0:P], start=False, stop=False, skip_group_check=True)
                        last = pe.matmul(z[:, P:MAPW], pick, f_cum[0:C_HEADS, :], start=False, stop=True, skip_group_check=True)
                    last.then_inc(score_done, 1)

                def turn(d, before_last):
                    pe.wait_ge(named("probs_ready"), d["turn"] + 1)
                    if before_last:
                        pe.wait_ge(named("turned_out"), before_last["turn"] + 1)
                    p = sm_p[d["m"] % 2]
                    for c in range(3):
                        last = pe.transpose(ps[:, d["turn"] % 2, c * P:(c + 1) * P], p[:, c * P:(c + 1) * P], ident[:, :])
                    last.then_inc(named("probs_turned"), 1)

                def weigh(d):
                    pe.wait_ge(named("turned_out"), d["turn"] + 1)
                    pT = sm_pT[d["turn"] % 2]
                    if d["kind"] == "head":
                        values(d["m"], d["av"], pT)
                        return
                    v = v_tok[:, :, DSA_HEADS * HEAD + 2 * HEAD * d["hb"]:DSA_HEADS * HEAD + 2 * HEAD * (d["hb"] + 1)]
                    o = ps[:, 2 + d["hb"] // 2, (d["hb"] % 2) * T:(d["hb"] % 2 + 1) * T]
                    pe.matmul(o, v[:, 0, :], pT[:, 0:T], start=True, stop=False, skip_group_check=True)
                    pe.matmul(o[:, P:T], v[:, 1, :], pT[:, T:MAPW], start=False, stop=True,
                              skip_group_check=True).then_inc(named("diff_av"), 1)

                turned = [d for d in maps if d["kind"] != "first"]
                for i in range(MAPS + 2):
                    if i < MAPS:
                        scores(i)
                    if 1 <= i <= MAPS and maps[i - 1]["kind"] != "first":
                        j = turned.index(maps[i - 1])
                        turn(maps[i - 1], turned[j - 2] if j >= 2 else None)
                    if i >= 2 and maps[i - 2]["kind"] != "first":
                        weigh(maps[i - 2])
                    if stage == "even" and i == 11:
                        sum_third(8)

            transpose_norm("even")
            make_row("even", 4)
            even = groups_of("even")
            project(*even[0])
            project(*even[1])
            project(*even[2])
            pe.wait_ge(named("kv_scaled"), 1)
            for c in range(LATENT // P):
                for t in range(NT):
                    last = pe.transpose(ps[:, 6, c * T + t * P:c * T + (t + 1) * P], ckv_tok[:, t, c * P:(c + 1) * P], ident[:, :])
            last.then_inc(named("kv_turned"), 1)

            def idx_scores(h):
                if h >= 2:
                    pe.wait_ge(named("idx_relu_done"), h - 1)
                lo = HEAD * (h % 2)
                q, k = qidx[lo:lo + HEAD, h // 2, :], kidx[lo:lo + HEAD, :]
                z = ps[:, 4 + h % 2, :]
                pe.matmul(z[:, 0:P], q[:, 0:P], k[:, 0:P], start=True, stop=False, skip_group_check=True)
                pe.matmul(z[:, P:MAPW], q[:, P:T], k[:, 0:T], start=False, stop=True, skip_group_check=True).then_inc(score_done, 1)

            pe.wait_ge(proj_out, even[2][0] + 1)
            for i in range(4):
                idx_scores(2 * i)
                idx_scores(2 * i + 1)
                project(*even[3 + i])
                if i >= 2:
                    sum_third(4 + i)
            pe.wait_ge(named("ckvT_ready"), 1)
            project(*even[7])
            project(*even[8])
            pe.wait_ge(proj_out, even[8][0] + 1)
            pe.wait_ge(named("idx_relu_done"), IDX_HEADS)
            softmax_attention("even")
            pe.wait_ge(named("diff_sq_done"), 1)
            pe.wait_ge(score_read, MAPS)
            for half in range(2):
                last = pe.matmul(ps[:, 4 + half, :], ones[:, :], diff_sq[:, 2 * half:2 * half + 2, :].rearrange("p h t -> p (h t)"),
                                 start=True, stop=True)
            last.then_inc(named("diff_summed"), 1)
            pe.wait_ge(named("diff_out"), 1)
            pe.wait_ge(av_out, MAPS + DSA_HEADS)
            for n, g in even[-2:]:
                project(n, g)
            def peer(stage):
                L = layer_of(stage)
                transpose_norm(stage)
                make_row(stage, 6)
                for b in range(4):
                    for k in range(4):
                        last = pe.transpose(ps[:, b, k * P:(k + 1) * P], hT[:, 4 * (b % 2) + k, (b // 2) * P:(b // 2 + 1) * P],
                                            ident[:, :])
                    last.then_inc(named("ht_psum"), 1)
                pe.wait_ge(named("keys_loaded"), 16 * (L + 1))
                for a in range(2):
                    last = pe.transpose(ps[:, 4, a * P:(a + 1) * P], keys_raw[:, a, :], ident[:, :])
                last.then_inc(named("keys_psum"), 1)
                pe.wait_ge(named("h_tok_ready"), 4 * (L + 2))
                pe.wait_ge(named("keysT_ready"), L + 1)

                def key_scores(i):
                    pe.wait_ge(proj_out, groups_of(stage)[i][0] + 1)
                    if i >= 2:
                        pe.wait_ge(named("keys_read"), 4 * L + i - 1)
                    for t in range(NT):
                        for j in range(GQ):
                            q = GQ * i + j
                            last = pe.matmul(ps[:, 4 + 2 * (i % 2) + t, j * P:(j + 1) * P], qkT[:, q, t * P:(t + 1) * P],
                                             keysT[:, q % 2, :], start=True, stop=True)
                    last.then_inc(named("key_scored"), 1)

                for i, (n, g) in enumerate(groups_of(stage)):
                    project(n, g)
                    if i >= 1:
                        key_scores(i - 1)
                key_scores(3)
                pe.wait_ge(named("picks_made"), L + 1)
                for n, (bank, pick) in enumerate(((4, pick_i), (4, pick_j), (5, gate))):
                    for t in range(NT):
                        src = pick[:, t, :] if n < 2 else pick[:, t * PEER_HEADS:(t + 1) * PEER_HEADS, :].rearrange("p h k -> p (h k)")
                        last = pe.transpose(ps[:, bank, ((n % 2) * NT + t) * P:((n % 2) * NT + t + 1) * P], src, ident[:, :])
                last.then_inc(named("picks_psum"), 1)
                pe.wait_ge(named("h_parts_loaded"), 24 * 16 * (L + 1))
                pe.wait_ge(named("h_parts_cleared"), L + 1)
                pe.wait_ge(named("experts_made"), L + 1)

                def spread(g, m):
                    pe.wait_ge(named("hots_made"), g * SUB + (L * T // 4 + m + 1))
                    pe.wait_ge(named("hots_j_made"), g * SUB + (L * T // 4 + m + 1))
                    pe.wait_ge(named("coef_out"), g * SUB + (L * T // 4 + m + 1))
                    for j in range(4):
                        last = pe.matmul(ps[:, 4 + m % 2, j * P:(j + 1) * P], hot_j[m % 2][:, j, :], hot_i[m % 2][:, j, :],
                                         start=True, stop=True)
                    last.then_inc(named("spread_done"), 1)

                with pe.Fori(0, BODIES) as g:
                    for i in range(BODY):
                        b, s = i // RING, i % RING
                        pe.wait_ge(named("dots_done"), g * BODY + (L * T + i + RING - 1))
                        for half in range(2):
                            last = pe.matmul(ps[:, 2 * (i % 2) + half, :], token_sel[:, i:i + 1].broadcast_to([P, P]),
                                             h_parts[:, bass.ds(g, 1), half * HALF:(half + 1) * HALF].rearrange("p g n -> p (g n)"),
                                             start=True, stop=True)
                        last.then_inc(named("row_spread"), 1)
                        if b >= 1 and s == 5:
                            spread(g, 2 * (b - 1))
                        if b >= 2 and s == 1:
                            spread(g, 2 * (b - 2) + 1)
                    for m in range(SUB - 3, SUB):
                        spread(g, m)

                pe.wait_ge(named("dots_done"), RING + T * (L + 1))
                for b in range(4):
                    pe.matmul(ps[:, b, :], zeros[:, :], x[:, 0, 0:HALF], start=True, stop=False, skip_group_check=True)
                with pe.Fori(0, CHUNKS // 2) as m:
                    for s in range(2):
                        pe.wait_ge(named(f"v_loaded{s}"), m * 16 + (L * CHUNKS // 2 + 1) * 16)
                        pe.wait_ge(named("keys_out"), 2 * m + (L * CHUNKS + s + 1))
                        for i in range(VI):
                            for t in range(NT):
                                for half in range(2):
                                    last = pe.matmul(ps[:, 2 * t + half, :], coef_ring[s][:, i, t * P:(t + 1) * P],
                                                     v_rows[s][:, i, half * HALF:(half + 1) * HALF], start=False, stop=True,
                                                     skip_group_check=True)
                        last.then_inc(named("v_used"), 1)

            pe.sem_inc(named("spread_done"), 2)
            peer("peer0")
            transpose_norm("odd")
            make_row("odd", 4)
            odd = groups_of("odd")
            for n, g in odd[:-2]:
                project(n, g)
            pe.wait_ge(proj_out, odd[-3][0] + 1)
            pe.wait_ge(named("f_summed"), 1)
            softmax_attention("odd")
            pe.wait_ge(av_out, MAPS + DSA_HEADS + MAPS)
            for n, g in odd[-2:]:
                project(n, g)
            peer("peer1")

        @block.vector
        def _(dve):
            step = stepper(dve, dve_step)

            def rms(stage):
                n = x_updates(stage)
                dve.wait_ge(ssq_done, NT * (n + 1))
                dve.tensor_scalar(var[:, :], ssq[:, :], 1.0 / D, EPS, ALU.mult, ALU.add).then_inc(var_done, 1)
                dve.wait_ge(std_done, n + 1)
                step(dve.reciprocal(rstd[:, :], std[:, :]))

            def norm(stage):
                rms(stage)
                n, a, v = NORM[stage]
                for t in range(NT):
                    dve.tensor_scalar(xn[:, t, :], x[:, t, :], rstd[:, t:t + 1], None, ALU.mult).then_inc(xn_done, 1)
                step(dve.scalar_tensor_tensor(a_cols[:, :], mod_cols[:, a, v + 1, :], 1.0, vec_cols[:, 0, KC * (2 + n):KC * (3 + n)],
                                              ALU.add, ALU.mult))
                for b in range(4):
                    t, half = b // 2, b % 2
                    dve.wait_ge(xt_done, 4 * n + b + 1)
                    for j in range(4):
                        k = 4 * half + j
                        last = dve.tensor_scalar(hT[:, k, t * P:(t + 1) * P], ps[:, b, j * P:(j + 1) * P], a_cols[:, k:k + 1],
                                                 mod_cols[:, a, v, k:k + 1], ALU.mult, ALU.add)
                    last.then_inc(hT_done, 1)

            def residual(stage):
                r = x_updates(stage)
                dve.wait_ge(row_loaded, 16 * (r + 1))
                for half, (n, g) in enumerate(groups_of(stage)[-2:]):
                    dve.wait_ge(proj_done, n + 1)
                    b = 2 * (n % 2)
                    cols = slice(half * HALF, (half + 1) * HALF)
                    dve.tensor_tensor(xn[:, :, cols], ps[:, b:b + 2, :], row[:, cols].unsqueeze(1).broadcast_to([P, NT, HALF]),
                                      ALU.mult).then_inc(proj_out, 1)
                    dve.wait_ge(proj_out, n + 1)
                    if half == 0:
                        step(dve.tensor_tensor(x[:, :, cols], x[:, :, cols], xn[:, :, cols], ALU.add))
                    else:
                        dve.tensor_tensor(x[:, :, cols], x[:, :, cols], xn[:, :, cols], ALU.add).then_inc(x_done, 1)
                        dve.wait_ge(x_done, r + 1)

            def ada_pieces(first, last):
                for n in range(first, last):
                    stage, i = ada_stage(n)
                    ring = ada_ring[stage]
                    third, k = n // KC, n % KC
                    slot = i % len(ring)
                    turns = i // len(ring) + 1
                    if stage == "even":
                        turns += EARLY // len(ada_ring["mix1"])
                    dve.wait_ge(ada_loaded[slot], 16 * turns)
                    acc = ada_acc[stage][third % 2]
                    c = c_silu[:, ADA[third // 3][1] + k:ADA[third // 3][1] + k + 1]
                    if k == 0:
                        if third >= 2:
                            dve.wait_ge(ada_sums, third - 1)
                        dve.tensor_scalar(acc, ring[slot], c, None, ALU.mult).then_inc(ada_used, 1)
                    else:
                        dve.scalar_tensor_tensor(acc, ring[slot], c, acc, ALU.mult, ALU.add).then_inc(ada_used, 1)
                    dve.wait_ge(ada_used, n + 1)

            def take_third(n):
                dve.wait_ge(ada_sums, n + 1)
                half, at = BIAS_AT[n // 3]
                at += 16 * (n % 3)
                dve.tensor_tensor(mod_cols[:, n // 3, 2 * (n % 3):2 * (n % 3) + 2, :].rearrange("p v k -> p (v k)"),
                                  ps[:, 7, 0:16], vec_cols[:, half, at:at + 16], ALU.add).then_inc(mod_made, 1)
                dve.wait_ge(mod_made, n + 1)

            dve.wait_ge(c_ready, 1)
            ada_pieces(0, KC)
            dve.wait_ge(named("vec_ready"), 1)
            take_third(0)
            dve.wait_ge(consts_made, 1)

            norm("mix1")
            ada_pieces(KC, KC + 20)
            take_third(1)
            done = KC + 20
            for h in range(MAPS):
                dve.wait_ge(named("stick_ln"), h + 1)
                keep = st_keep[h % 2]
                step(dve.scalar_tensor_tensor(keep, ps[:, 4 + h % 2, 0:MAPW], 0.0, st_ln[h % 2], ALU.max, ALU.add))
                dve.tensor_tensor(diag_blocks(keep), diag_blocks(keep), before[:, :].unsqueeze(1).broadcast_to([P, 2, P]),
                                  ALU.mult).then_inc(named("stick_kept"), 1)
                now = 2 if h < 4 else 1
                ada_pieces(done, done + now)
                done += now
                if h in (2, 7, 13):
                    take_third((2, 7, 13).index(h) + 2)
            take_third(5)
            residual("mix1")
            def moe_pass(p):
                def places(j):
                    for b in range(2):
                        for t in range(NT):
                            last = dve.tensor_scalar(disp[:, t, SLOTS * b:SLOTS * (b + 1)], iota[:, 0:SLOTS],
                                                     rank[:, t, bass.ds(2 * j + b, 1)], None, ALU.is_equal)
                    last.then_inc(named("disp_made"), 1)

                def weighted_places(e, b):
                    for t in range(NT):
                        last = dve.tensor_scalar(comb[b][:, t, :].rearrange("p (a s) -> p a s", a=2),
                                                 iota[:, 0:SLOTS].unsqueeze(1).broadcast_to([P, 2, SLOTS]),
                                                 rank[:, t, bass.ds(e, 1)], weight[:, t, bass.ds(e, 1)], ALU.is_equal, ALU.mult)
                    last.then_inc(named("comb_made"), 1)

                places(0)
                dve.wait_ge(named("xe_psum"), p * SENT + 1)
                places(1)
                with dve.Fori(0, PAIRS // 2) as i:
                    for h in range(2):
                        for b in range(2):
                            weighted_places(4 * i + (2 * h + b), b)
                        for b in range(2):
                            dve.wait_ge(named("silu_done"), p * EXPERTS + 4 * i + (2 * h + b + 1))
                            dve.tensor_tensor(act_e[b], silu_g[b], ps[:, 6 + b, FF // 2:FF], ALU.mult).then_inc(named("act_done"), 1)
                            if b == 0:
                                dve.wait_ge(named("xe_psum"), p * SENT + 2 * i + (h + 2))
                                places(2 * i + (h + 2))
                        for b in range(2):
                            dve.wait_ge(named("operands_made"), p * EXPERTS + 4 * i + (2 * h + b + 1))
                            dve.tensor_copy(turned[b].rearrange("p a n -> p (a n)"), ps[:, 4 + b, :]).then_inc(named("operands_out"), 1)

            def moe_overflow(p):
                dve.wait_ge(named("comb_done"), p * (EXPERTS + 1))
                dve.memset(turned[1], 0.0)
                dve.tensor_scalar(rank[:, :, :], rank[:, :, :], -float(SLOTS), None, ALU.add).then_inc(named("rank_moved"), 1)
                dve.wait_ge(named("rank_moved"), p)
                moe_pass(p)

            def moe_route():
                step(dve.memset(grp_logit[:, :, :], LOWEST))
                step(dve.memset(weight[:, :, :], 0.0))
                step(dve.memset(rank[:, :, :], -1.0))
                step(dve.memset(turned[1], 0.0))
                step(dve.memset(y_e[1], 0.0))
                dve.wait_ge(named("logits_done"), 1)
                logits = ps[:, 4, 0:128].rearrange("p (t n) -> p t n", t=NT)
                step(dve.tensor_copy(grp_logit[:, :, 0:GROUPS], logits[:, :, 0:GROUPS]))
                step(dve.tensor_copy(exp_logit[:, :, :], logits[:, :, GROUPS:GROUPS + EXPERTS]))
                for t in range(NT):
                    step(dve.max(grp_top[:, t, :], grp_logit[:, t, :]))
                    step(dve.max_index(grp_at[:, t, :], grp_top[:, t, :], grp_logit[:, t, :]))
                step(dve.tensor_copy(grp_num, grp_at[:, :, 0]))
                dve.tensor_scalar(grp_neg, grp_top[:, :, 0], -1.0, None, ALU.mult).then_inc(named("grp_neg_made"), 1)
                for t in range(NT):
                    step(dve.tensor_scalar(grp_hot[:, t, :], iota[:, 0:GROUPS], grp_num[:, t:t + 1], None, ALU.is_equal))
                    for g in range(GROUPS):
                        part = exp_logit[:, t, g * PER_GROUP:(g + 1) * PER_GROUP]
                        if g == 0:
                            step(dve.tensor_scalar(in_grp[:, t, :], part, grp_hot[:, t, 0:1], None, ALU.mult))
                        else:
                            step(dve.scalar_tensor_tensor(in_grp[:, t, :], part, grp_hot[:, t, g:g + 1], in_grp[:, t, :],
                                                          ALU.mult, ALU.add))
                    step(dve.max(in_top[:, t, :], in_grp[:, t, :]))
                    step(dve.max_index(in_at[:, t, :], in_top[:, t, :], in_grp[:, t, :]))
                dve.tensor_scalar(in_neg, in_top[:, :, 0], -1.0, None, ALU.mult).then_inc(named("in_neg_made"), 1)
                step(dve.tensor_copy(in_num[:, :, :], in_at[:, :, :]))
                for t in range(NT):
                    step(dve.scalar_tensor_tensor(expert[:, t, :], grp_num[:, t:t + 1].broadcast_to([P, 2]), float(PER_GROUP),
                                                  in_num[:, t, 0:2], ALU.mult, ALU.add))
                dve.wait_ge(named("grp_exp_done"), NT)
                step(dve.reciprocal(grp_p, grp_sum))
                dve.wait_ge(named("in_exp_done"), NT)
                step(dve.tensor_scalar(in_den, in_exp, 1.0, None, ALU.add))
                step(dve.reciprocal(in_den, in_den))
                step(dve.tensor_tensor(gate1, grp_p, in_den, ALU.mult))
                step(dve.tensor_tensor(gate2, gate1, in_exp, ALU.mult))
                for t in range(NT):
                    step(dve.tensor_scalar(hot1[:, t, :], iota[:, 0:EXPERTS], expert[:, t, 0:1], None, ALU.is_equal))
                    step(dve.tensor_scalar(hot2[:, t, :], iota[:, 0:EXPERTS], expert[:, t, 1:2], None, ALU.is_equal))
                dve.tensor_tensor(chosen[:, :, :], hot1[:, :, :], hot2[:, :, :], ALU.add).then_inc(named("chosen_made"), 1)
                dve.wait_ge(named("chosen_made"), 1)
                for t in range(NT):
                    step(dve.tensor_scalar(hot1[:, t, :], hot1[:, t, :], gate1[:, t:t + 1], None, ALU.mult))
                    step(dve.scalar_tensor_tensor(weight[:, t, 0:EXPERTS], hot2[:, t, :], gate2[:, t:t + 1], hot1[:, t, :],
                                                  ALU.mult, ALU.add))
                dve.wait_ge(named("ranks_done"), 1)
                counted = ps[:, 5, 0:128].rearrange("p (t n) -> p t n", t=NT)[:, :, 0:EXPERTS]
                step(dve.scalar_tensor_tensor(rank[:, :, 0:EXPERTS], counted, 1.0, chosen[:, :, :], ALU.add, ALU.mult))
                step(dve.tensor_scalar(rank[:, :, 0:EXPERTS], rank[:, :, 0:EXPERTS], -1.0, None, ALU.add))
                step(dve.tensor_reduce(most[:, 0:1], ps[:, 5, 128:128 + EXPERTS], AX_X, ALU.max))
                step(dve.tensor_scalar(most[:, 1:2], most[:, 0:1], SLOTS + 0.5, 1.0, ALU.is_gt, ALU.add))
                for more in range(2, T // SLOTS):
                    step(dve.scalar_tensor_tensor(most[:, more:more + 1], most[:, 0:1], more * SLOTS + 0.5, most[:, more - 1:more],
                                                  ALU.is_gt, ALU.add))
                dve.tensor_copy(passes[:, :], most[:, T // SLOTS - 1:T // SLOTS]).then_inc(named("passes_known"), 1)
                dve.sem_inc(named("rank_made"), 1)

            def residual_banks(stage, done):
                r = x_updates(stage)
                dve.wait_ge(row_loaded, 16 * (r + 1))
                for t in range(NT):
                    step(dve.tensor_tensor(xn[:, t, :], ps[:, 2 * t:2 * t + 2, :].rearrange("p b n -> p (b n)"), row[:, :], ALU.mult))
                dve.tensor_tensor(x[:, :, :], x[:, :, :], xn[:, :, :], ALU.add).then_inc(x_done, 1)
                dve.wait_ge(x_done, r + 1)

            def norm_rows(stage):
                rms(stage)
                r = x_updates(stage)
                dve.wait_ge(row_loaded, 16 * (r + 1))
                for t in range(NT):
                    last = dve.scalar_tensor_tensor(x[:, t, :], x[:, t, :], rstd[:, t:t + 1], row[:, :], ALU.mult, ALU.mult)
                    if t < NT - 1:
                        step(last)
                last.then_inc(x_done, 1)
                dve.wait_ge(x_done, r + 1)

            norm("moe")
            moe_route()
            dve.sem_inc(named("operands_out"), 1)
            moe_pass(0)
            overflow(dve, moe_overflow)
            dve.wait_ge(named("moe_combined"), 1)
            residual_banks("moe", None)
            norm_rows("fin1")
            def softmax_attention(stage, add):
                maps = SOFTMAX[stage]

                def scored(i):
                    d = maps[i]
                    b = i % 2
                    dve.wait_ge(score_done, MAPS + IDX_HEADS + d["n"] + 1)
                    dve.tensor_tensor(sm_s[b], ps[:, 4 + b, 0:MAPW], add(d["m"]), ALU.add).then_inc(score_read, 1)
                    dve.wait_ge(score_read, d["n"] + 1)
                    for t in range(NT):
                        last = dve.tensor_reduce(sm_max[b][:, t:t + 1], both_tiles(sm_s[b], t), AX_X, ALU.max, negate=True)
                    last.then_inc(named("max_made"), 1)

                def normed(i):
                    d = maps[i]
                    b = i % 2
                    dve.wait_ge(named("exp_done"), NT * (d["n"] + 1))
                    step(dve.reciprocal(sm_inv[b], sm_sum[b]))
                    if d["kind"] == "second":
                        step(dve.tensor_scalar(sm_inv[b], sm_inv[b], neg_lam[:, 0:1], None, ALU.mult))
                        for t in range(NT):
                            last = dve.scalar_tensor_tensor(both_tiles(sm_p[b], t), both_tiles(sm_p[b], t), sm_inv[b][:, t:t + 1],
                                                            both_tiles(sm_p[1 - b], t), ALU.mult, ALU.add)
                    else:
                        for t in range(NT):
                            last = dve.tensor_scalar(both_tiles(sm_p[b], t), both_tiles(sm_p[b], t), sm_inv[b][:, t:t + 1], None, ALU.mult)
                    if d["kind"] == "first":
                        step(last)
                    else:
                        last.then_inc(named("probs_ready"), 1)

                for i in range(MAPS + 1):
                    if i < MAPS:
                        scored(i)
                    if i >= 1:
                        normed(i - 1)
                    if stage == "even" and i < KC:
                        ada_pieces(8 * KC + i, 8 * KC + i + 1)

            norm("even")
            dve.wait_ge(named("kv_ssq_done"), NT)
            dve.tensor_scalar(kv_std, kv_ssq, 1.0 / LATENT, EPS, ALU.mult, ALU.add).then_inc(named("kv_var_done"), 1)
            dve.wait_ge(named("kv_std_done"), 1)
            step(dve.reciprocal(kv_std, kv_std))
            for t in range(NT):
                last = dve.tensor_scalar(ckv_tok[:, t, :], ckv_tok[:, t, :], kv_std[:, t:t + 1], None, ALU.mult)
            last.then_inc(named("kv_scaled"), 1)
            dve.wait_ge(named("even_vec_loaded"), 16 * 3)
            lam_pairs = lam_vec.rearrange("p (a b) d -> p a b d", b=2)
            step(dve.tensor_tensor(lam_prod[:, :, :], lam_pairs[:, :, 0, :], lam_pairs[:, :, 1, :], ALU.mult))
            dve.tensor_reduce(lam_sum, lam_prod[:, :, :], AX_X, ALU.add).then_inc(named("lam_sum_made"), 1)
            step(dve.tensor_scalar(subln_col, subln_raw, 1.0 - LAM_INIT, None, ALU.mult))
            dve.wait_ge(named("lam_exp_done"), 1)
            step(dve.tensor_tensor(neg_lam, lam_exp[:, 1:2], lam_exp[:, 0:1], ALU.subtract))
            step(dve.tensor_scalar(neg_lam, neg_lam, -LAM_INIT, None, ALU.add))
            dve.wait_ge(named("kv_turned"), 1)
            for c in range(LATENT // P):
                last = dve.tensor_scalar(ckvT[:, c, :], ps[:, 6, c * T:(c + 1) * T], kv_gain[:, c:c + 1], None, ALU.mult)
            last.then_inc(named("ckvT_ready"), 1)
            dve.wait_ge(proj_out, groups_of("even")[2][0] + 1)
            for h in range(IDX_HEADS):
                dve.wait_ge(named("idx_relu_done"), h + 1)
                if h == 0:
                    for t in range(NT):
                        last = dve.tensor_scalar(both_tiles(idx_score, t), both_tiles(idx_relu[0], t), widx[:, t, 0:1], 0.0, ALU.mult, ALU.add)
                else:
                    for t in range(NT):
                        last = dve.scalar_tensor_tensor(both_tiles(idx_score, t), both_tiles(idx_relu[h % 2], t), widx[:, t, h:h + 1],
                                                        both_tiles(idx_score, t), ALU.mult, ALU.add)
                last.then_inc(named("idx_summed"), 1)
                dve.wait_ge(named("idx_summed"), h + 1)
                ada_pieces(EARLY + 2 * h, EARLY + 2 * h + 2)
                if h == 6:
                    take_third(6)
            dve.wait_ge(named("idx_causal"), 1)
            for r in range(DSA_TOP // 8):
                for t in range(NT):
                    step(dve.max(idx_top, both_tiles(idx_score, t)))
                    step(dve.match_replace(both_tiles(idx_score, t), idx_top, both_tiles(idx_score, t), TAKEN))
            step(dve.tensor_scalar(idx_mask, idx_score, TAKEN, NEG, ALU.not_equal, ALU.mult))
            take_third(7)
            dve.wait_ge(named("rel_loaded"), 32)
            dsa_maps = rel_maps[:, 0:DSA_HEADS, :]
            step(dve.tensor_tensor(dsa_maps, dsa_maps, idx_mask.unsqueeze(1).broadcast_to([P, DSA_HEADS, MAPW]), ALU.add))
            softmax_attention("even", lambda m: rel_maps[:, m if m < DSA_HEADS else (m + DSA_HEADS) // 2, :])
            take_third(8)
            dve.wait_ge(named("diff_summed"), 1)
            dve.tensor_scalar(diff_std.rearrange("p h t -> p (h t)"), ps[:, 4:6, :].rearrange("p b n -> p (b n)"), 0.5 / HEAD, EPS,
                              ALU.mult, ALU.add).then_inc(named("diff_var_done"), 1)
            dve.wait_ge(named("diff_std_done"), 1)
            step(dve.reciprocal(diff_std[:, :, :], diff_std[:, :, :]))
            dve.scalar_tensor_tensor(oT[:, 4:8, :].rearrange("p h t -> p (h t)"), ps[:, 2:4, :].rearrange("p b n -> p (b n)"),
                                     subln_col[:, 0:1], diff_std.rearrange("p h t -> p (h t)"), ALU.mult, ALU.mult
                                     ).then_inc(named("diff_out"), 1)
            residual("even")
            def peer(stage):
                L = layer_of(stage)
                norm(stage)
                dve.wait_ge(named("h_tok_ready"), 4 * (L + 2))
                step(dve.tensor_copy(part_hi[:, :, :], h_tok[:, :, :]))
                step(dve.tensor_tensor(part_rest[:, :, :], h_tok[:, :, :], part_hi[:, :, :], ALU.subtract))
                step(dve.tensor_copy(part_mid[:, :, :], part_rest[:, :, :]))
                dve.tensor_tensor(part_lo[:, :, :], part_rest[:, :, :], part_mid[:, :, :], ALU.subtract).then_inc(named("parts_made"), 1)
                for i in range(4):
                    dve.wait_ge(named("key_scored"), 4 * L + i + 1)
                    rows = [(t * HP + GQ * i + j, ps[:, 4 + 2 * (i % 2) + t, j * P:(j + 1) * P], key_left[:, t * GQ + j, :])
                            for t in range(NT) for j in range(GQ)]
                    for r, s, _ in rows:
                        last = dve.max(key_top[:, r, 0:8], s)
                    step(last)
                    for r, s, left in rows:
                        dve.max_index(key_at[:, r, 0:8], key_top[:, r, 0:8], s)
                        last = dve.match_replace(left, key_top[:, r, 0:8], s, LOWEST)
                    last.then_inc(named("keys_read"), 1)
                    dve.wait_ge(named("keys_read"), 4 * L + i + 1)
                    for r, _, left in rows:
                        last = dve.max(key_top[:, r, 8:16], left)
                    step(last)
                    for r, _, left in rows:
                        last = dve.max_index(key_at[:, r, 8:16], key_top[:, r, 8:16], left)
                    step(last)
                    square = [P, GH, PEER_K, PEER_K]
                    firsts = [slice(t * HP + GQ * i, t * HP + GQ * (i + 1), 2) for t in range(NT)]
                    seconds = [slice(t * HP + GQ * i + 1, t * HP + GQ * (i + 1), 2) for t in range(NT)]
                    for t in range(NT):
                        mine = slice(t * HP + GQ * i, t * HP + GQ * (i + 1))
                        dve.tensor_copy(key_num[:, mine, :], key_at[:, mine, :])
                        last = dve.tensor_tensor(cand[:, t * GH:(t + 1) * GH, :].rearrange("p h (a b) -> p h a b", b=PEER_K),
                                                 key_top[:, firsts[t], :].unsqueeze(3).broadcast_to(square),
                                                 key_top[:, seconds[t], :].unsqueeze(2).broadcast_to(square), ALU.add)
                    step(last)
                    heads = [(t * PEER_HEADS + GH * i + h, cand[:, t * GH + h, :], cand_left[:, t * GH + h, :])
                             for t in range(NT) for h in range(GH)]
                    for r, s, _ in heads:
                        last = dve.max(best[:, r, 0:8], s)
                    step(last)
                    for r, s, left in heads:
                        dve.max_index(best_at[:, r, 0:8], best[:, r, 0:8], s)
                        last = dve.match_replace(left, best[:, r, 0:8], s, LOWEST)
                    step(last)
                    for r, _, left in heads:
                        last = dve.max(best[:, r, 8:16], left)
                    step(last)
                    for r, _, left in heads:
                        last = dve.max_index(best_at[:, r, 8:16], best[:, r, 8:16], left)
                    step(last)
                    at_of_group = best_at.rearrange("p (t h) k -> p t (h k)", t=NT)[:, :, GK * i:GK * (i + 1)]
                    dve.tensor_scalar(best_hi, at_of_group, 4, None, ALU.logical_shift_right)
                    step(dve.tensor_scalar(best_lo, at_of_group, PEER_K - 1, None, ALU.bitwise_and))
                    dve.tensor_copy(best_row, best_hi)
                    step(dve.tensor_copy(best_col, best_lo))
                    sides = [(match[2 * n + t], place[:, t, :], own[t], pick[:, t, GK * i:GK * (i + 1)])
                             for n, (place, own, pick) in enumerate(((best_row, firsts, pick_i), (best_col, seconds, pick_j)))
                             for t in range(NT)]
                    for hits, place, _, _ in sides:
                        last = dve.tensor_tensor(hits[:, :, :], iota[:, 0:PEER_K].unsqueeze(1).broadcast_to([P, GK, PEER_K]),
                                                 place.unsqueeze(2).broadcast_to([P, GK, PEER_K]), ALU.is_equal)
                    step(last)
                    for hits, _, own, _ in sides:
                        as_heads = hits.rearrange("p (h k) m -> p h k m", h=GH)
                        last = dve.tensor_tensor(as_heads, as_heads, key_num[:, own, :].unsqueeze(2).broadcast_to(square), ALU.mult)
                    step(last)
                    for hits, _, _, pick in sides:
                        last = dve.tensor_reduce(pick, hits[:, :, :], AX_X, ALU.add)
                    step(last)
                full = [P, NT * PEER_HEADS, PEER_K]
                dve.tensor_tensor(gate[:, :, :], best[:, :, :], best[:, :, 0:1].broadcast_to(full), ALU.subtract
                                  ).then_inc(named("gate_diff"), 1)
                dve.wait_ge(named("gate_exp"), L + 1)
                step(dve.tensor_reduce(gate_sum, gate[:, :, :], AX_X, ALU.add))
                step(dve.reciprocal(gate_sum, gate_sum))
                dve.tensor_tensor(gate[:, :, :], gate[:, :, :], gate_sum.unsqueeze(2).broadcast_to(full), ALU.mult
                                  ).then_inc(named("picks_made"), 1)
                dve.wait_ge(named("picks_psum"), L + 1)
                dve.tensor_copy(peer_i[:, :], ps[:, 4, 0:T])
                dve.tensor_scalar(peer_neg_j[:, :], ps[:, 4, T:2 * T], -1.0, None, ALU.mult)
                step(dve.tensor_copy(peer_g[:, :], ps[:, 5, 0:T]))
                step(dve.scalar_tensor_tensor(peer_num[:, :], peer_i[:, :], float(NKEYS), peer_neg_j[:, :], ALU.mult, ALU.subtract))
                dve.tensor_scalar(peer_e[:, :], peer_num[:, :], float(L * PEER_EXPERTS), None, ALU.add).then_inc(named("experts_made"), 1)

                def coefs(g, b):
                    n = g * (BODY // RING) + (L * T // RING + b + 1)
                    cols = slice(b * RING, (b + 1) * RING)
                    dve.wait_ge(named("gelu_done"), n)
                    dve.tensor_tensor(coef[:, cols], gelu[:, cols], peer_g[:, bass.ds(g * BODY + b * RING, RING)], ALU.mult
                                      ).then_inc(named("coef_made"), 1)
                    dve.wait_ge(named("coef_made"), n)

                def first_hots(g, m):
                    dve.wait_ge(named("spread_done"), g * SUB + (L * T // 4 + m + 1))
                    for j in range(4):
                        i = 4 * m + j
                        last = dve.tensor_scalar(hot_i[m % 2][:, j, :], iota[:, :], peer_i[:, bass.ds(g * BODY + i, 1)], coef[:, i:i + 1],
                                                 ALU.is_equal, ALU.mult)
                    last.then_inc(named("hots_made"), 1)

                with dve.Fori(0, BODIES) as g:
                    for i in range(BODY):
                        b, s = i // RING, i % RING
                        dve.wait_ge(named(f"u_loaded{s}"), g * (16 * BODY // RING) + (L * T // RING + b + 1) * 16)
                        dve.wait_ge(named("row_spread"), g * BODY + (L * T + i + 1))
                        dve.tensor_tensor_reduce(u_rows[s], u_rows[s], ps[:, 2 * (i % 2):2 * (i % 2) + 2, :].rearrange(
                            "p b n -> p (b n)"), 1.0, 0.0, ALU.mult, ALU.add, dots[:, i:i + 1]).then_inc(named("dots_done"), 1)
                        if b >= 1 and s == 3:
                            coefs(g, b - 1)
                            first_hots(g, 2 * (b - 1))
                        if b >= 1 and s == 7:
                            first_hots(g, 2 * (b - 1) + 1)
                    coefs(g, BODY // RING - 1)
                    first_hots(g, SUB - 2)
                    first_hots(g, SUB - 1)
                dve.wait_ge(named("v_used"), CHUNKS * (L + 1))
                residual_banks(stage, None)

            dve.sem_inc(named("dots_done"), RING)
            peer("peer0")
            norm("odd")
            n = groups_of("odd")[0][0]
            dve.wait_ge(proj_done, n + 1)
            dve.wait_ge(named("forget_loaded"), 16)
            step(dve.tensor_scalar(f_logit[0:C_HEADS, :], ps[0:C_HEADS, 2 * (n % 2), 0:T], forget_col[0:C_HEADS, 0:1], None, ALU.add))
            dve.sem_inc(proj_out, 1)
            dve.sem_inc(named("f_made"), 1)
            dve.wait_ge(named("f_log_done"), 1)
            step(dve.scalar_tensor_tensor(f_log[0:C_HEADS, :], f_logit[0:C_HEADS, :], 0.0, f_log[0:C_HEADS, :], ALU.min, ALU.subtract))
            step(dve.tensor_tensor_scan(f_cum[0:C_HEADS, :], ones[0:C_HEADS, 0:1].broadcast_to([C_HEADS, T]), f_log[0:C_HEADS, :],
                                        0.0, ALU.mult, ALU.add))
            dve.tensor_scalar(neg_ident[0:C_HEADS, :], ident[0:C_HEADS, 0:C_HEADS], -1.0, None, ALU.mult).then_inc(named("f_summed"), 1)
            softmax_attention("odd", lambda m: causal_add[:, :])
            residual("odd")
            peer("peer1")
            norm_rows("all")


INPUTS = [
    "x", "c", "ada_w", "ada_b", "norm_g", "final_g", "sb_w_in", "sb_w_out", "moe_w_grp", "moe_b_grp", "moe_w_exp",
    "moe_b_exp", "moe_w_gate", "moe_w_up", "moe_w_down", "c_2", "rel_bias_2", "ada_w_2", "ada_b_2", "norm_mix_2",
    "norm_ffn_2", "norm_final_2", "even_w_in_2", "even_w_out_2", "a_kv_norm_2", "a_w_uk_2", "a_w_uv_2", "b_lambda_2",
    "b_subln_2", "odd_w_in_2", "odd_b_forget_2", "odd_w_out_2", "peer_w_q_2", "peer_sub_keys_2", "peer_u_2", "peer_v_2",
]


def kernel(**inputs):
    import numpy as np
    import concourse.bacc as bacc
    from concourse.bass_utils import run_bass_kernel_spmd

    nc = bacc.Bacc("TRN2", target_bir_lowering=False, num_devices=1)
    arrays, args = {}, {}
    for name in INPUTS:
        a = np.ascontiguousarray(inputs[name])
        arrays["in_" + name] = a
        args[name] = nc.dram_tensor("in_" + name, a.shape, mybir.dt.from_np(a.dtype), kind="ExternalInput").ap()
    out = nc.dram_tensor("out_x", (1, T, D), F32, kind="ExternalOutput").ap()
    two_block_kernel(nc, args, out)
    r = run_bass_kernel_spmd(nc, [arrays], core_ids=[0])
    return r.results[0]["out_x"]
```

```python
import math
from contextlib import ExitStack

import concourse.bass as bass
from concourse import mybir

F32 = mybir.dt.float32
BF16 = mybir.dt.bfloat16
F32R = mybir.dt.float32r
U32 = mybir.dt.uint32
I32 = mybir.dt.int32
ALU = mybir.AluOpType
ACT = mybir.ActivationFunctionType
AX_X = mybir.AxisListType.X

P = 128
D = 1024
KC = D // P
T = 256
NT = T // P
HALF = D // 2
EPS = 1e-6
NEG = -1e30
LOWEST = -3.0e38
TAKEN = -3.3e38

HEAD = 64
MAPS = 16
SCALE = HEAD ** -0.5
MAPW = 3 * P

IDX_HEADS = 8
DSA_TOP = 64
DSA_HEADS = 8
DIFF_HEADS = 4
LATENT = 256
REL_BUCKETS = 32
REL_HEADS = 12

GROUPS = 4
PER_GROUP = 8
EXPERTS = 32
FF = 512
SLOTS = 64

PEER_HEADS = 8
PEER_K = 16
NKEYS = 128
PEER_EXPERTS = NKEYS * NKEYS
RING = 8
BODY = 32


def rel_bucket_ranges():
    exact = REL_BUCKETS // 2
    bucket = []
    for d in range(T):
        if d < exact:
            bucket.append(d)
        else:
            bucket.append(min(REL_BUCKETS - 1, exact + int(math.log(d / exact) / math.log(128 / exact) * exact)))
    return [(b, bucket.index(b), T - 1 - bucket[::-1].index(b)) for b in sorted(set(bucket))]


def two_block_kernel(nc, I, out):
    with ExitStack() as ctx:
        def sb(name, shape, dt=F32):
            return ctx.enter_context(nc.sbuf_tensor("sb_" + name, shape, dt))

        def sem(name):
            return ctx.enter_context(nc.semaphore(name))

        ps = ctx.enter_context(nc.psum_tensor("psum", [P, 8, HALF], F32))
        rel_rows_d = nc.dram_tensor("rel_rows_d", [REL_HEADS, P, MAPW], F32).ap()

        x = sb("x", [P, NT, D])
        row = sb("row", [P, D])
        ident = sb("ident", [P, P])
        iota = sb("iota", [P, P])
        iota_16 = sb("iota_16", [P, PEER_K], BF16)
        ones = sb("ones", [P, P])
        zeros = sb("zeros", [P, P])
        neg_ones = sb("neg_ones", [P, P])
        neg_tri = sb("neg_tri", [P, P])
        before = sb("before", [P, P])
        causal_add = sb("causal_add", [P, MAPW])
        token_sel = sb("token_sel", [P, BODY], BF16)
        vec_cols = sb("vec_cols", [P, 2, 112])
        mod_cols = sb("mod_cols", [P, 3, 6, KC])
        c_silu = sb("c_silu", [P, 2 * KC])
        a_cols = sb("a_cols", [P, KC])
        ssq = sb("ssq", [P, 2, NT])
        var = sb("var", [P, NT])
        std = sb("std", [P, NT])
        rstd = sb("rstd", [P, NT])
        small = sb("small", [P, 256])
        peer_neg_i = sb("peer_neg_i", [P, T])
        peer_neg_j = sb("peer_neg_j", [P, T])
        peer_g = sb("peer_g", [P, T])
        peer_e = sb("peer_e", [P, T], U32)
        passes = sb("passes", [P, 1], I32)

        AREA = 47104
        with nc.sbuf_tensor("sb_area", [P, AREA], F32) as area:
            pass
        F32R_AT = AREA - 5 * D * 2
        area_start = sb("area_start", [P, F32R_AT])
        f32r_area = sb("f32r_area", [P, AREA - F32R_AT], F32R)

        def view(at, *shape, dt=F32):
            n = math.prod(shape)
            words = n if dt != BF16 else n // 2
            assert at + words <= AREA, (at, shape)
            v = area[:, at:at + words]
            if dt != F32:
                v = v.bitcast(dt)
            if len(shape) == 2:
                v = v.rearrange("p (a b) -> p a b", b=shape[1])
            if len(shape) == 3:
                v = v.rearrange("p (a b c) -> p a b c", b=shape[1], c=shape[2])
            return v

        def start_view(at, *shape):
            n = math.prod(shape)
            assert at + n <= F32R_AT, (at, shape)
            return area_start[:, at:at + n].rearrange("p (a b) -> p a b", b=shape[1])

        def f32r_view(at, *shape):
            n = math.prod(shape)
            assert at >= F32R_AT and at + n <= AREA, (at, shape)
            return f32r_area[:, at - F32R_AT:at - F32R_AT + n].rearrange("p (a b) -> p a b", b=shape[1])

        hT = view(0, KC, T)
        xn = view(2048, NT, D)
        wring = [view(4096 + 4096 * i, KC, HALF) for i in range(3)]
        qkT = view(16384, MAPS, T)
        v_tok = view(20480, NT, D)
        oT = view(22528, KC, T)
        AT = 24576
        vec_raw = view(2048, 2, P)
        THIRD = 2 * D
        PIECES = 9 * KC
        EARLY = 6 * KC
        ADA_AT = 28416
        ada_acc = {"mix1": [view(ADA_AT + THIRD * i, THIRD) for i in range(2)]}
        ada_ring = {"mix1": [view(ADA_AT + THIRD * (2 + i), THIRD) for i in range(6)]}

        def ada_stage(n):
            return ("mix1", n) if n < EARLY else ("even", n - EARLY)

        consts_made = sem("consts_made")
        vec_loaded = sem("vec_loaded")
        x_loaded = sem("x_loaded")
        x_done = sem("x_done")
        row_loaded = sem("row_loaded")
        ada_loaded = [sem(f"ada_loaded{i}") for i in range(6)]
        ada_used = sem("ada_used")
        c_ready = sem("c_ready")
        ada_sums = sem("ada_sums")
        mod_made = sem("mod_made")
        ident_made = sem("ident_made")
        ssq_done = sem("ssq_done")
        var_done = sem("var_done")
        std_done = sem("std_done")
        xn_done = [sem(f"xn_done{t}") for t in range(NT)]
        x_parts = sem("x_parts")
        xt_done = sem("xt_done")
        hT_done = sem("hT_done")
        w_loaded = [sem(f"w_loaded{i}") for i in range(3)]
        proj_done = sem("proj_done")
        proj_out = sem("proj_out")
        score_done = sem("score_done")
        score_read = sem("score_read")
        av_done = sem("av_done")
        av_out = sem("av_out")
        dve_step = sem("dve_step")
        act_step = sem("act_step")
        pool_step = sem("pool_step")
        stored = sem("stored")
        sems = {}

        def named(name):
            if name not in sems:
                sems[name] = sem(name)
            return sems[name]

        def stepper(eng, step_sem):
            n = [0]

            def step(ins):
                n[0] += 1
                ins.then_inc(step_sem, 1)
                eng.wait_ge(step_sem, n[0])
            return step

        groups = []

        def group(stage, w, kind, src, dst, scale=1.0, by="act", dup=0):
            groups.append(dict(stage=stage, w=w, kind=kind, src=src, dst=dst, scale=scale, by=by, dup=dup))

        ckvT = view(AT, 2, T)
        ckv_tok = view(AT + 512, NT, LATENT)
        kidx = view(AT + 1024, T)
        widx = view(AT + 1280, NT, IDX_HEADS)
        qidx = view(AT + 1312, 4, T)
        EV = AT + 1312 + 1024
        f_cum = view(AT, T)

        def sb_groups():
            w = I["sb_w_in"][0]
            for g in range(4):
                group("mix1", w[:, g * HALF:(g + 1) * HALF], "F", hT, qkT[:, 4 * g:4 * g + 4, :], SCALE if g < 2 else 1.0)
            for g in range(2):
                group("mix1", w[:, (4 + g) * HALF:(5 + g) * HALF], "T", hT, v_tok[:, :, g * HALF:(g + 1) * HALF])
            for g in range(2):
                group("mix1", I["sb_w_out"][0][:, g * HALF:(g + 1) * HALF], "T", oT, g, by="residual")

        def even_groups():
            w = I["even_w_in_2"][0]
            a, i, kk = 512 + LATENT, 512 + LATENT + 512, 512 + LATENT + 512 + 64
            b = kk + 8
            group("even", w[:, 512:a], "T", hT, ckv_tok)
            group("even", w[:, a:i], "F", hT, qidx)
            group("even", w[:, i:b], "I", hT, None)
            group("even", w[:, 0:512], "F", hT, qkT[:, 0:4, :], SCALE)
            group("even", w[:, b:b + 512], "F", hT, qkT[:, 4:8, :], SCALE)
            group("even", w[:, b + 512:b + 1024], "F", hT, qkT[:, 12:16, :])
            group("even", w[:, b + 1024:b + 1536], "T", hT, v_tok[:, :, 512:1024])
            group("even", I["a_w_uk_2"][0].rearrange("c h d -> c (h d)"), "F", ckvT, qkT[:, 8:12, :])
            group("even", I["a_w_uv_2"][0].rearrange("c h d -> c (h d)"), "T", ckvT, v_tok[:, :, 0:512])
            for g in range(2):
                group("even", I["even_w_out_2"][0][:, g * HALF:(g + 1) * HALF], "T", oT, g, by="residual")

        def odd_groups():
            w = I["odd_w_in_2"][0]
            group("odd", w[:, 3072:3088], "C", hT, None, by="dve")
            for g in range(4):
                group("odd", w[:, g * HALF:(g + 1) * HALF], "F", hT, qkT[:, 4 * g:4 * g + 4, :], SCALE if g < 2 else 1.0)
            for g in range(2):
                group("odd", w[:, (4 + g) * HALF:(5 + g) * HALF], "T", hT, v_tok[:, :, g * HALF:(g + 1) * HALF])
            for g in range(2):
                group("odd", I["odd_w_out_2"][0][:, g * HALF:(g + 1) * HALF], "T", oT, g, by="residual")

        def peer_groups(layer):
            w = I["peer_w_q_2"][layer]
            for g in range(4):
                group(f"peer{layer}", w[:, g * HALF:(g + 1) * HALF], "F", hT, qkT[:, 4 * g:4 * g + 4, :])

        sb_groups()
        even_groups()
        peer_groups(0)
        odd_groups()
        peer_groups(1)

        def groups_of(stage):
            return [(n, g) for n, g in enumerate(groups) if g["stage"] == stage]

        def w_turns(n):
            return sum(32 if g["kind"] == "I" else 16 for g in groups[n % 3:n + 1:3])

        def x_updates(stage):
            return {"mix1": 0, "moe": 1, "fin1": 2, "even": 3, "peer0": 4, "odd": 5, "peer1": 6, "all": 7}[stage]

        NORM = {"mix1": (0, 0, 0), "moe": (1, 0, 3), "even": (2, 1, 0), "peer0": (3, 1, 3), "odd": (4, 2, 0), "peer1": (5, 2, 3)}
        GAINS = [I["norm_g"][0, 0], I["norm_g"][0, 1], I["norm_mix_2"][0], I["norm_ffn_2"][0], I["norm_mix_2"][1],
                 I["norm_ffn_2"][1]]
        h_tok = view(2048, NT, D)
        moe_at = ((24576, 24576 + 4096, 24576 + 8192), (36864, 36864 + 4096, 16384))
        moe_w = [[view(moe_at[b][i], (KC, KC, FF // P)[i], (FF, FF, D)[i]) for i in range(3)] for b in range(2)]
        M = 8192
        route_w = view(M, KC, GROUPS + EXPERTS)
        route_b = view(M + 288, GROUPS + EXPERTS)
        grp_logit = view(M + 352, NT, 8)
        exp_logit = view(M + 368, NT, EXPERTS)
        grp_top = view(M + 432, NT, 8)
        grp_at = view(M + 448, NT, 8, dt=U32)
        grp_num = view(M + 464, NT)
        grp_neg = view(M + 466, NT)
        grp_exp = view(M + 468, NT, GROUPS)
        grp_sum = view(M + 476, NT)
        grp_p = view(M + 478, NT)
        grp_hot = view(M + 480, NT, GROUPS)
        in_grp = view(M + 488, NT, PER_GROUP)
        in_top = view(M + 504, NT, 8)
        in_at = view(M + 520, NT, 8, dt=U32)
        in_num = view(M + 536, NT, 8)
        in_neg = view(M + 552, NT)
        in_exp = view(M + 554, NT)
        in_den = view(M + 556, NT)
        gate1 = view(M + 558, NT)
        gate2 = view(M + 560, NT)
        expert = view(M + 562, NT, 2)
        hot1 = view(M + 576, NT, EXPERTS)
        hot2 = view(M + 640, NT, EXPERTS)
        chosen = view(M + 704, NT, EXPERTS)
        RW = EXPERTS + 4
        weight = view(M + 768, NT, RW)
        rank = view(M + 768 + NT * RW, NT, RW)
        most = view(M + 768 + 2 * NT * RW, 8)
        disp = view(M + 1024, NT, 2 * SLOTS)
        comb = [view(M + 1280 + 256 * b, NT, 2 * SLOTS) for b in range(2)]
        xe = [view(M + 1792 + 1024 * b, KC, 2 * SLOTS) for b in range(2)]
        silu_g = [view(M + 3840 + 256 * b, FF // 2) for b in range(2)]
        act_e = [view(M + 4352 + 256 * b, FF // 2) for b in range(2)]
        turned = [view(M + 4864 + 512 * b, 4, P) for b in range(2)]
        y_e = [view(M + 5888 + 512 * b, HALF) for b in range(2)]
        PAIRS = EXPERTS // 2
        SENT = PAIRS + 1
        PLACED = PAIRS + 2

        def overflow(eng, one_pass):
            eng.wait_ge(named("passes_known"), 1)
            n = eng.value_load(passes[0:1, 0:1], min_val=1, max_val=T // SLOTS)
            with eng.If(n > 1):
                with eng.Fori(1, n) as p:
                    one_pass(p)
        idx_relu = [view(EV + MAPW * i, MAPW) for i in range(2)]
        idx_score = view(EV + 2 * MAPW, MAPW)
        idx_mask = view(EV + 3 * MAPW, MAPW)
        idx_top = view(EV + 4 * MAPW, 8)
        kv_ssq = view(EV + 1552, NT)
        kv_std = view(EV + 1554, NT)
        lam_prod = view(EV + 1556, 2, HEAD)
        lam_sum = view(EV + 1684, 2)
        lam_exp = view(EV + 1686, 2)
        neg_lam = view(EV + 1688, 1)
        subln_col = view(EV + 1689, 1)
        SM = EV + 1696
        sm_s = [view(SM + MAPW * i, MAPW) for i in range(2)]
        sm_p = [view(SM + MAPW * (2 + i), MAPW) for i in range(2)]
        sm_pT = [view(SM + MAPW * (4 + i), MAPW) for i in range(2)]
        sm_max = [view(SM + MAPW * 6 + 2 * i, 2) for i in range(2)]
        sm_sum = [view(SM + MAPW * 6 + 4 + 2 * i, 2) for i in range(2)]
        sm_inv = [view(SM + MAPW * 6 + 8 + 2 * i, 2) for i in range(2)]
        diff_sq = view(SM + MAPW * 6 + 16, DIFF_HEADS, T)
        diff_std = view(SM + MAPW * 6 + 16 + DIFF_HEADS * T, DIFF_HEADS, T)
        ada_acc["even"] = [view(SM + MAPW * 6 + 16 + THIRD, THIRD), view(SM + MAPW * 6 + 16, THIRD)]
        ada_ring["even"] = [view(SM + MAPW * 6 + 16 + THIRD * (2 + i), THIRD) for i in range(3)]
        LAM_INIT = 0.8 - 0.6 * math.exp(0.0)

        C_HEADS = MAPS
        f_logit = view(AT + T, T)
        f_abs = view(AT + 2 * T, T)
        f_log = view(AT + 3 * T, T)
        neg_ident = view(AT + 4 * T, C_HEADS)
        forget_col = view(AT + 4 * T + C_HEADS, 1)

        SOFTMAX = {"even": [], "odd": []}
        for m in range(MAPS):
            if m < DSA_HEADS:
                SOFTMAX["even"].append(dict(m=m, kind="head", n=m, turn=m, av=MAPS + m))
            else:
                hb = (m - DSA_HEADS) // 2
                SOFTMAX["even"].append(dict(m=m, kind="second" if m % 2 else "first", n=m, turn=DSA_HEADS + hb, hb=hb))
            SOFTMAX["odd"].append(dict(m=m, kind="head", n=MAPS + m, turn=DSA_HEADS + DIFF_HEADS + m, av=MAPS + DSA_HEADS + m))

        def both_tiles(t, nt):
            return t[:, 0:P] if nt == 0 else t[:, P:MAPW]

        def wait_read(eng, d):
            if d["kind"] == "head":
                eng.wait_ge(av_done, d["av"] + 1)
            else:
                eng.wait_ge(named("diff_av"), d["hb"] + 1)
        C_WORDS = NKEYS * T
        coef_all = start_view(0, T, NKEYS)
        UV = C_WORDS
        u_rows = [view(UV + D * s, D) for s in range(RING)]
        VI = 2
        v_rows = [start_view(UV + VI * D * s, VI, D) for s in range(2)]
        v_high = [f32r_view(UV + VI * D * (2 + s), VI, D) for s in range(2)]
        v_low = [f32r_view(UV + VI * D * (4 + s), VI, D) for s in range(2)]
        h_parts = view(UV + RING * D, 8, D, dt=BF16)
        AB = UV + RING * D + 4 * D
        hots = [view(AB + 8 * P * s, 8, P) for s in range(2)]
        hot_i = [h[:, 0:4, :] for h in hots]
        hot_j = [h[:, 4:8, :] for h in hots]
        coef_high = [f32r_view(AB + VI * T * s, VI, T) for s in range(2)]
        coef_low = [f32r_view(AB + VI * T * (2 + s), VI, T) for s in range(2)]
        keys_raw = view(AB, 2, P)
        keysT = view(AB + 2 * P, 2, P)
        part_hi = view(UV, NT, D, dt=BF16)
        part_mid = view(UV + D, NT, D, dt=BF16)
        part_lo = view(UV + 2 * D, NT, D, dt=BF16)
        part_rest = view(UV + 3 * D, NT, D)
        K = 20480
        HP = 2 * PEER_HEADS
        GQ = HP // 4
        GH = GQ // 2
        key_top = view(K, NT * HP, PEER_K)
        key_at = view(K + 512, NT * HP, PEER_K, dt=U32)
        key_num = view(K + 1024, NT * HP, PEER_K, dt=BF16)
        key_left = view(K + 1536, GQ, NKEYS)
        cand = view(K + 2560, GH, PEER_K * PEER_K)
        cand_left = view(K + 3584, GH, PEER_K * PEER_K)
        key_score = view(K + 10240, HP, NKEYS)
        best = view(K + 6144, NT * PEER_HEADS, PEER_K)
        best_at = view(K + 6400, NT * PEER_HEADS, PEER_K, dt=U32)
        GK = GH * PEER_K
        best_hi = view(K + 6656, GK, dt=U32)
        best_lo = view(K + 6784, GK, dt=U32)
        best_row = view(K + 6912, GK, dt=BF16)
        best_col = view(K + 7040, GK, dt=BF16)
        match = [view(K + 7168 + GK * PEER_K * i, GK, PEER_K, dt=BF16) for i in range(2)]
        pick_i = view(K + 9216, NT, P)
        pick_j = view(K + 9472, NT, P)
        gate = view(K + 9728, NT * PEER_HEADS, PEER_K)
        gate_sum = view(K + 9984, NT * PEER_HEADS)
        peer_num = small[:, P:2 * P]
        dots = small[:, 0:BODY]
        gelu = small[:, BODY:2 * BODY]
        coef = small[:, 2 * BODY:3 * BODY]
        idx_ring = [small[:, 3 * BODY + 8 * s:3 * BODY + 8 * s + 8].bitcast(U32) for s in range(2)]
        BODIES = T // BODY
        SUB = BODY // 4
        CHUNKS = NKEYS // VI
        by_key = coef_all.rearrange("p t i -> p i t")

        def layer_of(stage):
            return int(stage[-1])
        block = ctx.enter_context(nc.Block())
        ADA = [(I["ada_w"][0], 0), (I["ada_w_2"][0], KC), (I["ada_w_2"][1], KC)]
        BIAS_AT = [(0, 64), (1, 0), (1, 48)]

        st_abs = [view(AT + MAPW * i, MAPW) for i in range(2)]
        st_exp = [view(AT + MAPW * (2 + i), MAPW) for i in range(2)]
        st_ln = [view(AT + MAPW * (4 + i), MAPW) for i in range(2)]
        st_keep = [view(AT + MAPW * (6 + i), MAPW) for i in range(2)]
        st_a = [view(AT + MAPW * (8 + i), MAPW) for i in range(2)]

        RB = AREA - REL_HEADS * MAPW - 4 * HEAD - 3
        rel_maps = view(RB, REL_HEADS, MAPW)
        lam_vec = view(RB + REL_HEADS * MAPW, 4, HEAD)
        kv_gain = view(RB + REL_HEADS * MAPW + 4 * HEAD, LATENT // P)
        subln_raw = view(RB + REL_HEADS * MAPW + 4 * HEAD + 2, 1)
        rel_heads, rel_near, rel_far = small[:, 0:REL_BUCKETS], peer_neg_i, peer_neg_j

        def map_q(m):
            lo = HEAD * (m % 2)
            return qkT[lo:lo + HEAD, m // 2, :], qkT[lo:lo + HEAD, MAPS // 2 + m // 2, :]

        def diag_blocks(t):
            return t.rearrange("p (b c) -> p b c", c=P)[:, 0:3:2, :]

        ROW_TURN = {"mix1": 1, "moe": 2, "even": 3, "peer0": 4, "odd": 5, "peer1": 6}

        X_PARTS = {"mix1": "tiles", "moe": "halves", "fin1": "tiles", "even": "tiles", "peer0": "halves", "odd": "tiles",
                   "peer1": "halves", "all": "tiles"}

        @block.sync
        def _(sp):
            def load_row(stage, vector):
                sp.wait_ge(x_done, x_updates(stage))
                sp.dma_start(row[:, :], vector.rearrange("(a n) -> a n", a=1).broadcast_to([P, D])).then_inc(row_loaded, 16)

            def load_piece(n):
                stage, i = ada_stage(n)
                ring = ada_ring[stage]
                if i >= len(ring):
                    sp.wait_ge(ada_used, n - len(ring) + 1)
                third = n // KC
                k = n % KC
                w = ADA[third // 3][0]
                sp.dma_start(ring[i % len(ring)], w[k * P:(k + 1) * P, third % 3 * THIRD:(third % 3 + 1) * THIRD]
                             ).then_inc(ada_loaded[i % len(ring)], 16)

            def load_mixer(stage, first, pieces):
                n = first
                for i, (j, g) in enumerate(groups_of(stage)):
                    load_group(j, g, i == 0)
                    for _ in range(pieces[i]):
                        load_piece(n)
                        n += 1

            def load_group(n, g, first):
                if first and n:
                    sp.wait_ge(x_done, x_updates(g["stage"]))
                if n >= 3:
                    sp.wait_ge(proj_done, n - 2)
                cols = g["w"].shape[1]
                nk = g["w"].shape[0] // P
                w = g["w"].rearrange("(k p) n -> p k n", p=P)
                slot = wring[n % 3]
                if g["kind"] == "I":
                    sp.dma_start(slot[:, 0:nk, 0:64], w[:, :, 0:64]).then_inc(w_loaded[n % 3], 16)
                    sp.dma_start(slot[:, 0:nk, 64:64 + cols], w).then_inc(w_loaded[n % 3], 16)
                else:
                    sp.dma_start(slot[:, 0:nk, 0:cols], w).then_inc(w_loaded[n % 3], 16)

            def load_stage(stage):
                for i, (n, g) in enumerate(groups_of(stage)):
                    load_group(n, g, i == 0)

            VECS = [(I["c"][0], 0, 0), (I["c_2"][0], 0, KC)] + [(gain, 0, KC * (2 + i)) for i, gain in enumerate(GAINS)]
            VECS += [(I["ada_b"][0], *BIAS_AT[0]), (I["ada_b_2"][0], *BIAS_AT[1]), (I["ada_b_2"][1], *BIAS_AT[2])]
            for vector, half, at in VECS:
                rows = vector.shape[0] // P
                sp.dma_start(vec_raw[at:at + rows, half, :], vector.rearrange("(k p) -> k p", p=P)).then_inc(vec_loaded, 16)
            sp.dma_start(rel_heads[0:REL_HEADS, :], I["rel_bias_2"].rearrange("b h -> h b"),
                          allow_slow_non_contiguous=True).then_inc(named("rel_heads_loaded"), 16)
            for n in range(KC):
                load_piece(n)
            sp.dma_start(x[:, :, :], I["x"][0].rearrange("(t p) d -> p t d", p=P)).then_inc(x_loaded, 16)
            load_mixer("mix1", KC, [3, 2, 3, 3, 3, 3, 3, 20])
            sp.wait_ge(named("rel_made"), 1)
            for part, cols in ((rel_near, slice(0, T)), (rel_far, slice(T, MAPW))):
                width = cols.stop - cols.start
                sp.dma_start(rel_rows_d[:, :, cols], part[0:REL_HEADS, 0:width].unsqueeze(1).broadcast_to([REL_HEADS, P, width])
                             ).then_inc(named("rel_stored"), 16)
            def load_expert(e, b, part):
                for i, w in ((0, I["moe_w_gate"]), (1, I["moe_w_up"]), (2, I["moe_w_down"])):
                    if part == i // 2:
                        src = w[0, bass.ds(e, 1)].rearrange("e (k p) f -> p (e k) f", p=P)
                        sp.dma_start(moe_w[b][i], src).then_inc(named(("gu_loaded", "down_loaded")[part] + str(b)), 16)

            def load_pass(p):
                with sp.Fori(1, PAIRS) as i:
                    for b in range(2):
                        sp.wait_ge(named("gu_done"), p * EXPERTS + 2 * i + (b - 1))
                        load_expert(2 * i + b, b, 0)
                        sp.wait_ge(named("y_done"), p * EXPERTS + 2 * i + (b - 1))
                        load_expert(2 * i + b, b, 1)

            def load_overflow(p):
                sp.wait_ge(named("comb_done"), p * (EXPERTS + 1))
                for b in range(2):
                    for part in range(2):
                        load_expert(b, b, part)
                load_pass(p)

            sp.wait_ge(av_out, MAPS)
            sp.wait_ge(ada_sums, EARLY // KC)
            load_expert(0, 0, 0)
            load_expert(0, 0, 1)
            load_expert(1, 1, 0)
            load_expert(1, 1, 1)
            sp.wait_ge(x_done, x_updates("moe"))
            with nc.allow_non_contiguous_dma(reason="a router's few columns"):
                sp.dma_start(route_w[:, :, 0:GROUPS], I["moe_w_grp"][0].rearrange("(k p) n -> p k n", p=P)
                             ).then_inc(named("route_loaded"), 16)
                sp.dma_start(route_w[:, :, GROUPS:], I["moe_w_exp"][0].rearrange("(k p) n -> p k n", p=P)
                             ).then_inc(named("route_loaded"), 16)
            sp.dma_start(route_b[0:1, 0:GROUPS], I["moe_b_grp"][0:1, :]).then_inc(named("route_loaded"), 16)
            sp.dma_start(route_b[0:1, GROUPS:], I["moe_b_exp"][0:1, :]).then_inc(named("route_loaded"), 16)
            load_pass(0)
            overflow(sp, load_overflow)
            load_row("fin1", I["final_g"])
            sp.wait_ge(x_done, x_updates("even"))
            sp.dma_start(lam_vec.rearrange("p a d -> p (a d)"), I["b_lambda_2"].rearrange("e a d -> e (a d)").broadcast_to([P, 4 * HEAD])
                         ).then_inc(named("even_vec_loaded"), 16)
            sp.dma_start(kv_gain, I["a_kv_norm_2"][0].rearrange("(k p) -> p k", p=P),
                         allow_slow_non_contiguous=True).then_inc(named("even_vec_loaded"), 16)
            sp.dma_start(subln_raw, I["b_subln_2"][0].rearrange("(p a) -> p a", a=1)).then_inc(named("even_vec_loaded"), 16)
            sp.wait_ge(named("rel_stored"), 32)
            rows = rel_rows_d.tensor
            sp.dma_start(rel_maps[:, :, P:MAPW], bass.AP(rows, P - 1, [[MAPW - 1, P], [P * MAPW, REL_HEADS], [1, T]])
                         ).then_inc(named("rel_loaded"), 16)
            sp.dma_start(rel_maps[:, :, 0:P], bass.AP(rows, 2 * P - 1, [[MAPW - 1, P], [P * MAPW, REL_HEADS], [1, P]])
                         ).then_inc(named("rel_loaded"), 16)
            load_mixer("even", EARLY, [0, 0, 3, 1, 1, 1, 1, 1, 1, 0, 15])
            def peer(stage):
                L = layer_of(stage)
                sp.wait_ge(x_done, x_updates(stage))
                sp.dma_start(keys_raw[:, :, :], I["peer_sub_keys_2"][L].rearrange("a n d -> n a d")).then_inc(named("keys_loaded"), 16)
                load_stage(stage)
                sp.wait_ge(named("parts_made"), L + 1)
                for q in range(8):
                    lo = 32 * (q % 4)
                    for n, part in enumerate((part_hi, part_mid, part_lo)):
                        sp.dma_start(h_parts[32 * n:32 * n + 32, q, :], part[lo:lo + 32, q // 4, :]).then_inc(named("h_parts_loaded"), 16)
                v = I["peer_v_2"][L].rearrange("(i j) d -> j i d", j=NKEYS)

                def load_v(c, s):
                    sp.dma_start(v_rows[s], v[:, bass.ds(c * VI, VI), :]).then_inc(named(f"v_loaded{s}"), 16)

                for s in range(2):
                    sp.wait_ge(named("dots_done"), T * (L + 1) + VI * (s + 1))
                    load_v(s, s)
                with sp.Fori(1, CHUNKS // 2) as m:
                    for s in range(2):
                        sp.wait_ge(named("v_split"), 2 * m + (L * CHUNKS + s - 1))
                        load_v(2 * m + s, s)

            peer("peer0")
            sp.wait_ge(x_done, x_updates("odd"))
            sp.dma_start(forget_col[0:C_HEADS, :], I["odd_b_forget_2"][0].rearrange("(h a) -> h a", a=1)).then_inc(named("forget_loaded"), 16)
            load_stage("odd")
            peer("peer1")
            load_row("all", I["norm_final_2"])
            sp.wait_ge(named("rel_stored"), 32)
            sp.wait_ge(x_done, x_updates("all") + 1)
            sp.dma_start(out[0].rearrange("(t p) d -> p t d", p=P), x[:, :, :]).then_inc(stored, 16)
            sp.wait_ge(stored, 16)

        @block.gpsimd
        def _(pool):
            step = stepper(pool, pool_step)
            step(pool.memset(ident[:, :], 0.0))
            step(pool.affine_select(out=ident[:, :], in_=ident[:, :], compare_op=ALU.not_equal, fill=1.0,
                                    base=0, pattern=[[-1, P]], channel_multiplier=1))
            pool.sem_inc(ident_made, 1)
            step(pool.memset(ones[:, :], 1.0))
            step(pool.memset(neg_ones[:, :], -1.0))
            step(pool.memset(zeros[:, :], 0.0))
            step(pool.memset(causal_add[:, :], 0.0))
            step(pool.iota(iota[:, :], [[1, P]], base=0, channel_multiplier=0, allow_small_or_imprecise_dtypes=True))
            step(pool.tensor_copy(iota_16[:, :], iota[:, 0:PEER_K]))
            step(pool.affine_select(out=before[:, :], in_=ones[:, :], compare_op=ALU.is_gt, fill=0.0,
                                    base=0, pattern=[[1, P]], channel_multiplier=-1))
            step(pool.affine_select(out=neg_tri[:, :], in_=neg_ones[:, :], compare_op=ALU.is_ge, fill=0.0,
                                    base=0, pattern=[[-1, P]], channel_multiplier=1))
            step(pool.affine_select(out=diag_blocks(causal_add[:, :]), in_=diag_blocks(causal_add[:, :]),
                                    compare_op=ALU.is_ge, fill=NEG, base=0, pattern=[[0, 2], [-1, P]],
                                    channel_multiplier=1))
            step(pool.memset(token_sel[:, :], 0.0))
            for quadrant in range(3):
                part = token_sel[:, :]
                step(pool.affine_select(out=part, in_=part, compare_op=ALU.not_equal, fill=1.0,
                                        base=-BODY * quadrant, pattern=[[-1, BODY]], channel_multiplier=1))
            pool.sem_inc(consts_made, 1)

            pool.wait_ge(named("rel_heads_loaded"), 16)
            step(pool.memset(rel_far[0:REL_HEADS, :], NEG))
            for b, first, last in rel_bucket_ranges():
                step(pool.tensor_copy(rel_near[0:REL_HEADS, T - 1 - last:T - first],
                                      rel_heads[0:REL_HEADS, b:b + 1].broadcast_to([REL_HEADS, last - first + 1])))
            pool.sem_inc(named("rel_made"), 1)

            for h in range(MAPS):
                pool.wait_ge(named("stick_exp"), h + 1)
                a = diag_blocks(st_a[h % 2])
                pool.affine_select(out=a, in_=a, compare_op=ALU.is_gt, fill=0.0, base=0,
                                   pattern=[[0, 2], [1, P]], channel_multiplier=-1).then_inc(named("stick_mask"), 1)
            pool.wait_ge(named("idx_summed"), IDX_HEADS)
            pool.affine_select(out=diag_blocks(idx_score), in_=diag_blocks(idx_score), compare_op=ALU.is_ge, fill=LOWEST,
                               base=0, pattern=[[0, 2], [-1, P]], channel_multiplier=1).then_inc(named("idx_causal"), 1)
            def peer(stage):
                L = layer_of(stage)
                u = I["peer_u_2"].rearrange("l e d -> (l e) d")
                pool.wait_ge(x_done, x_updates(stage))
                step(pool.memset(h_parts[96:128, :, :], 0.0))
                pool.sem_inc(named("h_parts_cleared"), 1)
                pool.wait_ge(named("h_parts_loaded"), 24 * 16 * (L + 1))
                for t in range(NT):
                    pool.wait_ge(named("experts_made"), NT * L + t + 1)
                    with pool.Fori(t * BODIES // NT, (t + 1) * BODIES // NT) as g:
                        for b in range(BODY // RING):
                            at = g * BODY + b * RING
                            pool.tensor_copy(idx_ring[b % 2], peer_e[:, bass.ds(at, RING)]).then_inc(named("idx_copied"), 1)
                            pool.wait_ge(named("idx_copied"), g * (BODY // RING) + (L * T // RING + b + 1))
                            for s in range(RING):
                                pool.wait_ge(named("dots_done"), at + (L * T + s + 1))
                                pool.sem_inc(named("gathers_begun"), 1)
                                pool.indirect_dma_start(u_rows[s], None, u, bass.IndirectOffsetOnAxis(ap=idx_ring[b % 2][:, s:s + 1], axis=0)
                                                        ).then_inc(named(f"u_loaded{s}"), 16)

            peer("peer0")
            peer("peer1")

        @block.scalar
        def _(act):
            step = stepper(act, act_step)

            def roots(stage):
                n = x_updates(stage)
                for i in range(2):
                    if n:
                        act.wait_ge(x_parts, 2 * (n - 1) + i + 1)
                    else:
                        act.wait_ge(x_loaded, 16)
                    if X_PARTS[stage] == "halves":
                        cols = slice(i * HALF, (i + 1) * HALF)
                        for t in range(NT):
                            last = act.activation(xn[:, t, cols], x[:, t, cols], ACT.Square, accum_out=ssq[:, i, t:t + 1])
                    else:
                        last = act.activation(xn[:, i, :], x[:, i, :], ACT.Square, accum_out=ssq[:, 0, i:i + 1])
                last.then_inc(ssq_done, 1)
                act.wait_ge(var_done, n + 1)
                act.activation(std[:, :], var[:, :], ACT.Sqrt).then_inc(std_done, 1)

            def norm(stage):
                roots(stage)
                n, a, v = NORM[stage]
                act.wait_ge(named("rstd_done"), x_updates(stage) + 1)
                act.activation(xn[:, 1, :], x[:, 1, :], ACT.Copy, scale=rstd[:, 1:2]).then_inc(xn_done[1], 1)
                act.wait_ge(named("a_cols_made"), n + 1)
                for half in range(2):
                    act.wait_ge(xt_done, 4 * n + half + 3)
                    for j in range(4):
                        k = 4 * half + j
                        last = act.activation(hT[:, k, P:T], ps[:, 2 + half, j * P:(j + 1) * P], ACT.Identity,
                                              bias=mod_cols[:, a, v, k:k + 1], scale=a_cols[:, k:k + 1])
                    last.then_inc(hT_done, 1)

            def take(n, g):
                if g["by"] != "act":
                    return
                act.wait_ge(proj_done, n + 1)
                b = 2 * (n % 2)
                cols = g["w"].shape[1]
                if g["kind"] == "F":
                    src = ps[:, b:b + 2, :].rearrange("p b (f t) -> p (b f) t", t=T)
                    act.activation(g["dst"], src, ACT.Copy, scale=g["scale"]).then_inc(proj_out, 1)
                elif g["kind"] == "T":
                    act.activation(g["dst"], ps[:, b:b + 2, 0:cols], ACT.Copy, scale=g["scale"]).then_inc(proj_out, 1)
                else:
                    step(act.activation(kidx[:, :], ps[:, b, 0:T], ACT.Copy))
                    act.activation(widx[:, :, :], ps[:, b + 1, 0:16].rearrange("p (t h) -> p t h", t=NT), ACT.Copy,
                                   scale=IDX_HEADS ** -0.5).then_inc(proj_out, 1)

            def take_av(h, n):
                act.wait_ge(av_done, n + 1)
                lo = HEAD * (h % 2)
                act.activation(oT[lo:lo + HEAD, h // 2, :], ps[lo:lo + HEAD, 6, 0:T],
                               ACT.Copy).then_inc(av_out, 1)

            def take_row(stage, bank):
                act.wait_ge(named("row_made"), ROW_TURN[stage])
                act.activation(row[:, :], ps[:, bank:bank + 2, :].rearrange("p b n -> p (b n)"), ACT.Copy).then_inc(row_loaded, 16)

            act.wait_ge(named("vec_turned"), 1)
            act.activation(c_silu[:, :], ps[:, 5, 0:2 * KC], ACT.Silu).then_inc(c_ready, 1)
            act.activation(vec_cols[:, 0, :], ps[:, 5, 0:112], ACT.Copy)
            act.activation(vec_cols[:, 1, 0:96], ps[:, 5, P:P + 96], ACT.Copy).then_inc(named("vec_ready"), 1)

            norm("mix1")
            for n, g in groups_of("mix1"):
                take(n, g)

            def stick_small(pair):
                for h in (2 * pair, 2 * pair + 1):
                    act.wait_ge(score_done, h + 1)
                    step(act.activation(st_abs[h % 2], ps[:, h % 4, 0:MAPW], ACT.Abs))
                    step(act.activation(st_exp[h % 2], st_abs[h % 2], ACT.Exp, scale=-1.0))

            def stick_log(pair):
                for h in (2 * pair, 2 * pair + 1):
                    if h >= 2:
                        act.wait_ge(named("stick_kept"), h - 1)
                    act.activation(st_ln[h % 2], st_exp[h % 2], ACT.Ln, bias=1.0).then_inc(named("stick_ln"), 1)

            def stick_weight(pair):
                for h in (2 * pair, 2 * pair + 1):
                    act.wait_ge(named("stick_sum"), h + 1)
                    if h >= 2:
                        act.wait_ge(av_done, h - 1)
                    act.activation(st_a[h % 2], ps[:, h % 4, 0:MAPW], ACT.Exp).then_inc(named("stick_exp"), 1)

            for i in range(MAPS // 2 + 2):
                if i < MAPS // 2:
                    stick_small(i)
                if 1 <= i <= MAPS // 2:
                    stick_weight(i - 1)
                if i < MAPS // 2:
                    stick_log(i)
                if i >= 2:
                    for h in (2 * i - 4, 2 * i - 3):
                        take_av(h, h)
            take_row("mix1", 4)
            def moe_pass(p):
                def take_xe(j, buf):
                    act.wait_ge(named("xe_psum"), p * SENT + j + 1)
                    act.activation(xe[buf].rearrange("p k s -> p (k s)"), ps[:, 4:6, :].rearrange("p b n -> p (b n)"),
                                   ACT.Copy).then_inc(named("xe_ready"), 1)

                take_xe(0, 0)
                with act.Fori(0, PAIRS // 2) as i:
                    for h in range(2):
                        for b in range(2):
                            act.wait_ge(named("gu_done"), p * EXPERTS + 4 * i + (2 * h + b + 1))
                            act.activation(silu_g[b], ps[:, 6 + b, 0:FF // 2], ACT.Silu).then_inc(named("silu_done"), 1)
                            if b == 0:
                                take_xe(2 * i + (h + 1), 1 - h)
                        for b in range(2):
                            act.wait_ge(named("y_done"), p * EXPERTS + 4 * i + (2 * h + b + 1))
                            act.activation(y_e[b], ps[:, 6 + b, :], ACT.Copy).then_inc(named("y_ready"), 1)

            norm("moe")
            take_row("moe", 6)
            for b in range(4):
                act.wait_ge(named("ht_psum"), b + 1)
                act.activation(h_tok[:, b // 2, (b % 2) * HALF:(b % 2 + 1) * HALF], ps[:, b, :],
                               ACT.Copy).then_inc(named("h_tok_ready"), 1)
            act.sem_inc(named("y_ready"), 2)
            act.wait_ge(named("grp_neg_made"), 1)
            for t in range(NT):
                act.activation(grp_exp[:, t, :], grp_logit[:, t, 0:GROUPS], ACT.Exp, bias=grp_neg[:, t:t + 1],
                               accum_out=grp_sum[:, t:t + 1]).then_inc(named("grp_exp_done"), 1)
            act.wait_ge(named("in_neg_made"), 1)
            for t in range(NT):
                act.activation(in_exp[:, t:t + 1], in_top[:, t, 1:2], ACT.Exp,
                               bias=in_neg[:, t:t + 1]).then_inc(named("in_exp_done"), 1)
            moe_pass(0)
            overflow(act, moe_pass)
            roots("fin1")
            def softmax_attention(stage):
                maps = SOFTMAX[stage]

                def exps(i):
                    d = maps[i]
                    act.wait_ge(named("max_made"), d["n"] + 1)
                    if i >= 2:
                        if maps[i - 2]["kind"] == "first":
                            act.wait_ge(named("probs_ready"), maps[i - 2]["turn"] + 1)
                        else:
                            act.wait_ge(named("probs_turned"), maps[i - 2]["turn"] + 1)
                    b = i % 2
                    for t in range(NT):
                        act.activation(both_tiles(sm_p[b], t), both_tiles(sm_s[b], t), ACT.Exp, bias=sm_max[b][:, t:t + 1],
                                       accum_out=sm_sum[b][:, t:t + 1]).then_inc(named("exp_done"), 1)

                def take_turned(d, before_last):
                    act.wait_ge(named("probs_turned"), d["turn"] + 1)
                    if before_last:
                        wait_read(act, before_last)
                    act.activation(sm_pT[d["turn"] % 2], ps[:, d["turn"] % 2, 0:MAPW], ACT.Copy).then_inc(named("turned_out"), 1)

                turned = [d for d in maps if d["kind"] != "first"]
                for i in range(MAPS + 2):
                    if i < MAPS:
                        exps(i)
                    if 1 <= i <= MAPS and maps[i - 1]["kind"] != "first":
                        j = turned.index(maps[i - 1])
                        take_turned(maps[i - 1], turned[j - 2] if j >= 2 else None)
                    if i >= 2 and maps[i - 2]["kind"] == "head":
                        take_av(maps[i - 2]["m"], maps[i - 2]["av"])

            norm("even")
            take_row("even", 4)
            even = groups_of("even")
            take(*even[0])
            act.wait_ge(proj_out, even[0][0] + 1)
            for t in range(NT):
                act.activation(idx_relu[t][:, 0:LATENT], ckv_tok[:, t, :], ACT.Square,
                               accum_out=kv_ssq[:, t:t + 1]).then_inc(named("kv_ssq_done"), 1)
            act.wait_ge(named("kv_var_done"), 1)
            act.activation(kv_std, kv_std, ACT.Sqrt).then_inc(named("kv_std_done"), 1)
            take(*even[1])
            take(*even[2])
            act.wait_ge(named("lam_sum_made"), 1)
            act.activation(lam_exp, lam_sum, ACT.Exp).then_inc(named("lam_exp_done"), 1)

            def idx_relus(h):
                act.wait_ge(score_done, MAPS + h + 1)
                if h >= 2:
                    act.wait_ge(named("idx_summed"), h - 1)
                act.activation(idx_relu[h % 2], ps[:, 4 + h % 2, 0:MAPW], ACT.Relu, scale=HEAD ** -0.5).then_inc(named("idx_relu_done"), 1)

            act.wait_ge(named("kv_scaled"), 1)
            for i in range(4):
                idx_relus(2 * i)
                idx_relus(2 * i + 1)
                take(*even[3 + i])
            for n, g in even[7:9]:
                take(n, g)
            softmax_attention("even")
            act.wait_ge(named("diff_av"), DIFF_HEADS)
            act.wait_ge(ada_sums, 8)
            act.activation(diff_sq.rearrange("p h t -> p (h t)"), ps[:, 2:4, :].rearrange("p b n -> p (b n)"),
                           ACT.Square).then_inc(named("diff_sq_done"), 1)
            act.wait_ge(named("diff_var_done"), 1)
            act.activation(diff_std[:, :, :], diff_std[:, :, :], ACT.Sqrt).then_inc(named("diff_std_done"), 1)
            def peer(stage):
                L = layer_of(stage)
                norm(stage)
                take_row(stage, 6)
                for b in range(4):
                    act.wait_ge(named("ht_psum"), 4 * (L + 1) + b + 1)
                    act.activation(h_tok[:, b // 2, (b % 2) * HALF:(b % 2 + 1) * HALF], ps[:, b, :],
                                   ACT.Copy).then_inc(named("h_tok_ready"), 1)
                act.wait_ge(named("keys_psum"), L + 1)
                act.activation(keysT.rearrange("p a n -> p (a n)"), ps[:, 4, 0:2 * P], ACT.Copy).then_inc(named("keysT_ready"), 1)

                def copy_keys(i):
                    act.wait_ge(named("key_scored"), 4 * L + i + 1)
                    act.activation(key_score[:, GQ * i:GQ * (i + 1), :].rearrange("p q n -> p (q n)"), ps[:, 6 + i % 2, :],
                                   ACT.Copy).then_inc(named("keys_copied"), 1)

                def exp_gates(t):
                    heads = slice(t * PEER_HEADS, (t + 1) * PEER_HEADS)
                    act.wait_ge(named("gate_diff"), NT * L + t + 1)
                    act.activation(gate[:, heads, :], gate[:, heads, :], ACT.Exp).then_inc(named("gate_exp"), 1)

                for i, (n, g) in enumerate(groups_of(stage)):
                    take(n, g)
                    if i >= 1:
                        copy_keys(i - 1)
                copy_keys(3)
                exp_gates(0)

                def take_coef(g, m):
                    act.wait_ge(named("spread_done"), g * SUB + (2 + L * T // 4 + m + 1))
                    act.sem_inc(named("coef_begun"), 1)
                    act.activation(coef_all[:, bass.ds(g * BODY + 4 * m, 4), :], ps[:, 4 + m % 2, :].rearrange("p (t i) -> p t i", i=P),
                                   ACT.Copy).then_inc(named("coef_out"), 1)

                def key_hots(g, m):
                    n = g * SUB + (L * T // 4 + m + 1)
                    act.wait_ge(named("spread_done"), n)
                    act.sem_inc(named("hots_begun"), 1)
                    for j in range(8):
                        key = (peer_neg_i, peer_neg_j)[j // 4]
                        last = act.activation(hots[m % 2][:, j, :], iota[:, :], ACT.Abs,
                                              bias=key[:, bass.ds(g * BODY + 4 * m + j % 4, 1)])
                    last.then_inc(named("hots_apart"), 1)
                    act.wait_ge(named("hots_apart"), n)
                    act.activation(hots[m % 2], hots[m % 2], ACT.Relu, scale=-1.0, bias=1.0).then_inc(named("hots_made"), 1)

                def coefs_of_body(g, first=False):
                    for b in range(BODY // RING):
                        for m in (2 * b - 3, 2 * b - 2):
                            if m >= 0 or not first:
                                take_coef(g, m)
                        act.wait_ge(named("dots_done"), g * BODY + (RING + L * T + (b + 1) * RING))
                        cols = slice(b * RING, (b + 1) * RING)
                        act.activation(gelu[:, cols], dots[:, cols], ACT.Gelu_apprx_tanh).then_inc(named("gelu_done"), 1)
                        for m in range(2 * b, 2 * b + 2):
                            key_hots(g, m)

                coefs_of_body(0, first=True)
                coefs_of_body(1)
                exp_gates(1)
                with act.Fori(2, BODIES) as g:
                    coefs_of_body(g)
                for m in range(SUB - 3, SUB):
                    take_coef(BODIES - 1, m)

                act.wait_ge(named("coef_out"), 2 + T // 4 * (L + 1))
                act.wait_ge(named("spread_done"), 2 + T // 4 * (L + 1))
                act.wait_ge(named("dots_done"), RING + T * (L + 1))

                def take_high(m, s):
                    act.activation(coef_high[s], by_key[:, bass.ds((2 * m + s) * VI, VI), :], ACT.Copy).then_inc(named("coef_high_made"), 1)
                    act.wait_ge(named(f"v_loaded{s}"), m * 16 + (L * CHUNKS // 2 + 1) * 16)
                    act.activation(v_high[s], v_rows[s], ACT.Copy).then_inc(named("v_high_made"), 1)

                for s in range(2):
                    take_high(0, s)
                with act.Fori(1, CHUNKS // 2) as m:
                    for s in range(2):
                        act.wait_ge(named("v_used"), 2 * m + (L * CHUNKS + s - 1))
                        act.sem_inc(named("high_begun"), 1)
                        take_high(m, s)

            act.sem_inc(named("coef_out"), 2)
            peer("peer0")
            norm("odd")
            take_row("odd", 4)
            act.wait_ge(named("f_made"), 1)
            step(act.activation(f_abs[0:C_HEADS, :], f_logit[0:C_HEADS, :], ACT.Abs))
            step(act.activation(f_log[0:C_HEADS, :], f_abs[0:C_HEADS, :], ACT.Exp, scale=-1.0))
            act.activation(f_log[0:C_HEADS, :], f_log[0:C_HEADS, :], ACT.Ln, bias=1.0).then_inc(named("f_log_done"), 1)
            for n, g in groups_of("odd"):
                take(n, g)
            softmax_attention("odd")
            peer("peer1")
            roots("all")

        @block.tensor
        def _(pe):
            def project(n, g, between=None):
                pe.wait_ge(w_loaded[n % 3], w_turns(n))
                if n >= 2:
                    pe.wait_ge(proj_out, n - 1)
                w = wring[n % 3]
                nk = g["w"].shape[0] // P
                cols = g["w"].shape[1]
                b = 2 * (n % 2)
                src = g["src"]
                if g["kind"] == "F":
                    for f in range(cols // P):
                        for k in range(nk):
                            last = pe.matmul(ps[:, b + f // 2, (f % 2) * T:(f % 2 + 1) * T], w[:, k, f * P:(f + 1) * P],
                                             src[:, k, :], start=(k == 0), stop=(k == nk - 1))
                        if f == 0 and between:
                            between()
                elif g["kind"] == "T":
                    for t in range(NT):
                        for k in range(nk):
                            last = pe.matmul(ps[:, b + t, 0:cols], src[:, k, t * P:(t + 1) * P], w[:, k, 0:cols],
                                             start=(k == 0), stop=(k == nk - 1))
                elif g["kind"] == "I":
                    for k in range(nk):
                        pe.matmul(ps[:, b, 0:T], w[:, k, 0:P], src[:, k, :], start=(k == 0), stop=(k == nk - 1))
                    for t in range(NT):
                        for k in range(nk):
                            last = pe.matmul(ps[:, b + 1, t * 8:(t + 1) * 8], src[:, k, t * P:(t + 1) * P], w[:, k, P:P + 8],
                                             start=(k == 0), stop=(k == nk - 1))
                else:
                    for k in range(nk):
                        last = pe.matmul(ps[0:cols, b, 0:T], w[:, k, 0:cols], src[:, k, :],
                                         start=(k == 0), stop=(k == nk - 1))
                last.then_inc(proj_done, 1)

            def transpose_norm(stage):
                n = NORM[stage][0]
                for b in range(4):
                    t, half = b // 2, b % 2
                    pe.wait_ge(xn_done[t], n + 1)
                    for k in range(4):
                        last = pe.transpose(ps[:, b, k * P:(k + 1) * P], xn[:, t, (4 * half + k) * P:(4 * half + k + 1) * P],
                                            ident[:, :])
                    last.then_inc(xt_done, 1)
                pe.wait_ge(hT_done, 4 * (n + 1))

            def values(h, n, pT):
                if n >= 2:
                    pe.wait_ge(av_out, n - 1)
                lo = HEAD * (h % 2)
                o = ps[lo:lo + HEAD, 6, 0:T]
                pe.matmul(o, v_tok[:, 0, h * HEAD:(h + 1) * HEAD], pT[:, 0:T], start=True, stop=False, skip_group_check=True)
                pe.matmul(ps[lo:lo + HEAD, 6, P:T], v_tok[:, 1, h * HEAD:(h + 1) * HEAD], pT[:, T:MAPW],
                          start=False, stop=True, skip_group_check=True).then_inc(av_done, 1)

            def sum_third(n):
                stage, i = ada_stage(n * KC)
                pe.wait_ge(ada_used, KC * (n + 1))
                if n:
                    pe.wait_ge(mod_made, n)
                for j in range(THIRD // P):
                    last = pe.matmul(ps[:, 7, j:j + 1], ada_acc[stage][n % 2][:, j * P:(j + 1) * P],
                                     ones[:, 0:1], start=True, stop=True)
                last.then_inc(ada_sums, 1)

            def make_row(stage, bank):
                _, a, v = NORM[stage]
                v += 2
                pe.wait_ge(mod_made, 3 * a + v // 2 + 1)
                for k in range(KC):
                    last = pe.matmul(ps[:, bank + k // 4, k % 4 * P:(k % 4 + 1) * P], mod_cols[:, a, v, k:k + 1].broadcast_to([P, P]),
                                     ident[:, :], start=True, stop=True)
                last.then_inc(named("row_made"), 1)

            pe.wait_ge(ident_made, 1)
            pe.wait_ge(vec_loaded, 16 * 11)
            pe.transpose(ps[:, 5, 0:112], vec_raw[0:112, 0, :], ident[0:112, 0:112])
            pe.transpose(ps[:, 5, P:P + 96], vec_raw[0:96, 1, :], ident[0:96, 0:96]).then_inc(named("vec_turned"), 1)
            pe.wait_ge(consts_made, 1)
            sum_third(0)

            transpose_norm("mix1")
            for i, (n, g) in enumerate(groups_of("mix1")[:-2]):
                project(n, g)
                if i == 3:
                    sum_third(1)
            sum_third(2)
            pe.wait_ge(proj_out, 6)

            def stick_scores(h):
                if h >= 4:
                    pe.wait_ge(named("stick_exp"), h - 3)
                q, k = map_q(h)
                z = ps[:, h % 4, :]
                pe.matmul(z[:, 0:T], k[:, 0:P], q, start=True, stop=False, skip_group_check=True)
                pe.matmul(z[:, T:MAPW], k[:, P:T], q[:, P:T], start=False, stop=True,
                          skip_group_check=True).then_inc(score_done, 1)

            def stick_sums(h):
                pe.wait_ge(named("stick_kept"), h + 1)
                z = ps[:, h % 4, :]
                keep = st_keep[h % 2]
                pe.matmul(z[:, 0:T], neg_tri[:, :], keep[:, 0:T], start=False, stop=False, skip_group_check=True)
                pe.matmul(z[:, P:T], neg_ones[:, :], keep[:, T:MAPW], start=False, stop=False, skip_group_check=True)
                pe.matmul(z[:, T:MAPW], neg_tri[:, :], keep[:, T:MAPW], start=False, stop=True,
                          skip_group_check=True).then_inc(named("stick_sum"), 1)

            for i in range(MAPS // 2 + 2):
                for side in range(2):
                    if i < MAPS // 2:
                        stick_scores(2 * i + side)
                for side in range(2):
                    if 1 <= i <= MAPS // 2:
                        stick_sums(2 * (i - 1) + side)
                for side in range(2):
                    if i >= 2:
                        h = 2 * (i - 2) + side
                        pe.wait_ge(named("stick_mask"), h + 1)
                        values(h, h, st_a[h % 2])
                if i in (2, 5):
                    sum_third(3 + i // 5)
            sum_third(5)
            pe.wait_ge(named("stick_exp"), MAPS)
            make_row("mix1", 4)
            pe.wait_ge(av_out, MAPS)
            for n, g in groups_of("mix1")[-2:]:
                project(n, g)
            def moe_pass(p):
                def dispatch(j, first=False):
                    pe.wait_ge(named("disp_made"), p * PLACED + j + 1)
                    if not first:
                        pe.wait_ge(named("operands_out"), p * EXPERTS + 2 * j - 1)
                    for k in range(KC):
                        for t in range(NT):
                            last = pe.matmul(ps[:, 4 + k // 4, k % 4 * P:(k % 4 + 1) * P], h_tok[:, t, k * P:(k + 1) * P],
                                             disp[:, t, :], start=(t == 0), stop=(t == NT - 1))
                    last.then_inc(named("xe_psum"), 1)

                with_pass = p * EXPERTS

                def gate_up(i, h, b):
                    pe.wait_ge(named(f"gu_loaded{b}"), p * (PAIRS * 32) + 64 * i + 32 * (h + 1))
                    pe.wait_ge(named("xe_ready"), p * SENT + 2 * i + (h + 1))
                    pe.wait_ge(named("y_ready"), with_pass + 4 * i + (2 * h + b + 1))
                    for m in range(2):
                        for k in range(KC):
                            for half in range(2):
                                last = pe.matmul(ps[SLOTS * half:SLOTS * (half + 1), 6 + b, m * FF // 2:(m + 1) * FF // 2],
                                                 xe[h][:, k, SLOTS * b:SLOTS * (b + 1)],
                                                 moe_w[b][m][:, k, half * FF // 2:(half + 1) * FF // 2],
                                                 start=(k == 0), stop=(k == KC - 1), skip_group_check=True)
                    last.then_inc(named("gu_done"), 1)

                def turn_places(i, h, b):
                    pe.wait_ge(named("comb_made"), with_pass + 4 * i + (2 * h + b + 1))
                    pe.wait_ge(named("xe_ready"), p * SENT + 2 * i + (h + 2))
                    for t in range(NT):
                        pe.transpose(ps[:, 4 + b, (2 + t) * P:(3 + t) * P], comb[b][:, t, :], ident[:, :])

                def turn_act(i, h, b):
                    pe.wait_ge(named("act_done"), with_pass + 4 * i + (2 * h + b + 1))
                    for c in range(2):
                        last = pe.transpose(ps[:, 4 + b, c * P:(c + 1) * P], act_e[b][:, c * P:(c + 1) * P], ident[:, :])
                    last.then_inc(named("operands_made"), 1)

                def down(i, h, b):
                    pe.wait_ge(named(f"down_loaded{b}"), p * (PAIRS * 16) + 32 * i + 16 * (h + 1))
                    pe.wait_ge(named("operands_out"), with_pass + 4 * i + (2 * h + b + 2))
                    for f in range(FF // P):
                        for half in range(2):
                            last = pe.matmul(ps[SLOTS * half:SLOTS * (half + 1), 6 + b, :],
                                             turned[b][:, f % 2, SLOTS * (f // 2):SLOTS * (f // 2 + 1)],
                                             moe_w[b][2][:, f, half * HALF:(half + 1) * HALF],
                                             start=(f == 0), stop=(f == FF // P - 1), skip_group_check=True)
                    last.then_inc(named("y_done"), 1)

                def combine(b, ready):
                    pe.wait_ge(named("y_ready"), ready)
                    for t in range(NT):
                        for half in range(2):
                            rows = slice(SLOTS * half, SLOTS * (half + 1))
                            last = pe.matmul(ps[:, 2 * t + half, :], turned[b][rows, 2 + t, :], y_e[b][rows, :],
                                             start=False, stop=True, skip_group_check=True)
                    last.then_inc(named("comb_done"), 1)

                dispatch(0, first=True)
                with pe.Fori(0, PAIRS // 2) as i:
                    for h in range(2):
                        gate_up(i, h, 0)
                        dispatch(2 * i + (h + 1))
                        combine(1, with_pass + 4 * i + (2 * h + 2))
                        gate_up(i, h, 1)
                        turn_places(i, h, 0)
                        turn_act(i, h, 0)
                        turn_places(i, h, 1)
                        turn_act(i, h, 1)
                        down(i, h, 0)
                        down(i, h, 1)
                        combine(0, with_pass + 4 * i + (2 * h + 3))
                combine(1, with_pass + (EXPERTS + 2))

            transpose_norm("moe")
            make_row("moe", 6)
            for b in range(4):
                for k in range(4):
                    last = pe.transpose(ps[:, b, k * P:(k + 1) * P], hT[:, 4 * (b % 2) + k, (b // 2) * P:(b // 2 + 1) * P],
                                        ident[:, :])
                last.then_inc(named("ht_psum"), 1)
            pe.wait_ge(named("route_loaded"), 64)
            for t in range(NT):
                o = ps[:, 4, t * 64:t * 64 + GROUPS + EXPERTS]
                for k in range(KC):
                    pe.matmul(o, hT[:, k, t * P:(t + 1) * P], route_w[:, k, :], start=(k == 0), stop=False)
                last = pe.matmul(o, ones[0:1, :], route_b[0:1, :], start=False, stop=True)
            last.then_inc(named("logits_done"), 1)
            pe.wait_ge(named("h_tok_ready"), 4)
            for b in range(4):
                pe.matmul(ps[:, b, :], zeros[:, :], x[:, 0, 0:HALF], start=True, stop=False, skip_group_check=True)
            pe.wait_ge(named("chosen_made"), 1)
            pe.matmul(ps[:, 5, 0:EXPERTS], before[:, :], chosen[:, 0, :], start=True, stop=True)
            pe.matmul(ps[:, 5, 64:64 + EXPERTS], ones[:, :], chosen[:, 0, :], start=True, stop=False)
            pe.matmul(ps[:, 5, 64:64 + EXPERTS], before[:, :], chosen[:, 1, :], start=False, stop=True)
            pe.matmul(ps[:, 5, 128:128 + EXPERTS], ones[:, :], chosen[:, 0, :], start=True, stop=False)
            pe.matmul(ps[:, 5, 128:128 + EXPERTS], ones[:, :], chosen[:, 1, :], start=False, stop=True
                      ).then_inc(named("ranks_done"), 1)
            pe.wait_ge(named("rank_made"), 1)
            moe_pass(0)
            overflow(pe, moe_pass)
            pe.matmul(ps[:, 0, :], zeros[:, :], x[:, 0, 0:HALF], start=False, stop=True,
                      skip_group_check=True).then_inc(named("moe_combined"), 1)
            def softmax_attention(stage):
                maps = SOFTMAX[stage]

                def scores(i):
                    d = maps[i]
                    if i >= 2:
                        pe.wait_ge(score_read, d["n"] - 1)
                    q, k = map_q(d["m"])
                    z = ps[:, 4 + i % 2, :]
                    forget = stage == "odd"
                    pe.matmul(z[:, 0:P], q[:, 0:P], k[:, 0:P], start=True, stop=False, skip_group_check=True)
                    last = pe.matmul(z[:, P:MAPW], q[:, P:T], k[:, 0:T], start=False, stop=not forget, skip_group_check=True)
                    if forget:
                        pick = neg_ident[0:C_HEADS, d["m"]:d["m"] + 1].broadcast_to([C_HEADS, P])
                        pe.matmul(z[:, 0:P], pick, f_cum[0:C_HEADS, 0:P], start=False, stop=False, skip_group_check=True)
                        last = pe.matmul(z[:, P:MAPW], pick, f_cum[0:C_HEADS, :], start=False, stop=True, skip_group_check=True)
                    last.then_inc(score_done, 1)

                def turn(d, before_last):
                    pe.wait_ge(named("probs_ready"), d["turn"] + 1)
                    if before_last:
                        pe.wait_ge(named("turned_out"), before_last["turn"] + 1)
                    p = sm_p[d["m"] % 2]
                    for c in range(3):
                        last = pe.transpose(ps[:, d["turn"] % 2, c * P:(c + 1) * P], p[:, c * P:(c + 1) * P], ident[:, :])
                    last.then_inc(named("probs_turned"), 1)

                def weigh(d):
                    pe.wait_ge(named("turned_out"), d["turn"] + 1)
                    pT = sm_pT[d["turn"] % 2]
                    if d["kind"] == "head":
                        values(d["m"], d["av"], pT)
                        return
                    v = v_tok[:, :, DSA_HEADS * HEAD + 2 * HEAD * d["hb"]:DSA_HEADS * HEAD + 2 * HEAD * (d["hb"] + 1)]
                    o = ps[:, 2 + d["hb"] // 2, (d["hb"] % 2) * T:(d["hb"] % 2 + 1) * T]
                    pe.matmul(o, v[:, 0, :], pT[:, 0:T], start=True, stop=False, skip_group_check=True)
                    pe.matmul(o[:, P:T], v[:, 1, :], pT[:, T:MAPW], start=False, stop=True,
                              skip_group_check=True).then_inc(named("diff_av"), 1)

                turned = [d for d in maps if d["kind"] != "first"]
                for i in range(MAPS + 2):
                    if i < MAPS:
                        scores(i)
                    if 1 <= i <= MAPS and maps[i - 1]["kind"] != "first":
                        j = turned.index(maps[i - 1])
                        turn(maps[i - 1], turned[j - 2] if j >= 2 else None)
                    if i >= 2 and maps[i - 2]["kind"] != "first":
                        weigh(maps[i - 2])
                    if stage == "even" and i == 10:
                        sum_third(7)

            transpose_norm("even")
            make_row("even", 4)
            even = groups_of("even")
            project(*even[0])
            project(*even[1])
            project(*even[2])
            pe.wait_ge(named("kv_scaled"), 1)
            for c in range(LATENT // P):
                for t in range(NT):
                    last = pe.transpose(ps[:, 6, c * T + t * P:c * T + (t + 1) * P], ckv_tok[:, t, c * P:(c + 1) * P], ident[:, :])
            last.then_inc(named("kv_turned"), 1)

            def idx_scores(h):
                if h >= 2:
                    pe.wait_ge(named("idx_relu_done"), h - 1)
                lo = HEAD * (h % 2)
                q, k = qidx[lo:lo + HEAD, h // 2, :], kidx[lo:lo + HEAD, :]
                z = ps[:, 4 + h % 2, :]
                pe.matmul(z[:, 0:P], q[:, 0:P], k[:, 0:P], start=True, stop=False, skip_group_check=True)
                pe.matmul(z[:, P:MAPW], q[:, P:T], k[:, 0:T], start=False, stop=True, skip_group_check=True).then_inc(score_done, 1)

            pe.wait_ge(proj_out, even[2][0] + 1)
            for i in range(4):
                idx_scores(2 * i)
                idx_scores(2 * i + 1)
                project(*even[3 + i])
            sum_third(6)
            pe.wait_ge(named("ckvT_ready"), 1)
            project(*even[7])
            project(*even[8])
            pe.wait_ge(proj_out, even[8][0] + 1)
            pe.wait_ge(named("idx_relu_done"), IDX_HEADS)
            softmax_attention("even")
            sum_third(8)
            pe.wait_ge(named("diff_sq_done"), 1)
            pe.wait_ge(score_read, MAPS)
            for half in range(2):
                last = pe.matmul(ps[:, 4 + half, :], ones[:, :], diff_sq[:, 2 * half:2 * half + 2, :].rearrange("p h t -> p (h t)"),
                                 start=True, stop=True)
            last.then_inc(named("diff_summed"), 1)
            pe.wait_ge(named("diff_out"), 1)
            pe.wait_ge(av_out, MAPS + DSA_HEADS)
            for n, g in even[-2:]:
                project(n, g)
            def peer(stage):
                L = layer_of(stage)
                transpose_norm(stage)
                make_row(stage, 6)
                for b in range(4):
                    for k in range(4):
                        last = pe.transpose(ps[:, b, k * P:(k + 1) * P], hT[:, 4 * (b % 2) + k, (b // 2) * P:(b // 2 + 1) * P],
                                            ident[:, :])
                    last.then_inc(named("ht_psum"), 1)
                pe.wait_ge(named("keys_loaded"), 16 * (L + 1))
                for a in range(2):
                    last = pe.transpose(ps[:, 4, a * P:(a + 1) * P], keys_raw[:, a, :], ident[:, :])
                last.then_inc(named("keys_psum"), 1)
                pe.wait_ge(named("h_tok_ready"), 4 * (L + 2))
                pe.wait_ge(named("keysT_ready"), L + 1)

                def key_scores(i):
                    pe.wait_ge(proj_out, groups_of(stage)[i][0] + 1)
                    if i >= 2:
                        pe.wait_ge(named("keys_read"), 4 * L + i - 1)
                        pe.wait_ge(named("keys_copied"), 4 * L + i - 1)
                    for t in range(NT):
                        for j in range(GQ):
                            q = GQ * i + j
                            last = pe.matmul(ps[:, 4 + 2 * t + i % 2, j * P:(j + 1) * P], qkT[:, q, t * P:(t + 1) * P],
                                             keysT[:, q % 2, :], start=True, stop=True)
                    last.then_inc(named("key_scored"), 1)

                def turn_picks(t):
                    pe.wait_ge(named("picks_made"), NT * L + t + 1)
                    for n, pick in enumerate((pick_i[:, t, :], pick_j[:, t, :],
                                              gate[:, t * PEER_HEADS:(t + 1) * PEER_HEADS, :].rearrange("p h k -> p (h k)"))):
                        last = pe.transpose(ps[:, 6, n * P:(n + 1) * P], pick, ident[:, :])
                    last.then_inc(named("picks_psum"), 1)

                for i, (n, g) in enumerate(groups_of(stage)):
                    project(n, g, (lambda: key_scores(i - 1)) if i else None)
                key_scores(3)
                pe.wait_ge(named("keys_copied"), 4 * (L + 1))
                turn_picks(0)
                pe.wait_ge(named("h_parts_loaded"), 24 * 16 * (L + 1))
                pe.wait_ge(named("h_parts_cleared"), L + 1)
                pe.wait_ge(named("experts_made"), NT * L + 1)

                def spread(g, m):
                    pe.wait_ge(named("hots_weighed"), g * SUB + (L * T // 4 + m + 1))
                    pe.wait_ge(named("coef_out"), g * SUB + (L * T // 4 + m + 1))
                    for j in range(4):
                        last = pe.matmul(ps[:, 4 + m % 2, j * P:(j + 1) * P], hot_j[m % 2][:, j, :], hot_i[m % 2][:, j, :],
                                         start=True, stop=True)
                    last.then_inc(named("spread_done"), 1)

                def rows_of_body(g, first=False):
                    for i in range(BODY):
                        b, s = i // RING, i % RING
                        pe.wait_ge(named("dots_done"), g * BODY + (L * T + i + RING - 1))
                        for half in range(2):
                            last = pe.matmul(ps[:, 2 * (i % 2) + half, :], token_sel[:, i:i + 1].broadcast_to([P, P]),
                                             h_parts[:, bass.ds(g, 1), half * HALF:(half + 1) * HALF].rearrange("p g n -> p (g n)"),
                                             start=True, stop=True)
                        last.then_inc(named("row_spread"), 1)
                        m = {1: 2 * b - 3, 5: 2 * b - 2}.get(s)
                        if m is not None and (m >= 0 or not first):
                            spread(g, m)

                rows_of_body(0, first=True)
                with pe.Fori(1, 3) as g:
                    rows_of_body(g)
                turn_picks(1)
                with pe.Fori(3, BODIES) as g:
                    rows_of_body(g)
                for m in range(SUB - 3, SUB):
                    spread(BODIES - 1, m)

                pe.wait_ge(named("dots_done"), RING + T * (L + 1))
                for b in range(4):
                    pe.matmul(ps[:, b, :], zeros[:, :], x[:, 0, 0:HALF], start=True, stop=False, skip_group_check=True)
                with pe.Fori(0, CHUNKS // 2) as m:
                    for s in range(2):
                        pe.wait_ge(named("v_split"), 2 * m + (L * CHUNKS + s + 1))
                        for i in range(VI):
                            for t in range(NT):
                                for weights, rows in ((coef_high, v_high), (coef_high, v_low), (coef_low, v_high)):
                                    for half in range(2):
                                        last = pe.matmul(ps[:, 2 * t + half, :], weights[s][:, i, t * P:(t + 1) * P],
                                                         rows[s][:, i, half * HALF:(half + 1) * HALF], start=False, stop=True,
                                                         skip_group_check=True)
                        last.then_inc(named("v_used"), 1)

            pe.sem_inc(named("spread_done"), 2)
            peer("peer0")
            transpose_norm("odd")
            make_row("odd", 4)
            odd = groups_of("odd")
            for n, g in odd[:-2]:
                project(n, g)
            pe.wait_ge(proj_out, odd[-3][0] + 1)
            pe.wait_ge(named("f_summed"), 1)
            softmax_attention("odd")
            pe.wait_ge(av_out, MAPS + DSA_HEADS + MAPS)
            for n, g in odd[-2:]:
                project(n, g)
            peer("peer1")

        @block.vector
        def _(dve):
            step = stepper(dve, dve_step)

            def rms(stage):
                n = x_updates(stage)
                dve.wait_ge(ssq_done, n + 1)
                if X_PARTS[stage] == "halves":
                    step(dve.tensor_tensor(ssq[:, 0, :], ssq[:, 0, :], ssq[:, 1, :], ALU.add))
                dve.tensor_scalar(var[:, :], ssq[:, 0, :], 1.0 / D, EPS, ALU.mult, ALU.add).then_inc(var_done, 1)
                dve.wait_ge(std_done, n + 1)
                dve.reciprocal(rstd[:, :], std[:, :]).then_inc(named("rstd_done"), 1)
                dve.wait_ge(named("rstd_done"), n + 1)

            def norm(stage):
                n, a, v = NORM[stage]
                dve.scalar_tensor_tensor(a_cols[:, :], mod_cols[:, a, v + 1, :], 1.0, vec_cols[:, 0, KC * (2 + n):KC * (3 + n)],
                                         ALU.add, ALU.mult).then_inc(named("a_cols_made"), 1)
                dve.wait_ge(named("a_cols_made"), n + 1)
                rms(stage)
                dve.tensor_scalar(xn[:, 0, :], x[:, 0, :], rstd[:, 0:1], None, ALU.mult).then_inc(xn_done[0], 1)
                for half in range(2):
                    dve.wait_ge(xt_done, 4 * n + half + 1)
                    for j in range(4):
                        k = 4 * half + j
                        last = dve.tensor_scalar(hT[:, k, 0:P], ps[:, half, j * P:(j + 1) * P], a_cols[:, k:k + 1],
                                                 mod_cols[:, a, v, k:k + 1], ALU.mult, ALU.add)
                    last.then_inc(hT_done, 1)

            def residual(stage):
                r = x_updates(stage)
                dve.wait_ge(row_loaded, 16 * (r + 1))
                for half, (n, g) in enumerate(groups_of(stage)[-2:]):
                    dve.wait_ge(proj_done, n + 1)
                    b = 2 * (n % 2)
                    cols = slice(half * HALF, (half + 1) * HALF)
                    dve.tensor_tensor(xn[:, :, cols], ps[:, b:b + 2, :], row[:, cols].unsqueeze(1).broadcast_to([P, NT, HALF]),
                                      ALU.mult).then_inc(proj_out, 1)
                    dve.wait_ge(proj_out, n + 1)
                    dve.tensor_tensor(x[:, :, cols], x[:, :, cols], xn[:, :, cols], ALU.add).then_inc(x_parts, 1)
                    dve.wait_ge(x_parts, 2 * r + half + 1)
                dve.sem_inc(x_done, 1)

            def ada_pieces(first, last):
                for n in range(first, last):
                    stage, i = ada_stage(n)
                    ring = ada_ring[stage]
                    third, k = n // KC, n % KC
                    slot = i % len(ring)
                    turns = i // len(ring) + 1
                    if stage == "even":
                        turns += EARLY // len(ada_ring["mix1"])
                    dve.wait_ge(ada_loaded[slot], 16 * turns)
                    acc = ada_acc[stage][third % 2]
                    c = c_silu[:, ADA[third // 3][1] + k:ADA[third // 3][1] + k + 1]
                    if k == 0:
                        if third >= 2:
                            dve.wait_ge(ada_sums, third - 1)
                        dve.tensor_scalar(acc, ring[slot], c, None, ALU.mult).then_inc(ada_used, 1)
                    else:
                        dve.scalar_tensor_tensor(acc, ring[slot], c, acc, ALU.mult, ALU.add).then_inc(ada_used, 1)
                    dve.wait_ge(ada_used, n + 1)

            def take_third(n):
                dve.wait_ge(ada_sums, n + 1)
                half, at = BIAS_AT[n // 3]
                at += 16 * (n % 3)
                dve.tensor_tensor(mod_cols[:, n // 3, 2 * (n % 3):2 * (n % 3) + 2, :].rearrange("p v k -> p (v k)"),
                                  ps[:, 7, 0:16], vec_cols[:, half, at:at + 16], ALU.add).then_inc(mod_made, 1)
                dve.wait_ge(mod_made, n + 1)

            dve.wait_ge(c_ready, 1)
            ada_pieces(0, KC)
            dve.wait_ge(named("vec_ready"), 1)
            take_third(0)
            dve.wait_ge(consts_made, 1)

            norm("mix1")
            ada_pieces(KC, KC + 20)
            take_third(1)
            done = KC + 20
            for h in range(MAPS):
                dve.wait_ge(named("stick_ln"), h + 1)
                keep = st_keep[h % 2]
                step(dve.scalar_tensor_tensor(keep, ps[:, h % 4, 0:MAPW], 0.0, st_ln[h % 2], ALU.max, ALU.add))
                dve.tensor_tensor(diag_blocks(keep), diag_blocks(keep), before[:, :].unsqueeze(1).broadcast_to([P, 2, P]),
                                  ALU.mult).then_inc(named("stick_kept"), 1)
                now = 0 if h % 2 == 0 else 3 if h < 8 else 2
                ada_pieces(done, done + now)
                done += now
                if h in (3, 7, 13):
                    take_third((3, 7, 13).index(h) + 2)
            take_third(5)
            residual("mix1")
            def moe_pass(p):
                def places(j):
                    for b in range(2):
                        for t in range(NT):
                            last = dve.tensor_scalar(disp[:, t, SLOTS * b:SLOTS * (b + 1)], iota[:, 0:SLOTS],
                                                     rank[:, t, bass.ds(2 * j + b, 1)], None, ALU.is_equal)
                    last.then_inc(named("disp_made"), 1)

                def weighted_places(e, b):
                    for t in range(NT):
                        last = dve.tensor_scalar(comb[b][:, t, :].rearrange("p (a s) -> p a s", a=2),
                                                 iota[:, 0:SLOTS].unsqueeze(1).broadcast_to([P, 2, SLOTS]),
                                                 rank[:, t, bass.ds(e, 1)], weight[:, t, bass.ds(e, 1)], ALU.is_equal, ALU.mult)
                    last.then_inc(named("comb_made"), 1)

                places(0)
                dve.wait_ge(named("xe_psum"), p * SENT + 1)
                places(1)
                with dve.Fori(0, PAIRS // 2) as i:
                    for h in range(2):
                        for b in range(2):
                            weighted_places(4 * i + (2 * h + b), b)
                        for b in range(2):
                            dve.wait_ge(named("silu_done"), p * EXPERTS + 4 * i + (2 * h + b + 1))
                            dve.tensor_tensor(act_e[b], silu_g[b], ps[:, 6 + b, FF // 2:FF], ALU.mult).then_inc(named("act_done"), 1)
                            if b == 0:
                                dve.wait_ge(named("xe_psum"), p * SENT + 2 * i + (h + 2))
                                places(2 * i + (h + 2))
                        for b in range(2):
                            dve.wait_ge(named("operands_made"), p * EXPERTS + 4 * i + (2 * h + b + 1))
                            dve.tensor_copy(turned[b].rearrange("p a n -> p (a n)"), ps[:, 4 + b, :]).then_inc(named("operands_out"), 1)

            def moe_overflow(p):
                dve.wait_ge(named("comb_done"), p * (EXPERTS + 1))
                dve.memset(turned[1], 0.0)
                dve.tensor_scalar(rank[:, :, :], rank[:, :, :], -float(SLOTS), None, ALU.add).then_inc(named("rank_moved"), 1)
                dve.wait_ge(named("rank_moved"), p)
                moe_pass(p)

            def moe_route():
                step(dve.memset(grp_logit[:, :, :], LOWEST))
                step(dve.memset(weight[:, :, :], 0.0))
                step(dve.memset(rank[:, :, :], -1.0))
                step(dve.memset(turned[1], 0.0))
                step(dve.memset(y_e[1], 0.0))
                dve.wait_ge(named("logits_done"), 1)
                logits = ps[:, 4, 0:128].rearrange("p (t n) -> p t n", t=NT)
                step(dve.tensor_copy(grp_logit[:, :, 0:GROUPS], logits[:, :, 0:GROUPS]))
                step(dve.tensor_copy(exp_logit[:, :, :], logits[:, :, GROUPS:GROUPS + EXPERTS]))
                for t in range(NT):
                    step(dve.max(grp_top[:, t, :], grp_logit[:, t, :]))
                    step(dve.max_index(grp_at[:, t, :], grp_top[:, t, :], grp_logit[:, t, :]))
                step(dve.tensor_copy(grp_num, grp_at[:, :, 0]))
                dve.tensor_scalar(grp_neg, grp_top[:, :, 0], -1.0, None, ALU.mult).then_inc(named("grp_neg_made"), 1)
                for t in range(NT):
                    step(dve.tensor_scalar(grp_hot[:, t, :], iota[:, 0:GROUPS], grp_num[:, t:t + 1], None, ALU.is_equal))
                    for g in range(GROUPS):
                        part = exp_logit[:, t, g * PER_GROUP:(g + 1) * PER_GROUP]
                        if g == 0:
                            step(dve.tensor_scalar(in_grp[:, t, :], part, grp_hot[:, t, 0:1], None, ALU.mult))
                        else:
                            step(dve.scalar_tensor_tensor(in_grp[:, t, :], part, grp_hot[:, t, g:g + 1], in_grp[:, t, :],
                                                          ALU.mult, ALU.add))
                    step(dve.max(in_top[:, t, :], in_grp[:, t, :]))
                    step(dve.max_index(in_at[:, t, :], in_top[:, t, :], in_grp[:, t, :]))
                dve.tensor_scalar(in_neg, in_top[:, :, 0], -1.0, None, ALU.mult).then_inc(named("in_neg_made"), 1)
                step(dve.tensor_copy(in_num[:, :, :], in_at[:, :, :]))
                for t in range(NT):
                    step(dve.scalar_tensor_tensor(expert[:, t, :], grp_num[:, t:t + 1].broadcast_to([P, 2]), float(PER_GROUP),
                                                  in_num[:, t, 0:2], ALU.mult, ALU.add))
                dve.wait_ge(named("grp_exp_done"), NT)
                step(dve.reciprocal(grp_p, grp_sum))
                dve.wait_ge(named("in_exp_done"), NT)
                step(dve.tensor_scalar(in_den, in_exp, 1.0, None, ALU.add))
                step(dve.reciprocal(in_den, in_den))
                step(dve.tensor_tensor(gate1, grp_p, in_den, ALU.mult))
                step(dve.tensor_tensor(gate2, gate1, in_exp, ALU.mult))
                for t in range(NT):
                    step(dve.tensor_scalar(hot1[:, t, :], iota[:, 0:EXPERTS], expert[:, t, 0:1], None, ALU.is_equal))
                    step(dve.tensor_scalar(hot2[:, t, :], iota[:, 0:EXPERTS], expert[:, t, 1:2], None, ALU.is_equal))
                dve.tensor_tensor(chosen[:, :, :], hot1[:, :, :], hot2[:, :, :], ALU.add).then_inc(named("chosen_made"), 1)
                dve.wait_ge(named("chosen_made"), 1)
                for t in range(NT):
                    step(dve.tensor_scalar(hot1[:, t, :], hot1[:, t, :], gate1[:, t:t + 1], None, ALU.mult))
                    step(dve.scalar_tensor_tensor(weight[:, t, 0:EXPERTS], hot2[:, t, :], gate2[:, t:t + 1], hot1[:, t, :],
                                                  ALU.mult, ALU.add))
                dve.wait_ge(named("ranks_done"), 1)
                counted = ps[:, 5, 0:128].rearrange("p (t n) -> p t n", t=NT)[:, :, 0:EXPERTS]
                step(dve.scalar_tensor_tensor(rank[:, :, 0:EXPERTS], counted, 1.0, chosen[:, :, :], ALU.add, ALU.mult))
                step(dve.tensor_scalar(rank[:, :, 0:EXPERTS], rank[:, :, 0:EXPERTS], -1.0, None, ALU.add))
                step(dve.tensor_reduce(most[:, 0:1], ps[:, 5, 128:128 + EXPERTS], AX_X, ALU.max))
                step(dve.tensor_scalar(most[:, 1:2], most[:, 0:1], SLOTS + 0.5, 1.0, ALU.is_gt, ALU.add))
                for more in range(2, T // SLOTS):
                    step(dve.scalar_tensor_tensor(most[:, more:more + 1], most[:, 0:1], more * SLOTS + 0.5, most[:, more - 1:more],
                                                  ALU.is_gt, ALU.add))
                dve.tensor_copy(passes[:, :], most[:, T // SLOTS - 1:T // SLOTS]).then_inc(named("passes_known"), 1)
                dve.sem_inc(named("rank_made"), 1)

            def residual_banks(stage, done):
                r = x_updates(stage)
                dve.wait_ge(row_loaded, 16 * (r + 1))
                for t in range(NT):
                    step(dve.tensor_tensor(xn[:, t, :], ps[:, 2 * t:2 * t + 2, :].rearrange("p b n -> p (b n)"), row[:, :], ALU.mult))
                    dve.tensor_tensor(x[:, t, :], x[:, t, :], xn[:, t, :], ALU.add).then_inc(x_parts, 1)
                dve.wait_ge(x_parts, 2 * (r + 1))
                dve.sem_inc(x_done, 1)

            def norm_rows(stage):
                rms(stage)
                r = x_updates(stage)
                dve.wait_ge(row_loaded, 16 * (r + 1))
                for t in range(NT):
                    dve.scalar_tensor_tensor(x[:, t, :], x[:, t, :], rstd[:, t:t + 1], row[:, :], ALU.mult, ALU.mult).then_inc(x_parts, 1)
                dve.wait_ge(x_parts, 2 * (r + 1))
                dve.sem_inc(x_done, 1)

            norm("moe")
            moe_route()
            dve.sem_inc(named("operands_out"), 1)
            moe_pass(0)
            overflow(dve, moe_overflow)
            dve.wait_ge(named("moe_combined"), 1)
            residual_banks("moe", None)
            norm_rows("fin1")
            def softmax_attention(stage, add):
                maps = SOFTMAX[stage]

                def scored(i):
                    d = maps[i]
                    b = i % 2
                    dve.wait_ge(score_done, MAPS + IDX_HEADS + d["n"] + 1)
                    dve.tensor_tensor(sm_s[b], ps[:, 4 + b, 0:MAPW], add(d["m"]), ALU.add).then_inc(score_read, 1)
                    dve.wait_ge(score_read, d["n"] + 1)
                    for t in range(NT):
                        last = dve.tensor_reduce(sm_max[b][:, t:t + 1], both_tiles(sm_s[b], t), AX_X, ALU.max, negate=True)
                    last.then_inc(named("max_made"), 1)

                def normed(i):
                    d = maps[i]
                    b = i % 2
                    dve.wait_ge(named("exp_done"), NT * (d["n"] + 1))
                    step(dve.reciprocal(sm_inv[b], sm_sum[b]))
                    if d["kind"] == "second":
                        step(dve.tensor_scalar(sm_inv[b], sm_inv[b], neg_lam[:, 0:1], None, ALU.mult))
                        for t in range(NT):
                            last = dve.scalar_tensor_tensor(both_tiles(sm_p[b], t), both_tiles(sm_p[b], t), sm_inv[b][:, t:t + 1],
                                                            both_tiles(sm_p[1 - b], t), ALU.mult, ALU.add)
                    else:
                        for t in range(NT):
                            last = dve.tensor_scalar(both_tiles(sm_p[b], t), both_tiles(sm_p[b], t), sm_inv[b][:, t:t + 1], None, ALU.mult)
                    if d["kind"] == "first":
                        step(last)
                    else:
                        last.then_inc(named("probs_ready"), 1)

                for i in range(MAPS + 1):
                    if i < MAPS:
                        scored(i)
                    if i >= 1:
                        normed(i - 1)
                    if stage == "even" and i < MAPS:
                        ada_pieces(7 * KC + i, 7 * KC + i + 1)
                    if stage == "even" and i == 12:
                        take_third(7)

            norm("even")
            dve.wait_ge(named("kv_ssq_done"), NT)
            dve.tensor_scalar(kv_std, kv_ssq, 1.0 / LATENT, EPS, ALU.mult, ALU.add).then_inc(named("kv_var_done"), 1)
            dve.wait_ge(named("kv_std_done"), 1)
            step(dve.reciprocal(kv_std, kv_std))
            for t in range(NT):
                last = dve.tensor_scalar(ckv_tok[:, t, :], ckv_tok[:, t, :], kv_std[:, t:t + 1], None, ALU.mult)
            last.then_inc(named("kv_scaled"), 1)
            dve.wait_ge(named("even_vec_loaded"), 16 * 3)
            lam_pairs = lam_vec.rearrange("p (a b) d -> p a b d", b=2)
            step(dve.tensor_tensor(lam_prod[:, :, :], lam_pairs[:, :, 0, :], lam_pairs[:, :, 1, :], ALU.mult))
            dve.tensor_reduce(lam_sum, lam_prod[:, :, :], AX_X, ALU.add).then_inc(named("lam_sum_made"), 1)
            step(dve.tensor_scalar(subln_col, subln_raw, 1.0 - LAM_INIT, None, ALU.mult))
            dve.wait_ge(named("lam_exp_done"), 1)
            step(dve.tensor_tensor(neg_lam, lam_exp[:, 1:2], lam_exp[:, 0:1], ALU.subtract))
            step(dve.tensor_scalar(neg_lam, neg_lam, -LAM_INIT, None, ALU.add))
            dve.wait_ge(named("kv_turned"), 1)
            for c in range(LATENT // P):
                last = dve.tensor_scalar(ckvT[:, c, :], ps[:, 6, c * T:(c + 1) * T], kv_gain[:, c:c + 1], None, ALU.mult)
            last.then_inc(named("ckvT_ready"), 1)
            dve.wait_ge(proj_out, groups_of("even")[2][0] + 1)
            for h in range(IDX_HEADS):
                dve.wait_ge(named("idx_relu_done"), h + 1)
                if h == 0:
                    for t in range(NT):
                        last = dve.tensor_scalar(both_tiles(idx_score, t), both_tiles(idx_relu[0], t), widx[:, t, 0:1], 0.0, ALU.mult, ALU.add)
                else:
                    for t in range(NT):
                        last = dve.scalar_tensor_tensor(both_tiles(idx_score, t), both_tiles(idx_relu[h % 2], t), widx[:, t, h:h + 1],
                                                        both_tiles(idx_score, t), ALU.mult, ALU.add)
                last.then_inc(named("idx_summed"), 1)
                dve.wait_ge(named("idx_summed"), h + 1)
                ada_pieces(EARLY + h, EARLY + h + 1)
            dve.wait_ge(named("idx_causal"), 1)
            for r in range(DSA_TOP // 8):
                for t in range(NT):
                    step(dve.max(idx_top, both_tiles(idx_score, t)))
                    step(dve.match_replace(both_tiles(idx_score, t), idx_top, both_tiles(idx_score, t), TAKEN))
            step(dve.tensor_scalar(idx_mask, idx_score, TAKEN, NEG, ALU.not_equal, ALU.mult))
            take_third(6)
            dve.wait_ge(named("rel_loaded"), 32)
            dsa_maps = rel_maps[:, 0:DSA_HEADS, :]
            step(dve.tensor_tensor(dsa_maps, dsa_maps, idx_mask.unsqueeze(1).broadcast_to([P, DSA_HEADS, MAPW]), ALU.add))
            softmax_attention("even", lambda m: rel_maps[:, m if m < DSA_HEADS else (m + DSA_HEADS) // 2, :])
            take_third(8)
            dve.wait_ge(named("diff_summed"), 1)
            dve.tensor_scalar(diff_std.rearrange("p h t -> p (h t)"), ps[:, 4:6, :].rearrange("p b n -> p (b n)"), 0.5 / HEAD, EPS,
                              ALU.mult, ALU.add).then_inc(named("diff_var_done"), 1)
            dve.wait_ge(named("diff_std_done"), 1)
            step(dve.reciprocal(diff_std[:, :, :], diff_std[:, :, :]))
            dve.scalar_tensor_tensor(oT[:, 4:8, :].rearrange("p h t -> p (h t)"), ps[:, 2:4, :].rearrange("p b n -> p (b n)"),
                                     subln_col[:, 0:1], diff_std.rearrange("p h t -> p (h t)"), ALU.mult, ALU.mult
                                     ).then_inc(named("diff_out"), 1)
            residual("even")
            def peer(stage):
                L = layer_of(stage)
                norm(stage)
                dve.wait_ge(named("h_tok_ready"), 4 * (L + 2))
                step(dve.tensor_copy(part_hi[:, :, :], h_tok[:, :, :]))
                step(dve.tensor_tensor(part_rest[:, :, :], h_tok[:, :, :], part_hi[:, :, :], ALU.subtract))
                step(dve.tensor_copy(part_mid[:, :, :], part_rest[:, :, :]))
                dve.tensor_tensor(part_lo[:, :, :], part_rest[:, :, :], part_mid[:, :, :], ALU.subtract).then_inc(named("parts_made"), 1)
                def best_of_group(t, i):
                    if t == 0:
                        dve.wait_ge(named("key_scored"), 4 * L + i + 1)
                    else:
                        dve.wait_ge(named("keys_copied"), 4 * L + i + 1)
                    rows = [(t * HP + GQ * i + j, key_score[:, GQ * i + j, :] if t else ps[:, 4 + i % 2, j * P:(j + 1) * P],
                             key_left[:, j, :]) for j in range(GQ)]
                    for r, s, _ in rows:
                        last = dve.max(key_top[:, r, 0:8], s)
                    step(last)
                    for r, s, left in rows:
                        dve.max_index(key_at[:, r, 0:8], key_top[:, r, 0:8], s)
                        last = dve.match_replace(left, key_top[:, r, 0:8], s, LOWEST)
                    step(last)
                    if t == 0:
                        dve.sem_inc(named("keys_read"), 1)
                    for r, _, left in rows:
                        last = dve.max(key_top[:, r, 8:16], left)
                    step(last)
                    for r, _, left in rows:
                        last = dve.max_index(key_at[:, r, 8:16], key_top[:, r, 8:16], left)
                    step(last)
                    square = [P, GH, PEER_K, PEER_K]
                    first = slice(t * HP + GQ * i, t * HP + GQ * (i + 1), 2)
                    second = slice(t * HP + GQ * i + 1, t * HP + GQ * (i + 1), 2)
                    mine = slice(t * HP + GQ * i, t * HP + GQ * (i + 1))
                    dve.tensor_copy(key_num[:, mine, :], key_at[:, mine, :])
                    step(dve.tensor_tensor(cand.rearrange("p h (a b) -> p h a b", b=PEER_K),
                                           key_top[:, first, :].unsqueeze(3).broadcast_to(square),
                                           key_top[:, second, :].unsqueeze(2).broadcast_to(square), ALU.add))
                    heads = [(t * PEER_HEADS + GH * i + h, cand[:, h, :], cand_left[:, h, :]) for h in range(GH)]
                    for r, s, _ in heads:
                        last = dve.max(best[:, r, 0:8], s)
                    step(last)
                    for r, s, left in heads:
                        dve.max_index(best_at[:, r, 0:8], best[:, r, 0:8], s)
                        last = dve.match_replace(left, best[:, r, 0:8], s, LOWEST)
                    step(last)
                    for r, _, left in heads:
                        last = dve.max(best[:, r, 8:16], left)
                    step(last)
                    for r, _, left in heads:
                        last = dve.max_index(best_at[:, r, 8:16], best[:, r, 8:16], left)
                    step(last)
                    flat = best_at[:, t * PEER_HEADS + GH * i:t * PEER_HEADS + GH * (i + 1), :].rearrange("p h k -> p (h k)")
                    dve.tensor_scalar(best_hi, flat, 4, None, ALU.logical_shift_right)
                    step(dve.tensor_scalar(best_lo, flat, PEER_K - 1, None, ALU.bitwise_and))
                    dve.tensor_copy(best_row, best_hi)
                    step(dve.tensor_copy(best_col, best_lo))
                    sides = [(match[0], best_row, first, pick_i), (match[1], best_col, second, pick_j)]
                    for hits, place, _, _ in sides:
                        last = dve.tensor_tensor(hits[:, :, :], iota_16[:, :].unsqueeze(1).broadcast_to([P, GK, PEER_K]),
                                                 place.unsqueeze(2).broadcast_to([P, GK, PEER_K]), ALU.is_equal)
                    step(last)
                    for hits, _, own, _ in sides:
                        as_heads = hits.rearrange("p (h k) m -> p h k m", h=GH)
                        last = dve.tensor_tensor(as_heads, as_heads, key_num[:, own, :].unsqueeze(2).broadcast_to(square), ALU.mult)
                    step(last)
                    for hits, _, _, pick in sides:
                        last = dve.tensor_reduce(pick[:, t, GK * i:GK * (i + 1)], hits[:, :, :], AX_X, ALU.add)
                    step(last)

                full = [P, PEER_HEADS, PEER_K]

                def gates_begin(t):
                    heads = slice(t * PEER_HEADS, (t + 1) * PEER_HEADS)
                    dve.tensor_tensor(gate[:, heads, :], best[:, heads, :], best[:, heads, 0:1].broadcast_to(full), ALU.subtract
                                      ).then_inc(named("gate_diff"), 1)

                def gates_end(t):
                    heads = slice(t * PEER_HEADS, (t + 1) * PEER_HEADS)
                    dve.wait_ge(named("gate_exp"), NT * L + t + 1)
                    step(dve.tensor_reduce(gate_sum[:, heads], gate[:, heads, :], AX_X, ALU.add))
                    step(dve.reciprocal(gate_sum[:, heads], gate_sum[:, heads]))
                    dve.tensor_tensor(gate[:, heads, :], gate[:, heads, :], gate_sum[:, heads].unsqueeze(2).broadcast_to(full), ALU.mult
                                      ).then_inc(named("picks_made"), 1)

                def take_picks(t):
                    cols = slice(t * P, (t + 1) * P)
                    dve.wait_ge(named("picks_psum"), NT * L + t + 1)
                    dve.tensor_scalar(peer_neg_i[:, cols], ps[:, 6, 0:P], -1.0, None, ALU.mult)
                    dve.tensor_scalar(peer_neg_j[:, cols], ps[:, 6, P:2 * P], -1.0, None, ALU.mult)
                    step(dve.tensor_copy(peer_g[:, cols], ps[:, 6, 2 * P:3 * P]))
                    step(dve.scalar_tensor_tensor(peer_num[:, :], peer_neg_i[:, cols], -float(NKEYS), peer_neg_j[:, cols], ALU.mult, ALU.subtract))
                    dve.tensor_scalar(peer_e[:, cols], peer_num[:, :], float(L * PEER_EXPERTS), None, ALU.add).then_inc(named("experts_made"), 1)

                for i in range(4):
                    best_of_group(0, i)
                gates_begin(0)
                gates_end(0)
                take_picks(0)

                def coefs(g, b):
                    n = g * (BODY // RING) + (L * T // RING + b + 1)
                    at = b % (BODY // RING) * RING
                    dve.wait_ge(named("gelu_done"), n)
                    dve.tensor_tensor(coef[:, at:at + RING], gelu[:, at:at + RING], peer_g[:, bass.ds(g * BODY + b * RING, RING)], ALU.mult
                                      ).then_inc(named("coef_made"), 1)
                    dve.wait_ge(named("coef_made"), n)

                def weigh_hots(g, m):
                    n = g * SUB + (L * T // 4 + m + 1)
                    dve.wait_ge(named("hots_made"), n)
                    dve.sem_inc(named("weigh_begun"), 1)
                    dve.tensor_tensor(hot_i[m % 2], hot_i[m % 2], coef[:, 4 * (m % SUB):4 * (m % SUB) + 4].unsqueeze(2).broadcast_to([P, 4, P]),
                                      ALU.mult).then_inc(named("hots_weighed"), 1)

                def dots_of_body(g, between, first=False):
                    for i in range(BODY):
                        b, s = i // RING, i % RING
                        dve.wait_ge(named(f"u_loaded{s}"), g * (16 * BODY // RING) + (L * T // RING + b + 1) * 16)
                        dve.wait_ge(named("row_spread"), g * BODY + (L * T + i + 1))
                        dve.tensor_tensor_reduce(u_rows[s], u_rows[s], ps[:, 2 * (i % 2):2 * (i % 2) + 2, :].rearrange(
                            "p b n -> p (b n)"), 1.0, 0.0, ALU.mult, ALU.add, dots[:, i:i + 1]).then_inc(named("dots_done"), 1)
                        if b >= 1 or not first:
                            if s == 3:
                                coefs(g, b - 1)
                                weigh_hots(g, 2 * (b - 1))
                            if s == 7:
                                weigh_hots(g, 2 * (b - 1) + 1)
                        if s == 7 and b in between:
                            between[b]()

                dots_of_body(0, {1: lambda: best_of_group(1, 0), 3: lambda: best_of_group(1, 1)}, first=True)
                dots_of_body(1, {1: lambda: best_of_group(1, 2), 3: lambda: best_of_group(1, 3)})
                gates_begin(1)
                dots_of_body(2, {1: lambda: gates_end(1)})
                take_picks(1)
                with dve.Fori(3, BODIES) as g:
                    dots_of_body(g, {})
                coefs(BODIES - 1, BODY // RING - 1)
                weigh_hots(BODIES - 1, SUB - 2)
                weigh_hots(BODIES - 1, SUB - 1)
                with dve.Fori(0, CHUNKS // 2) as m:
                    for s in range(2):
                        dve.wait_ge(named("coef_high_made"), 2 * m + (L * CHUNKS + s + 1))
                        dve.tensor_tensor(coef_low[s], by_key[:, bass.ds((2 * m + s) * VI, VI), :], coef_high[s], ALU.subtract)
                        dve.wait_ge(named("v_high_made"), 2 * m + (L * CHUNKS + s + 1))
                        dve.tensor_tensor(v_low[s], v_rows[s], v_high[s], ALU.subtract).then_inc(named("v_split"), 1)
                dve.wait_ge(named("v_used"), CHUNKS * (L + 1))
                residual_banks(stage, None)

            dve.sem_inc(named("dots_done"), RING)
            peer("peer0")
            norm("odd")
            n = groups_of("odd")[0][0]
            dve.wait_ge(proj_done, n + 1)
            dve.wait_ge(named("forget_loaded"), 16)
            step(dve.tensor_scalar(f_logit[0:C_HEADS, :], ps[0:C_HEADS, 2 * (n % 2), 0:T], forget_col[0:C_HEADS, 0:1], None, ALU.add))
            dve.sem_inc(proj_out, 1)
            dve.sem_inc(named("f_made"), 1)
            dve.wait_ge(named("f_log_done"), 1)
            step(dve.scalar_tensor_tensor(f_log[0:C_HEADS, :], f_logit[0:C_HEADS, :], 0.0, f_log[0:C_HEADS, :], ALU.min, ALU.subtract))
            step(dve.tensor_tensor_scan(f_cum[0:C_HEADS, :], ones[0:C_HEADS, 0:1].broadcast_to([C_HEADS, T]), f_log[0:C_HEADS, :],
                                        0.0, ALU.mult, ALU.add))
            dve.tensor_scalar(neg_ident[0:C_HEADS, :], ident[0:C_HEADS, 0:C_HEADS], -1.0, None, ALU.mult).then_inc(named("f_summed"), 1)
            softmax_attention("odd", lambda m: causal_add[:, :])
            residual("odd")
            peer("peer1")
            norm_rows("all")


INPUTS = [
    "x", "c", "ada_w", "ada_b", "norm_g", "final_g", "sb_w_in", "sb_w_out", "moe_w_grp", "moe_b_grp", "moe_w_exp",
    "moe_b_exp", "moe_w_gate", "moe_w_up", "moe_w_down", "c_2", "rel_bias_2", "ada_w_2", "ada_b_2", "norm_mix_2",
    "norm_ffn_2", "norm_final_2", "even_w_in_2", "even_w_out_2", "a_kv_norm_2", "a_w_uk_2", "a_w_uv_2", "b_lambda_2",
    "b_subln_2", "odd_w_in_2", "odd_b_forget_2", "odd_w_out_2", "peer_w_q_2", "peer_sub_keys_2", "peer_u_2", "peer_v_2",
]


def kernel(**inputs):
    import numpy as np
    import concourse.bacc as bacc
    from concourse.bass_utils import run_bass_kernel_spmd

    nc = bacc.Bacc("TRN2", target_bir_lowering=False, num_devices=1)
    arrays, args = {}, {}
    for name in INPUTS:
        a = np.ascontiguousarray(inputs[name])
        arrays["in_" + name] = a
        args[name] = nc.dram_tensor("in_" + name, a.shape, mybir.dt.from_np(a.dtype), kind="ExternalInput").ap()
    out = nc.dram_tensor("out_x", (1, T, D), F32, kind="ExternalOutput").ap()
    two_block_kernel(nc, args, out)
    r = run_bass_kernel_spmd(nc, [arrays], core_ids=[0])
    return r.results[0]["out_x"]
```
